# Optimizing a Trainium2 kernel written in Bass

```python
import math
import functools
import jax
import jax.numpy as jnp
from jax import lax
import numpy as np

D_MODEL = 1024
BATCH = 1
SEQ = 1024
DEPTH = 1
DEC_BATCH = 8
DEC_SEQ = 4
PAST_LEN = 4096
PAGE_SIZE = 128

NSA_HEADS = 8
NSA_KV_HEADS = 2
NSA_GROUP = NSA_HEADS // NSA_KV_HEADS
HEAD_DIM = 64
CMP_BLOCK = 32
CMP_STRIDE = 16
CMP_HIDDEN = 2 * HEAD_DIM
SEL_BLOCK = 64
N_SEL = 16
WINDOW = 512
Q_BLOCK = 128
ROPE_THETA = 10000.0
HGRN_HEADS = 4
HGRN_DK = 128
HGRN_DV = 128
HGRN_CHUNK = 64
N_GROUPS = 4
EXPERTS_PER_GROUP = 8
N_EXPERTS = N_GROUPS * EXPERTS_PER_GROUP
TOP_K_EXPERTS = 2
D_EXPERT = 512
MOE_BLOCK = 128
NSA_WIDTH = NSA_HEADS * HEAD_DIM
KV_WIDTH = 2 * NSA_KV_HEADS * HEAD_DIM
HGRN_KW = HGRN_HEADS * HGRN_DK
HGRN_VW = HGRN_HEADS * HGRN_DV
IN_SPLITS = (NSA_WIDTH, KV_WIDTH, KV_WIDTH, KV_WIDTH, 3 * NSA_HEADS, HGRN_KW, HGRN_KW, HGRN_VW, HGRN_VW, D_MODEL, D_MODEL)
IN_WIDTH = sum(IN_SPLITS)
NORM_EPS = 1e-6
NEG = -1e9
BIG = 1e9

kernel_name = "nsa_hgrn2_hmoe_hybrid_step"

def rmsnorm(x, g):
    xf = x.astype(jnp.float32)
    y = xf * lax.rsqrt(jnp.mean(xf * xf, axis=-1, keepdims=True) + NORM_EPS)
    return (y * g.astype(jnp.float32)).astype(x.dtype)

def rope(x, pos):
    half = x.shape[-1] // 2
    inv = ROPE_THETA ** (-jnp.arange(half, dtype=jnp.float32) / half)
    ang = pos.astype(jnp.float32)[:, None] * inv[None, :]
    cos = jnp.cos(ang)[:, None, :]
    sin = jnp.sin(ang)[:, None, :]
    xf = x.astype(jnp.float32)
    x1, x2 = xf[..., :half], xf[..., half:]
    return jnp.concatenate([x1 * cos - x2 * sin, x2 * cos + x1 * sin], axis=-1).astype(x.dtype)

def masked_softmax(s, ok):
    s = s.astype(jnp.float32)
    m = jnp.max(jnp.where(ok, s, NEG), axis=-1, keepdims=True)
    e = jnp.exp(jnp.where(ok, s - m, NEG))
    return e / jnp.maximum(jnp.sum(e, axis=-1, keepdims=True), 1e-30)

def shared_attend(q, k, v, ok):
    s = jnp.einsum('tkgd,lkd->kgtl', q, k) * HEAD_DIM ** -0.5
    p = masked_softmax(s, ok)
    return jnp.einsum('kgtl,lkd->tkgd', p.astype(v.dtype), v), p

def gathered_attend(q, kg, vg, ok):
    s = jnp.einsum('tkgd,ktjd->kgtj', q, kg) * HEAD_DIM ** -0.5
    p = masked_softmax(s, ok[:, None])
    return jnp.einsum('kgtj,ktjd->tkgd', p.astype(vg.dtype), vg)

def window_mask(tq, kpos):
    kp = kpos[None, :]
    tt = tq[:, None]
    return (kp >= 0) & (kp <= tt) & (kp > tt - WINDOW)

def compress_kv(kv, pe, w1, b1, w2, b2):
    n_ch = kv.shape[-4] // CMP_STRIDE
    ch = kv[..., : n_ch * CMP_STRIDE, :, :, :].reshape(kv.shape[:-4] + (n_ch, CMP_STRIDE, 2, NSA_KV_HEADS, HEAD_DIM))
    w1r = w1.reshape(2, 2, CMP_STRIDE, HEAD_DIM, CMP_HIDDEN)
    h_a = jnp.einsum('...nsckd,csdh->...nckh', ch, w1r[:, 0])
    h_b = jnp.einsum('...nsckd,csdh->...nckh', ch, w1r[:, 1])
    c0 = jnp.einsum('crd,crdh->ch', pe, w1.reshape(2, CMP_BLOCK, HEAD_DIM, CMP_HIDDEN)) + b1
    hid = jax.nn.gelu(h_a[..., :-1, :, :, :] + h_b[..., 1:, :, :, :] + c0[:, None, :])
    return jnp.einsum('...nckh,chd->...nckd', hid, w2) + b2[:, None, :]

def cmp_branch(qg, kv_rows, tpos, cmp_params):
    ckv = compress_kv(kv_rows, *cmp_params)
    n_cmp = ckv.shape[1]
    c_end = jnp.arange(n_cmp) * CMP_STRIDE + CMP_BLOCK - 1
    ok = c_end[None, :] <= tpos[:, None]
    return jax.vmap(shared_attend, in_axes=(0, 0, 0, None))(qg, ckv[:, :, 0], ckv[:, :, 1], ok)

def cover_matrix(n_cmp, n_sel):
    start = jnp.arange(n_cmp)[:, None] * CMP_STRIDE
    j = jnp.arange(n_sel)[None, :]
    return ((start < (j + 1) * SEL_BLOCK) & (start + CMP_BLOCK > j * SEL_BLOCK)).astype(jnp.float32)

def select_blocks(p_cmp, tpos, n_sel):
    imp = jnp.einsum('...kgtn,nj->...ktj', p_cmp, cover_matrix(p_cmp.shape[-1], n_sel))
    j = jnp.arange(n_sel)[None, :]
    cur = (tpos // SEL_BLOCK)[:, None]
    valid = j * SEL_BLOCK <= tpos[:, None]
    forced = (j == 0) | (j == cur) | (j == cur - 1)
    score = jnp.where(valid, jnp.where(forced, BIG, imp), NEG)
    vals, idx = lax.top_k(score, min(N_SEL, n_sel))
    return idx, vals > 0.5 * NEG

def sel_attend(q, g, idx, blk_ok, tq):
    kvh, t_len, n_top = idx.shape
    kpos = idx[..., None] * SEL_BLOCK + jnp.arange(SEL_BLOCK)
    ok = blk_ok[..., None] & (kpos <= tq[None, :, None, None])
    j_len = n_top * SEL_BLOCK
    kg = g[..., 0, :].reshape(kvh, t_len, j_len, HEAD_DIM)
    vg = g[..., 1, :].reshape(kvh, t_len, j_len, HEAD_DIM)
    return gathered_attend(q, kg, vg, ok.reshape(kvh, t_len, j_len))

def nsa_prompt(q, qr, kvc, kvs, kvw, cmp_params):
    b_sz, s_len = q.shape[:2]
    tpos = jnp.arange(s_len)
    qg = q.reshape(b_sz, s_len, NSA_KV_HEADS, NSA_GROUP, HEAD_DIM)
    qrg = qr.reshape(b_sz, s_len, NSA_KV_HEADS, NSA_GROUP, HEAD_DIM)
    o_cmp, p_cmp = cmp_branch(qg, kvc, tpos, cmp_params)
    n_sel = s_len // SEL_BLOCK
    idx, blk_ok = select_blocks(p_cmp, tpos, n_sel)
    sblk = kvs.reshape(b_sz, n_sel, SEL_BLOCK, 2, NSA_KV_HEADS, HEAD_DIM)
    wpad = jnp.pad(kvw, ((0, 0), (WINDOW, 0), (0, 0), (0, 0), (0, 0)))
    hh = jnp.arange(NSA_KV_HEADS)[:, None, None]
    n_qb = s_len // Q_BLOCK

    def item(args):
        b, qb = args
        t0 = qb * Q_BLOCK
        tq = t0 + jnp.arange(Q_BLOCK)
        q_blk = lax.dynamic_slice_in_dim(qrg[b], t0, Q_BLOCK, axis=0)
        ib = lax.dynamic_slice_in_dim(idx[b], t0, Q_BLOCK, axis=1)
        okb = lax.dynamic_slice_in_dim(blk_ok[b], t0, Q_BLOCK, axis=1)
        g = sblk[b][ib, :, :, hh, :]
        o_s = sel_attend(q_blk, g, ib, okb, tq)
        wk = lax.dynamic_slice_in_dim(wpad[b], t0, Q_BLOCK + WINDOW, axis=0)
        wpos = t0 - WINDOW + jnp.arange(Q_BLOCK + WINDOW)
        o_w, _ = shared_attend(q_blk, wk[:, 0], wk[:, 1], window_mask(tq, wpos))
        return o_s, o_w

    bids = jnp.repeat(jnp.arange(b_sz), n_qb)
    qids = jnp.tile(jnp.arange(n_qb), b_sz)
    o_slc, o_win = lax.map(item, (bids, qids))
    shp = (b_sz, s_len, NSA_HEADS, HEAD_DIM)
    new_win = kvw[:, s_len - min(WINDOW, s_len):]
    return o_cmp.reshape(shp), o_slc.reshape(shp), o_win.reshape(shp), (kvc, kvs, new_win)

def nsa_sample(q, qr, kvc, kvs, kvw, cache_cmp, cache_slc, cache_win, page_table, cmp_params):
    b_sz, t_len = q.shape[:2]
    past = page_table.shape[1] * PAGE_SIZE
    total = past + t_len
    tpos = past + jnp.arange(t_len)
    qg = q.reshape(b_sz, t_len, NSA_KV_HEADS, NSA_GROUP, HEAD_DIM)
    qrg = qr.reshape(b_sz, t_len, NSA_KV_HEADS, NSA_GROUP, HEAD_DIM)
    past_cmp = cache_cmp[page_table].reshape(b_sz, past, 2, NSA_KV_HEADS, HEAD_DIM)
    full_cmp = jnp.concatenate([past_cmp, kvc.astype(past_cmp.dtype)], axis=1)
    o_cmp, p_cmp = cmp_branch(qg, full_cmp, tpos, cmp_params)
    n_sel = -(-total // SEL_BLOCK)
    idx, blk_ok = select_blocks(p_cmp, tpos, n_sel)
    n_past_blk = past // SEL_BLOCK
    n_new_blk = n_sel - n_past_blk
    blk_per_page = PAGE_SIZE // SEL_BLOCK
    pool_blk = cache_slc.reshape(-1, SEL_BLOCK, 2, NSA_KV_HEADS, HEAD_DIM)
    new_blk = jnp.pad(kvs, ((0, 0), (0, n_new_blk * SEL_BLOCK - t_len), (0, 0), (0, 0), (0, 0)))
    new_blk = new_blk.reshape(b_sz, n_new_blk, SEL_BLOCK, 2, NSA_KV_HEADS, HEAD_DIM)
    win_rows = jnp.concatenate([cache_win, kvw.astype(cache_win.dtype)], axis=1)
    wpos = past - cache_win.shape[1] + jnp.arange(win_rows.shape[1])
    wok = window_mask(tpos, wpos)
    hh = jnp.arange(NSA_KV_HEADS)[:, None, None]

    def item(b):
        ib = idx[b]
        jc = jnp.minimum(ib, n_past_blk - 1)
        phys = page_table[b][jc // blk_per_page] * blk_per_page + jc % blk_per_page
        g_past = pool_blk[phys, :, :, hh, :]
        g_new = new_blk[b][jnp.clip(ib - n_past_blk, 0, n_new_blk - 1), :, :, hh, :]
        g = jnp.where((ib < n_past_blk)[..., None, None, None], g_past, g_new.astype(g_past.dtype))
        o_s = sel_attend(qrg[b], g, ib, blk_ok[b], tpos)
        o_w, _ = shared_attend(qrg[b], win_rows[b][:, 0], win_rows[b][:, 1], wok)
        return o_s, o_w

    o_slc, o_win = lax.map(item, jnp.arange(b_sz))
    shp = (b_sz, t_len, NSA_HEADS, HEAD_DIM)
    new_win = win_rows[:, win_rows.shape[1] - min(WINDOW, total):]
    return o_cmp.reshape(shp), o_slc.reshape(shp), o_win.reshape(shp), (kvc, kvs, new_win)

def gla_scan(q, k, v, logf, s0, chunk):
    b_sz, t_len, n_h, _ = q.shape
    n_c = t_len // chunk

    def to_chunks(a):
        return a.reshape(b_sz, n_c, chunk, n_h, a.shape[-1]).transpose(1, 0, 3, 2, 4)

    tri = jnp.tril(jnp.ones((chunk, chunk), bool))[:, :, None]

    def step(s, xs):
        qc, kc, vc, fc = xs
        cum = jnp.cumsum(fc, axis=2)
        diff = cum[:, :, :, None, :] - cum[:, :, None, :, :]
        decay = jnp.exp(jnp.where(tri, diff, NEG))
        att = jnp.einsum('bhtk,bhsk,bhtsk->bhts', qc, kc, decay)
        o = jnp.einsum('bhts,bhsv->bhtv', att, vc) + jnp.einsum('bhtk,bhkv->bhtv', qc * jnp.exp(cum), s)
        last = cum[:, :, -1:, :]
        s = jnp.exp(last[:, :, 0, :, None]) * s + jnp.einsum('bhsk,bhsv->bhkv', kc * jnp.exp(last - cum), vc)
        return s, o

    s_fin, o = lax.scan(step, s0, (to_chunks(q), to_chunks(k), to_chunks(v), to_chunks(logf)))
    return o.transpose(1, 0, 3, 2, 4).reshape(b_sz, t_len, n_h, v.shape[-1]), s_fin

def hgrn2(hq, hf, hi, hg, lb, gnorm, s0):
    b_sz, t_len, _ = hq.shape
    shp_k = (b_sz, t_len, HGRN_HEADS, HGRN_DK)
    shp_v = (b_sz, t_len, HGRN_HEADS, HGRN_DV)
    q = (jax.nn.silu(hq.astype(jnp.float32)) * HGRN_DK ** -0.5).reshape(shp_k)
    f = (lb + (1.0 - lb) * jax.nn.sigmoid(hf.astype(jnp.float32))).reshape(shp_k)
    v = hi.astype(jnp.float32).reshape(shp_v)
    o, s_new = gla_scan(q, 1.0 - f, v, jnp.log(f), s0.astype(jnp.float32), math.gcd(t_len, HGRN_CHUNK))
    o = rmsnorm(o, gnorm) * jax.nn.silu(hg.astype(jnp.float32)).reshape(shp_v)
    return o.reshape(b_sz, t_len, HGRN_VW).astype(hq.dtype), s_new

def swiglu(x, w_gate, w_up, w_down):
    return (jax.nn.silu(x @ w_gate) * (x @ w_up)) @ w_down

def moe_dispatch(h, eid, gate, w_gate, w_up, w_down):
    n, d = h.shape
    k = eid.shape[1]
    a = n * k
    ne = w_gate.shape[0]
    flat = eid.reshape(a)
    order = jnp.argsort(flat)
    sorted_e = flat[order]
    counts = jnp.zeros((ne,), jnp.int32).at[flat].add(1)
    padded = (counts + MOE_BLOCK - 1) // MOE_BLOCK * MOE_BLOCK
    pad_end = jnp.cumsum(padded)
    pad_start = pad_end - padded
    start = jnp.cumsum(counts) - counts
    dest = pad_start[sorted_e] + jnp.arange(a, dtype=jnp.int32) - start[sorted_e]
    n_blocks = -(-(a + ne * (MOE_BLOCK - 1)) // MOE_BLOCK)
    rows_total = n_blocks * MOE_BLOCK
    src = jnp.full((rows_total,), n, jnp.int32).at[dest].set((order // k).astype(jnp.int32))
    h_pad = jnp.concatenate([h, jnp.zeros((1, d), h.dtype)], axis=0)
    xb = h_pad[src].reshape(n_blocks, MOE_BLOCK, d)
    blk_e = jnp.minimum(jnp.searchsorted(pad_end, jnp.arange(n_blocks, dtype=jnp.int32) * MOE_BLOCK, side='right'), ne - 1)

    def run(args):
        x_rows, e = args
        return swiglu(x_rows, w_gate[e], w_up[e], w_down[e])

    yb = lax.map(run, (xb, blk_e)).reshape(rows_total, d)
    y = jnp.zeros((a, d), yb.dtype).at[order].set(yb[dest]).reshape(n, k, d)
    return jnp.einsum('nkd,nk->nd', y, gate.astype(y.dtype))

def hier_moe(h, w_rg, b_rg, w_re, b_re, w_gate, w_up, w_down):
    lg = jnp.dot(h, w_rg).astype(jnp.float32) + b_rg.astype(jnp.float32)
    pg_top, g_top = lax.top_k(jax.nn.softmax(lg, axis=-1), 1)
    le_all = jnp.einsum('nd,gde->nge', h, w_re).astype(jnp.float32) + b_re.astype(jnp.float32)
    le = jnp.take_along_axis(le_all, g_top[:, :, None], axis=1)[:, 0]
    lv, e_top = lax.top_k(le, TOP_K_EXPERTS)
    gate = jax.nn.softmax(lv, axis=-1) * pg_top
    eid = g_top * EXPERTS_PER_GROUP + e_top
    return moe_dispatch(h, eid, gate, w_gate, w_up, w_down)

def trunk_layer(x, pos, nsa_fn, s0, norm1, w_in, lb, gnorm, w_proj_a, w_proj_b, w_out, norm2,
                w_rg, b_rg, w_re, b_re, w_gate, w_up, w_down):
    b_sz, t_len, _ = x.shape
    h = rmsnorm(x, norm1)
    z = jnp.einsum('btd,de->bte', h, w_in)
    q, k_c, k_s, k_w, g_nsa, hq, hf, hi, hg, m_a, m_b = jnp.split(z, np.cumsum(IN_SPLITS)[:-1].tolist(), axis=-1)
    q = q.reshape(b_sz, t_len, NSA_HEADS, HEAD_DIM)
    qr = rope(q, pos)
    kv_shape = (b_sz, t_len, 2, NSA_KV_HEADS, HEAD_DIM)
    kvc = k_c.reshape(kv_shape)
    kvs = k_s.reshape(kv_shape)
    kvs = jnp.stack([rope(kvs[:, :, 0], pos), kvs[:, :, 1]], axis=2)
    kvw = k_w.reshape(kv_shape)
    kvw = jnp.stack([rope(kvw[:, :, 0], pos), kvw[:, :, 1]], axis=2)
    o_cmp, o_slc, o_win, nsa_state = nsa_fn(q, qr, kvc, kvs, kvw)
    gate = jax.nn.sigmoid(g_nsa.astype(jnp.float32)).reshape(b_sz, t_len, NSA_HEADS, 3, 1).astype(x.dtype)
    o_a = (gate[..., 0, :] * o_cmp + gate[..., 1, :] * o_slc + gate[..., 2, :] * o_win).reshape(b_sz, t_len, NSA_WIDTH)
    o_b, s_new = hgrn2(hq, hf, hi, hg, lb, gnorm, s0)
    merged = jax.nn.sigmoid(m_a) * (o_a @ w_proj_a) + jax.nn.sigmoid(m_b) * (o_b @ w_proj_b)
    x = x + merged @ w_out
    h2 = rmsnorm(x, norm2).reshape(b_sz * t_len, D_MODEL)
    x = x + hier_moe(h2, w_rg, b_rg, w_re, b_re, w_gate, w_up, w_down).reshape(b_sz, t_len, D_MODEL)
    return x, nsa_state, s_new

def setup_inputs(seed: int = 0) -> dict:
    key = jax.random.key(seed)
    ks = jax.random.split(key, 28)
    n_pages = PAST_LEN // PAGE_SIZE
    n_phys = DEC_BATCH * n_pages * 5 // 4
    win_buf = min(WINDOW, PAST_LEN)
    kv_row = (2, NSA_KV_HEADS, HEAD_DIM)

    def nrm(k, shape, scale):
        return jax.random.normal(k, shape, jnp.float32) * scale

    def gain(k, shape):
        return 1.0 + nrm(k, shape, 0.02)

    page_table = jax.random.permutation(ks[6], n_phys)[: DEC_BATCH * n_pages].reshape(DEC_BATCH, n_pages).astype(jnp.int32)
    return {
        "x_prompt": nrm(ks[0], (BATCH, SEQ, D_MODEL), 1.0),
        "x_sample": nrm(ks[1], (DEC_BATCH, DEC_SEQ, D_MODEL), 1.0),
        "cache_cmp_kv": nrm(ks[2], (DEPTH, n_phys, PAGE_SIZE) + kv_row, 1.0),
        "cache_slc_kv": nrm(ks[3], (DEPTH, n_phys, PAGE_SIZE) + kv_row, 1.0),
        "cache_win_kv": nrm(ks[4], (DEPTH, DEC_BATCH, win_buf) + kv_row, 1.0),
        "state_hgrn": nrm(ks[5], (DEPTH, DEC_BATCH, HGRN_HEADS, HGRN_DK, HGRN_DV), 0.5),
        "page_table": page_table,
        "norm1": gain(ks[7], (DEPTH, D_MODEL)),
        "w_in": nrm(ks[8], (DEPTH, D_MODEL, IN_WIDTH), D_MODEL ** -0.5),
        "cmp_pe": nrm(ks[9], (DEPTH, 2, CMP_BLOCK, HEAD_DIM), 0.1),
        "cmp_w1": nrm(ks[10], (DEPTH, 2, CMP_BLOCK * HEAD_DIM, CMP_HIDDEN), (CMP_BLOCK * HEAD_DIM) ** -0.5),
        "cmp_b1": nrm(ks[11], (DEPTH, 2, CMP_HIDDEN), 0.01),
        "cmp_w2": nrm(ks[12], (DEPTH, 2, CMP_HIDDEN, HEAD_DIM), CMP_HIDDEN ** -0.5),
        "cmp_b2": nrm(ks[13], (DEPTH, 2, HEAD_DIM), 0.01),
        "hgrn_lb_logits": nrm(ks[14], (DEPTH + 1, HGRN_KW), 0.5),
        "hgrn_gnorm": gain(ks[15], (DEPTH, HGRN_DV)),
        "w_proj_a": nrm(ks[16], (DEPTH, NSA_WIDTH, D_MODEL), NSA_WIDTH ** -0.5),
        "w_proj_b": nrm(ks[17], (DEPTH, HGRN_VW, D_MODEL), HGRN_VW ** -0.5),
        "w_out": nrm(ks[18], (DEPTH, D_MODEL, D_MODEL), D_MODEL ** -0.5),
        "norm2": gain(ks[19], (DEPTH, D_MODEL)),
        "w_router_group": nrm(ks[20], (DEPTH, D_MODEL, N_GROUPS), D_MODEL ** -0.5),
        "b_router_group": nrm(ks[21], (DEPTH, N_GROUPS), 0.01),
        "w_router_expert": nrm(ks[22], (DEPTH, N_GROUPS, D_MODEL, EXPERTS_PER_GROUP), D_MODEL ** -0.5),
        "b_router_expert": nrm(ks[23], (DEPTH, N_GROUPS, EXPERTS_PER_GROUP), 0.01),
        "w_exp_gate": nrm(ks[24], (DEPTH, N_EXPERTS, D_MODEL, D_EXPERT), D_MODEL ** -0.5),
        "w_exp_up": nrm(ks[25], (DEPTH, N_EXPERTS, D_MODEL, D_EXPERT), D_MODEL ** -0.5),
        "w_exp_down": nrm(ks[26], (DEPTH, N_EXPERTS, D_EXPERT, D_MODEL), D_EXPERT ** -0.5),
        "final_norm": gain(ks[27], (D_MODEL,)),
    }

def _stack_field(rows, i):
    return jnp.stack([r[i] for r in rows], axis=0)

def reference(x_prompt, x_sample, cache_cmp_kv, cache_slc_kv, cache_win_kv, state_hgrn, page_table,
              norm1, w_in, cmp_pe, cmp_w1, cmp_b1, cmp_w2, cmp_b2, hgrn_lb_logits, hgrn_gnorm,
              w_proj_a, w_proj_b, w_out, norm2, w_router_group, b_router_group, w_router_expert,
              b_router_expert, w_exp_gate, w_exp_up, w_exp_down, final_norm):
    b_sz, s_len = x_prompt.shape[:2]
    past = page_table.shape[1] * PAGE_SIZE
    pos_p = jnp.arange(s_len)
    pos_s = past + jnp.arange(x_sample.shape[1])
    lb_all = jnp.cumsum(jax.nn.softmax(hgrn_lb_logits.astype(jnp.float32), axis=0), axis=0)
    xp, xs = x_prompt, x_sample
    rows_p, rows_s = [], []
    for l in range(DEPTH):
        cmp_params = (cmp_pe[l], cmp_w1[l], cmp_b1[l], cmp_w2[l], cmp_b2[l])
        lw = (norm1[l], w_in[l], lb_all[l], hgrn_gnorm[l], w_proj_a[l], w_proj_b[l], w_out[l], norm2[l],
              w_router_group[l], b_router_group[l], w_router_expert[l], b_router_expert[l],
              w_exp_gate[l], w_exp_up[l], w_exp_down[l])
        nsa_p = functools.partial(nsa_prompt, cmp_params=cmp_params)
        nsa_s = functools.partial(nsa_sample, cache_cmp=cache_cmp_kv[l], cache_slc=cache_slc_kv[l],
                                  cache_win=cache_win_kv[l], page_table=page_table, cmp_params=cmp_params)
        s0 = jnp.zeros((b_sz, HGRN_HEADS, HGRN_DK, HGRN_DV), jnp.float32)
        xp, (pc, ps, pw), ph = trunk_layer(xp, pos_p, nsa_p, s0, *lw)
        xs, (sc, ss, sw), sh = trunk_layer(xs, pos_s, nsa_s, state_hgrn[l], *lw)
        rows_p.append((pc, ps, pw, ph))
        rows_s.append((sc, ss, sw, sh))
    y_prompt = rmsnorm(xp, final_norm)
    y_sample = rmsnorm(xs, final_norm)
    return (y_prompt, y_sample,
            _stack_field(rows_p, 0), _stack_field(rows_s, 0),
            _stack_field(rows_p, 1), _stack_field(rows_s, 1),
            _stack_field(rows_p, 2), _stack_field(rows_s, 2),
            _stack_field(rows_p, 3), _stack_field(rows_s, 3))


_drawn_inputs = setup_inputs


def setup_inputs(seed=0):
    import zlib

    import numpy as np

    out = dict(_drawn_inputs(seed))
    spreads = {}
    factors = {'cache_cmp_kv': 3.258,
     'cmp_b1': 23.885,
     'cmp_b2': 4.669,
     'hgrn_gnorm': 2.843,
     'b_router_group': 28.917,
     'b_router_expert': 9.604,
     'final_norm': 9.542,
     'cache_slc_kv': 2.766,
     'cmp_pe': 3.093}
    for name, (base, spread) in spreads.items():
        noise = np.random.default_rng([zlib.crc32(name.encode()), seed]).standard_normal(out[name].shape)
        drawn = base * np.exp(spread * noise) if base else spread * noise
        out[name] = jnp.asarray(drawn.astype(out[name].dtype))
    for name, factor in factors.items():
        out[name] = (out[name] * factor).astype(out[name].dtype)
    return out
```

```python
import math
from contextlib import ExitStack

import numpy as np

import concourse.bass as bass
from concourse import mybir
from concourse.alu_op_type import AluOpType as ALU

ACT = mybir.ActivationFunctionType
AX = mybir.AxisListType
F32 = mybir.dt.float32
I32 = mybir.dt.int32
U32 = mybir.dt.uint32

P = 128
D = 1024
KD = D // P
SEQ = 1024
NSEQ, NNEW = 8, 4
NSMP = NSEQ * NNEW
QT = SEQ // P
NT = QT + 1
TPAD = NT * P
HD = 64
HEADS, KVH, GRP = 8, 2, 4
KVW = 2 * KVH * HD
PAST, PAGE = 4096, 128
WINDOW = 512
SBLK, NSEL = 64, 16
CBLK, CSTR = 32, 16
PCMP = SEQ // CSTR - 1
SCMP = PAST // CSTR - 1
CHW = CSTR * KVW
NBLK = PAST // SBLK + 1
HH, DK = 4, 128
SUB = 16
ZC = 1304
ZCH = 326
NE, NG, EPG, DE = 32, 4, 8, 512
NOVER = (2 * (SEQ + NSMP)) // (P + 1)
NB = NE + NOVER
ROWS = NB * P
EPS = 1e-6
NEG = -1e9
ATT_SCALE = HD ** -0.5
MASKW = SEQ + WINDOW + P + PCMP + 1


class Kernel:

    def __init__(self, nc, ctx):
        self.nc, self.ctx = nc, ctx
        self.words = 53120
        self.arena = ctx.enter_context(nc.sbuf_tensor("arena", [P, self.words], F32))
        self.ps = ctx.enter_context(nc.psum_tensor("ps", [P, 8, 512], F32))
        self.low, self.high = 0, self.words
        self.programs = {e: [] for e in ("sync", "tensor", "scalar", "vector", "gpsimd")}
        self.pinned = ctx.enter_context(nc.semaphore("pinned"))
        self.stages = self.taken = 0
        self.sems, self.used = ([], []), []
        self.eps = self.keep(1)

    def buf(self, *shape, parts=P):
        n = math.prod(shape)
        a = self.arena[0:parts, self.low:self.low + n]
        self.low += n
        assert self.low <= self.high, (self.low, self.high)
        return shaped(a, shape)

    def keep(self, *shape):
        n = math.prod(shape)
        self.high -= n
        assert self.low <= self.high
        return shaped(self.arena[:, self.high:self.high + n], shape)

    def sem(self, name):
        group = self.sems[self.stages % 2]
        if self.taken == len(group):
            group.append(self.ctx.enter_context(self.nc.semaphore(name)))
        self.taken += 1
        return group[self.taken - 1]

    def pin(self, eng):
        eng.sem_inc(self.pinned, 1)

    def own_sem(self, name):
        return self.ctx.enter_context(self.nc.semaphore(name))

    def stage(self, **programs):
        for e in self.programs:
            self.programs[e].append(programs.get(e))
        self.used.append(self.sems[self.stages % 2][:self.taken])
        self.low = self.taken = 0
        self.stages += 1

    def emit(self, block):
        over = self.ctx.enter_context(self.nc.semaphore("stage_over"))
        cleared = self.ctx.enter_context(self.nc.semaphore("stage_cleared"))

        def run(eng, name):
            for n, program in enumerate(self.programs[name]):
                if name == "vector" and n:
                    for s in self.used[n - 1]:
                        ins = eng.sem_clear(s)
                    ins.then_inc(cleared, 1)
                    eng.wait_ge(cleared, n)
                if program:
                    program(eng)
                eng.drain().then_inc(over, 1)
                eng.wait_ge(over, len(self.programs) * (n + 1))
                eng.drain()

        @block.sync
        def _(sp):
            run(sp, "sync")

        @block.tensor
        def _(pe):
            run(pe, "tensor")

        @block.scalar
        def _(act):
            run(act, "scalar")

        @block.vector
        def _(dve):
            run(dve, "vector")

        @block.gpsimd
        def _(pool):
            run(pool, "gpsimd")


def shaped(a, shape):
    if len(shape) == 1:
        return a
    names = "abcde"[:len(shape)]
    return a.rearrange(f"p ({' '.join(names)}) -> p {' '.join(names)}", **dict(zip(names, shape)))


class Steps:

    def __init__(self, eng, sem, per=0, i=0):
        self.eng, self.sem, self.per, self.i, self.n = eng, sem, per, i, 0

    def __call__(self, ins):
        self.n += 1
        ins.then_inc(self.sem, 1)
        self.eng.wait_ge(self.sem, self.i * self.per + self.n)

    def close(self):
        assert not self.per or self.n == self.per, (self.n, self.per)


def tile(i):
    return bass.ds(i * P, P)


def bc(a, axis, n):
    u = a.unsqueeze(axis)
    shape = list(u.shape)
    shape[axis] = n
    return u.broadcast_to(shape)


def norm_stage(k, d, hT, ident):
    nc = k.nc
    x, h, g = k.buf(2, D), k.buf(2, D), k.buf(D)
    ss = k.buf(2, 4)
    eps_ready = k.sem("n_eps_ready")
    gain_loaded, x_loaded = k.sem("n_gain_loaded"), [k.sem(f"n_x_loaded{u}") for u in (0, 1)]
    squared, h_ready = k.sem("n_squared"), k.sem("n_h_ready")
    transposed, copied = k.sem("n_transposed"), k.sem("n_copied")
    step_sem = k.sem("n_step")

    def sync(sp):
        sp.dma_start(ident, d["ident"]).then_inc(gain_loaded, 16)
        sp.dma_start(g, d["norm1"].partition_broadcast(P).rearrange("p o n -> p (o n)")).then_inc(gain_loaded, 16)
        for t in range(NT):
            if t >= 2:
                sp.wait_ge(h_ready, t - 1)
            sp.dma_start(x[:, t % 2], d["x_all"][t * P:(t + 1) * P, :]).then_inc(x_loaded[t % 2], 16)

    def scalar(act):
        for t in range(NT):
            act.wait_ge(x_loaded[t % 2], 16 * (t // 2 + 1))
            if t >= 2:
                act.wait_ge(transposed, t - 1)
            nc.scalar.activation(h[:, t % 2], x[:, t % 2], ACT.Square,
                                 accum_out=ss[:, t % 2, 0:1]).then_inc(squared, 1)
            if t == 0:
                act.wait_ge(eps_ready, 1)
            act.wait_ge(squared, 2 * t + 1)
            nc.scalar.activation(ss[:, t % 2, 1:2], ss[:, t % 2, 0:1], ACT.Sqrt, scale=1.0 / D, bias=k.eps
                                 ).then_inc(squared, 1)

    def vector(dve):
        step = Steps(dve, step_sem)
        nc.vector.memset(k.eps, EPS).then_inc(eps_ready, 1)
        dve.wait_ge(gain_loaded, 32)
        for t in range(NT):
            dve.wait_ge(squared, 2 * t + 2)
            s = ss[:, t % 2]
            step(nc.vector.reciprocal(s[:, 2:3], s[:, 1:2]))
            nc.vector.scalar_tensor_tensor(out=h[:, t % 2], in0=x[:, t % 2], scalar=s[:, 2:3], in1=g,
                                           op0=ALU.mult, op1=ALU.mult).then_inc(h_ready, 1)
            dve.wait_ge(transposed, t + 1)
            for b in range(2):
                ins = nc.vector.tensor_copy(hT[:, 4 * b:4 * b + 4, t * P:(t + 1) * P],
                                            k.ps[:, 2 * (t % 2) + b].rearrange("p (c n) -> p c n", c=4))
            ins.then_inc(copied, 1)

    def tensor(pe):
        for t in range(NT):
            pe.wait_ge(h_ready, t + 1)
            if t >= 2:
                pe.wait_ge(copied, t - 1)
            for c in range(KD):
                ins = nc.tensor.transpose(k.ps[:, 2 * (t % 2) + c // 4, (c % 4) * P:(c % 4 + 1) * P],
                                          h[:, t % 2, c * P:(c + 1) * P], ident)
            ins.then_inc(transposed, 1)

    k.stage(sync=sync, scalar=scalar, vector=vector, tensor=tensor)


def project_rows_stage(k, name, hT, w, out, chunks, width):
    nc = k.nc
    wbuf = k.buf(2, KD, width)
    z = k.buf(2, NT, width)
    w_loaded = [k.sem(f"{name}_w_loaded{u}") for u in (0, 1)]
    w_used = [k.sem(f"{name}_w_used{u}") for u in (0, 1)]
    multiplied = k.sem(f"{name}_multiplied")
    act_copied, dve_copied = k.sem(f"{name}_act_copied"), k.sem(f"{name}_dve_copied")
    stored = [k.sem(f"{name}_stored{u}") for u in (0, 1)]
    NA, NV = (NT + 1) // 2, NT // 2
    rounds = chunks // 2

    def sync(sp):
        with sp.Fori(0, rounds) as i:
            for u in range(2):
                sp.wait_ge(w_used[u], i + 1)
                sp.dma_start(wbuf[:, u], w[bass.ds(2 * i + u, 1)].rearrange("o p (c n) -> (o p) c n", c=KD)
                             ).then_inc(w_loaded[u], 16)

    def bank(t):
        return t % 4

    def tensor(pe):
        for u in range(2):
            pe.sem_inc(w_used[u], 1)
        with pe.Fori(0, rounds) as i:
            for u in range(2):
                pe.wait_ge(w_loaded[u], 16 * i + 16)
                for t in range(NT):
                    if t % 2 == 0:
                        pe.wait_ge(act_copied, (2 * i + u) * NA + max(0, t // 2 - 1) + 1)
                    else:
                        pe.wait_ge(dve_copied, (2 * i + u) * NV + max(0, t // 2 - 1) + 1)
                    for c in range(KD):
                        ins = nc.tensor.matmul(k.ps[:, bank(t), 0:width], hT[:, c, t * P:(t + 1) * P],
                                               wbuf[:, u, c], start=(c == 0), stop=(c == KD - 1))
                    ins.then_inc(multiplied, 1)
                pe.drain().then_inc(w_used[u], 1)

    def scalar(act):
        act.sem_inc(act_copied, 1)
        for u in range(2):
            act.sem_inc(stored[u], 16)
        with act.Fori(0, rounds) as i:
            for u in range(2):
                act.wait_ge(stored[u], 16 * i + 16)
                for t in range(0, NT, 2):
                    act.wait_ge(multiplied, (2 * i + u) * NT + t + 1)
                    nc.scalar.activation(z[:, u, t], k.ps[:, bank(t), 0:width], ACT.Copy
                                         ).then_inc(act_copied, 1)
                act.wait_ge(act_copied, (2 * i + u + 1) * NA + 1)
                act.wait_ge(dve_copied, (2 * i + u + 1) * NV + 1)
                act.dma_start(out.rearrange("(t p) (c n) -> p t c n", p=P, n=width)[:, :, bass.ds(2 * i + u, 1), :]
                              .rearrange("p t o n -> p t (o n)"),
                              z[:, u]).then_inc(stored[u], 16)
        for u in range(2):
            act.wait_ge(stored[u], 16 * rounds + 16)

    def vector(dve):
        dve.sem_inc(dve_copied, 1)
        with dve.Fori(0, rounds) as i:
            for u in range(2):
                dve.wait_ge(stored[u], 16 * i + 16)
                for t in range(1, NT, 2):
                    dve.wait_ge(multiplied, (2 * i + u) * NT + t + 1)
                    nc.vector.tensor_copy(z[:, u, t], k.ps[:, bank(t), 0:width]).then_inc(dve_copied, 1)

    k.stage(sync=sync, tensor=tensor, scalar=scalar, vector=vector)


def project_columns_stage(k, hT, w, out, blocks):
    nc = k.nc
    W3 = TPAD // 3
    wbuf, z = k.buf(2, KD, P), k.buf(2, TPAD)
    w_loaded = [k.sem(f"pc_w_loaded{u}") for u in (0, 1)]
    w_used = [k.sem(f"pc_w_used{u}") for u in (0, 1)]
    multiplied, act_copied, dve_copied = k.sem("pc_multiplied"), k.sem("pc_act_copied"), k.sem("pc_dve_copied")
    stored = [k.sem(f"pc_stored{u}") for u in (0, 1)]
    rounds = blocks // 2

    def sync(sp):
        with sp.Fori(0, rounds) as i:
            for u in range(2):
                sp.wait_ge(w_used[u], i + 1)
                sp.dma_start(wbuf[:, u], w[bass.ds(2 * i + u, 1)].rearrange("o p (c n) -> (o p) c n", c=KD)
                             ).then_inc(w_loaded[u], 16)

    def tensor(pe):
        for u in range(2):
            pe.sem_inc(w_used[u], 1)
        with pe.Fori(0, rounds) as i:
            for u in range(2):
                pe.wait_ge(w_loaded[u], 16 * i + 16)
                pe.wait_ge(act_copied, (2 * i + u) * 2 + 2)
                pe.wait_ge(dve_copied, (2 * i + u) + 1)
                for g in range(3):
                    for c in range(KD):
                        ins = nc.tensor.matmul(k.ps[:, 3 * u + g, 0:W3], wbuf[:, u, c],
                                               hT[:, c, g * W3:(g + 1) * W3], start=(c == 0), stop=(c == KD - 1))
                    ins.then_inc(multiplied, 1)
                pe.drain().then_inc(w_used[u], 1)

    def scalar(act):
        act.sem_inc(act_copied, 4)
        for u in range(2):
            act.sem_inc(stored[u], 16)
        with act.Fori(0, rounds) as i:
            for u in range(2):
                act.wait_ge(stored[u], 16 * i + 16)
                for g in (0, 2):
                    act.wait_ge(multiplied, (2 * i + u) * 3 + g + 1)
                    nc.scalar.activation(z[:, u, g * W3:(g + 1) * W3], k.ps[:, 3 * u + g, 0:W3], ACT.Copy
                                         ).then_inc(act_copied, 1)
                act.wait_ge(act_copied, (2 * i + u) * 2 + 6)
                act.wait_ge(dve_copied, (2 * i + u) + 3)
                act.dma_start(out[bass.ds(2 * i + u, 1)].rearrange("o p n -> (o p) n"), z[:, u]
                              ).then_inc(stored[u], 16)
        for u in range(2):
            act.wait_ge(stored[u], 16 * rounds + 16)

    def vector(dve):
        dve.sem_inc(dve_copied, 2)
        with dve.Fori(0, rounds) as i:
            for u in range(2):
                dve.wait_ge(stored[u], 16 * i + 16)
                dve.wait_ge(multiplied, (2 * i + u) * 3 + 2)
                nc.vector.tensor_copy(z[:, u, W3:2 * W3], k.ps[:, 3 * u + 1, 0:W3]).then_inc(dve_copied, 1)

    k.stage(sync=sync, tensor=tensor, scalar=scalar, vector=vector)


def rotary_stage(k, d, res, ident):
    nc = k.nc
    NR = HEADS + 2 * KVH
    z, tab = k.buf(ZC), k.buf(HD)
    rin, ro, t = k.buf(NR, HD), k.buf(NR, HD), k.buf(4, NR, HD // 2)
    skv, wkv = k.buf(KVW), k.buf(KVW)
    z_loaded, turned, transposed = k.sem("r_z_loaded"), k.sem("r_turned"), k.sem("r_transposed")
    act_copied, dve_copied = k.sem("r_act_copied"), k.sem("r_dve_copied")
    stored, step_sem, rows_out = k.sem("r_stored"), k.sem("r_step"), k.sem("r_rows_out")
    H2 = HD // 2
    PER = 10

    def sync(sp):
        with sp.Fori(0, NT) as i:
            sp.wait_ge(stored, 32 * i + 32)
            sp.dma_start(z, d["zn"][tile(i), :]).then_inc(z_loaded, 16)
            sp.dma_start(tab, d["rope"][tile(i), :]).then_inc(z_loaded, 16)
        sp.wait_ge(stored, 32 * NT + 32)
        for src, new_p, new_s in ((d["zn"][:, 512:512 + KVW], "cmp_p", "cmp_s"), (d["slc_rows"], "slc_p", "slc_s")):
            sp.dma_start(d[new_p], src[0:SEQ, :]).then_inc(rows_out, 16)
            sp.dma_start(d[new_s], src[SEQ:SEQ + NSMP, :]).then_inc(rows_out, 16)
        sp.dma_start(d["win_p"], d["win_rows"][SEQ - WINDOW:SEQ, :]).then_inc(rows_out, 16)
        sp.dma_start(d["win_s"][:, WINDOW - NNEW:WINDOW, :],
                     d["win_rows"][SEQ:SEQ + NSMP, :].rearrange("(b t) n -> b t n", t=NNEW)).then_inc(rows_out, 16)
        sp.dma_start(d["win_s"][:, 0:WINDOW - NNEW, :], d["cache_win"][:, NNEW:WINDOW, :]).then_inc(rows_out, 16)
        sp.wait_ge(rows_out, 16 * 7)

    def vector(dve):
        nc.vector.memset(res["kwT"][:, 0:WINDOW], 0.0)
        nc.vector.memset(res["vw"][:, 0:WINDOW // P, :], 0.0)
        with dve.Fori(0, NT) as i:
            step = Steps(dve, step_sem, PER, i)
            dve.wait_ge(z_loaded, 32 * i + 32)
            dve.wait_ge(stored, 32 * i + 32)
            step(nc.vector.tensor_copy(rin[:, 0:HEADS].rearrange("p h n -> p (h n)"), z[:, 0:512]))
            step(nc.vector.tensor_copy(rin[:, 8:10].rearrange("p h n -> p (h n)"), z[:, 768:896]))
            step(nc.vector.tensor_copy(rin[:, 10:12].rearrange("p h n -> p (h n)"), z[:, 1024:1152]))
            x1, x2 = rin[:, :, 0:H2], rin[:, :, H2:HD]
            cos, sin = bc(tab[:, 0:H2], 1, NR), bc(tab[:, H2:HD], 1, NR)
            for n, (a, b) in enumerate(((x1, cos), (x2, sin), (x2, cos), (x1, sin))):
                step(nc.vector.tensor_tensor(t[:, n], a, b, ALU.mult))
            nc.vector.tensor_tensor(ro[:, :, 0:H2], t[:, 0], t[:, 1], ALU.subtract).then_inc(turned, 1)
            nc.vector.tensor_tensor(ro[:, :, H2:HD], t[:, 2], t[:, 3], ALU.add).then_inc(turned, 1)
            dve.wait_ge(turned, 2 * i + 2)
            flat = ro.rearrange("p h n -> p (h n)")
            step(nc.vector.tensor_copy(skv[:, 0:P], flat[:, 512:640]))
            step(nc.vector.tensor_copy(skv[:, P:KVW], z[:, 896:1024]))
            step(nc.vector.tensor_copy(wkv[:, 0:P], flat[:, 640:768]))
            nc.vector.tensor_copy(wkv[:, P:KVW], z[:, 1152:1280]).then_inc(dve_copied, 1)
            nc.vector.tensor_copy(res["vs"][:, bass.ds(i, 1), :], z[:, 896:1024].unsqueeze(1)).then_inc(dve_copied, 1)
            nc.vector.tensor_copy(res["vw"][:, bass.ds(i + WINDOW // P, 1), :], z[:, 1152:1280].unsqueeze(1)
                                  ).then_inc(dve_copied, 1)
            dve.wait_ge(transposed, i + 1)
            nc.vector.tensor_copy(res["qrT"][:, :, tile(i)], k.ps[:, 1].rearrange("p (j n) -> p j n", j=4)
                                  ).then_inc(dve_copied, 1)
            step.close()

    def tensor(pe):
        flat = ro.rearrange("p h n -> p (h n)")
        pe.sem_inc(dve_copied, 4)
        with pe.Fori(0, NT) as i:
            pe.wait_ge(turned, 2 * i + 2)
            pe.wait_ge(stored, 32 * i + 32)
            for j in range(4):
                nc.tensor.transpose(k.ps[:, 0, j * P:(j + 1) * P], z[:, j * P:(j + 1) * P], ident)
                nc.tensor.transpose(k.ps[:, 1, j * P:(j + 1) * P], flat[:, j * P:(j + 1) * P], ident)
            nc.tensor.transpose(k.ps[:, 2, 0:P], flat[:, 512:640], ident)
            nc.tensor.transpose(k.ps[:, 2, P:2 * P], flat[:, 640:768], ident).then_inc(transposed, 1)

    def scalar(act):
        act.sem_inc(stored, 32)
        with act.Fori(0, NT) as i:
            act.wait_ge(transposed, i + 1)
            nc.scalar.activation(res["qT"][:, :, tile(i)], k.ps[:, 0].rearrange("p (j n) -> p j n", j=4), ACT.Copy
                                 ).then_inc(act_copied, 1)
            nc.scalar.activation(res["ksT"][:, tile(i)], k.ps[:, 2, 0:P], ACT.Copy).then_inc(act_copied, 1)
            nc.scalar.activation(res["kwT"][:, bass.ds(i * P + WINDOW, P)], k.ps[:, 2, P:2 * P], ACT.Copy
                                 ).then_inc(act_copied, 1)
            act.wait_ge(act_copied, 3 * i + 3)
            act.wait_ge(dve_copied, 4 * i + 8)
            act.dma_start(d["slc_rows"][tile(i), :], skv).then_inc(stored, 16)
            act.dma_start(d["win_rows"][tile(i), :], wkv).then_inc(stored, 16)

    k.stage(sync=sync, vector=vector, tensor=tensor, scalar=scalar)


class Compress:

    def __init__(self, k, d, name, halves, chunks, ident, ckT, cv):
        self.k, self.d, self.ident, self.ckT, self.cv = k, d, ident, ckT, cv
        self.halves, self.chunks, self.n = halves, chunks, halves * chunks
        self.w1, self.w2 = k.buf(2, 16, P), k.buf(2, HD)
        self.b1, self.pe = k.buf(2), k.buf(2, 16)
        self.b2k, self.b2v, self.c0 = k.buf(1), k.buf(P), k.buf(2)
        self.xT = k.buf(2, 8, KVH * self.n)
        self.x, self.t, self.hid = (k.buf(KVH * self.n) for _ in range(3))
        s = lambda what: k.sem(f"{name}_{what}")
        self.params_loaded, self.chunks_transposed = s("params_loaded"), s("chunks_transposed")
        self.act_copied, self.dve_copied, self.hid_summed = s("act_copied"), s("dve_copied"), s("hid_summed")
        self.cubed, self.sigmoid_ready, self.hid_ready = s("cubed"), s("sigmoid_ready"), s("hid_ready")
        self.kv_summed, self.ckv_ready, self.step = s("kv_summed"), s("ckv_ready"), s("c_step")
        self.c0_summed, self.c0_ready = s("c0_summed"), s("c0_ready")

    def sync_start(self, sp):
        d = self.d
        for to, src in ((self.w1, d["cmp_w1"].rearrange("p (c j n) -> p c j n", c=2, j=16)),
                        (self.w2, d["cmp_w2"].rearrange("p (c n) -> p c n", c=2)), (self.b1, d["cmp_b1"]),
                        (self.pe, d["pe"].rearrange("p (c j) -> p c j", c=2)), (self.b2k, d["cmp_b2k"]),
                        (self.b2v, d["cmp_b2v"].partition_broadcast(P).rearrange("p o n -> p (o n)"))):
            sp.dma_start(to, src).then_inc(self.params_loaded, 16)

    def pe_start(self, pe):
        nc, ps = self.k.nc, self.k.ps
        pe.wait_ge(self.params_loaded, 96)
        for c in range(2):
            for j in range(16):
                ins = nc.tensor.matmul(ps[:, 7, c:c + 1], self.w1[:, c, j], self.pe[:, c, j:j + 1],
                                       start=(j == 0), stop=(j == 15))
        ins.then_inc(self.c0_summed, 1)
        pe.sem_inc(self.hid_summed, 2)
        pe.sem_inc(self.kv_summed, 1)

    def dve_start(self, dve):
        dve.wait_ge(self.c0_summed, 1)
        self.k.nc.vector.tensor_tensor(self.c0, self.k.ps[:, 7, 0:2], self.b1, ALU.add).then_inc(self.c0_ready, 1)
        dve.wait_ge(self.c0_ready, 1)
        dve.sem_inc(self.dve_copied, 2)
        dve.sem_inc(self.hid_ready, 2)
        dve.sem_inc(self.ckv_ready, 1)
        self.k.nc.vector.memset(self.t, 0.0).then_inc(self.c0_ready, 1)
        dve.wait_ge(self.c0_ready, 2)

    def act_start(self, act):
        act.sem_inc(self.act_copied, 2)

    def turn(self, pe, it, c, source):
        nc, ps, n = self.k.nc, self.k.ps, self.n
        for s2 in range(8):
            m = c * 8 + s2
            pe.wait_ge(self.act_copied if m % 2 == 0 else self.dve_copied, it * 8 + m // 2 + 1)
            for h in range(KVH):
                for half in range(self.halves):
                    o = h * n + half * self.chunks
                    lo = ((c * KVH + h) * CSTR + 2 * s2) * HD
                    ins = nc.tensor.transpose(ps[:, s2 % 4, o:o + self.chunks], source(half)[:, lo:lo + P],
                                              self.ident[0:self.chunks, 0:self.chunks])
            ins.then_inc(self.chunks_transposed, 1)

    def hidden(self, pe, it, c, parts=(0, 1)):
        nc, ps, n = self.k.nc, self.k.ps, self.n
        if 0 in parts:
            pe.wait_ge(self.act_copied, it * 8 + 4 * c + 6)
            pe.wait_ge(self.dve_copied, it * 8 + 4 * c + 6)
            pe.wait_ge(self.hid_ready, it * 2 + c + 1)
        out = ps[:, 4 + c, 0:KVH * n].rearrange("p (h n) -> p h n", h=KVH)[:, :, 0:n - 1]
        for part in parts:
            for s2 in range(8):
                x = self.xT[:, c, s2].rearrange("p (h n) -> p h n", h=KVH)[:, :, part:part + n - 1]
                ins = nc.tensor.matmul(out, self.w1[:, c, part * 8 + s2], x,
                                       start=(part + s2 == 0), stop=(part + s2 == 8))
        if 1 in parts:
            ins.then_inc(self.hid_summed, 1)

    def keys_values(self, pe, it, c):
        nc, ps, n = self.k.nc, self.k.ps, self.n
        pe.wait_ge(self.ckv_ready, it + 1)
        pe.wait_ge(self.hid_ready, it * 2 + c + 3)
        hid = self.hid.rearrange("p (h n) -> p h n", h=KVH)
        for h in range(KVH):
            if c == 0:
                ins = nc.tensor.matmul(ps[h * HD:(h + 1) * HD, 6, 0:n - 1], self.w2[:, 0], hid[:, h, 0:n - 1],
                                       start=True, stop=True)
            else:
                for b in range(self.halves):
                    rows = min(P, n - 1 - b * P)
                    ins = nc.tensor.matmul(ps[0:rows, 7, b * P + h * HD:b * P + (h + 1) * HD],
                                           hid[:, h, b * P:b * P + rows], self.w2[:, 1], start=True, stop=True)
        ins.then_inc(self.kv_summed, 1)

    def copies(self, eng, it, c, pieces):
        nc, ps, w = self.k.nc, self.k.ps, KVH * self.n
        eng.wait_ge(self.hid_summed, it * 2 + c + 1)
        for s2 in pieces:
            eng.wait_ge(self.chunks_transposed, it * 16 + c * 8 + s2 + 1)
            if s2 % 2 == 0:
                nc.scalar.activation(self.xT[:, c, s2], ps[:, s2 % 4, 0:w], ACT.Copy).then_inc(self.act_copied, 1)
            else:
                nc.vector.tensor_copy(self.xT[:, c, s2], ps[:, s2 % 4, 0:w]).then_inc(self.dve_copied, 1)

    def sigmoid(self, act, it, c):
        act.wait_ge(self.cubed, it * 2 + c + 1)
        self.k.nc.scalar.activation(self.t, self.t, ACT.Sigmoid, scale=2.0 * math.sqrt(2.0 / math.pi)
                                    ).then_inc(self.sigmoid_ready, 1)

    def heads(self, a):
        return a.rearrange("p (h n) -> p h n", h=KVH)[:, :, 0:self.n - 1]

    def cube(self, dve, it, c):
        nc, ps, n = self.k.nc, self.k.ps, self.n
        step = Steps(dve, self.step, 6 + self.halves, it)
        step.n = 3 * c
        dve.wait_ge(self.hid_summed, it * 2 + c + 3)
        x, t = self.heads(self.x), self.heads(self.t)
        step(nc.vector.tensor_scalar(x, self.heads(ps[:, 4 + c, 0:KVH * n]), self.c0[:, c:c + 1], None, ALU.add))
        step(nc.vector.tensor_tensor(t, x, x, ALU.mult))
        step(nc.vector.tensor_scalar(t, t, 0.044715, 1.0, ALU.mult, ALU.add))
        nc.vector.tensor_tensor(t, t, x, ALU.mult).then_inc(self.cubed, 1)

    def gelu(self, dve, it, c):
        dve.wait_ge(self.sigmoid_ready, it * 2 + c + 1)
        dve.wait_ge(self.kv_summed, it * 2 + c + 1)
        self.k.nc.vector.tensor_tensor(self.heads(self.hid), self.heads(self.t), self.heads(self.x), ALU.mult
                                       ).then_inc(self.hid_ready, 1)

    def biases(self, dve, it):
        nc, ps, n = self.k.nc, self.k.ps, self.n
        step = Steps(dve, self.step, 6 + self.halves, it)
        step.n = 6
        dve.wait_ge(self.kv_summed, it * 2 + 2 + 1)
        step(nc.vector.tensor_scalar(self.ckT[:, 0:n - 1], ps[:, 6, 0:n - 1], self.b2k, None, ALU.add))
        for b in range(self.halves):
            rows = min(P, n - 1 - b * P)
            ins = nc.vector.tensor_tensor(self.cv[0:rows, b * P:(b + 1) * P], ps[0:rows, 7, b * P:(b + 1) * P],
                                          self.b2v[0:rows], ALU.add)
            if b < self.halves - 1:
                step(ins)
        ins.then_inc(self.ckv_ready, 1)
        step.close()


def prompt_compress_stage(k, d, res, ident):
    nc = k.nc
    n = SEQ // CSTR
    x = k.buf(CHW)
    comp = Compress(k, d, "pcmp", 1, n, ident, res["ckT"], res["cv"])
    rows_loaded = k.sem("pc_rows_loaded")

    def sync(sp):
        comp.sync_start(sp)
        for ch in range(2 * KVH):
            sp.dma_start(x[0:n, ch * CSTR * HD:(ch + 1) * CSTR * HD].rearrange("p (s n) -> p s n", s=CSTR),
                         d["zn"].rearrange("(p s) c -> p s c", s=CSTR)[0:n, :, 512 + ch * HD:512 + (ch + 1) * HD]
                         ).then_inc(rows_loaded, 16)

    def tensor(pe):
        comp.pe_start(pe)
        pe.wait_ge(rows_loaded, 64)
        comp.turn(pe, 0, 0, lambda half: x[0:n])
        comp.hidden(pe, 0, 0)
        comp.turn(pe, 0, 1, lambda half: x[0:n])
        comp.keys_values(pe, 0, 0)
        comp.hidden(pe, 0, 1)
        comp.keys_values(pe, 0, 1)

    def scalar(act):
        comp.act_start(act)
        for c in range(2):
            comp.copies(act, 0, c, range(0, 8, 2))
            comp.sigmoid(act, 0, c)

    def vector(dve):
        comp.dve_start(dve)
        for c in range(2):
            comp.copies(dve, 0, c, range(1, 8, 2))
            comp.cube(dve, 0, c)
            comp.gelu(dve, 0, c)
        comp.biases(dve, 0)

    k.stage(sync=sync, tensor=tensor, scalar=scalar, vector=vector)


def prompt_stage(k, d, res, ident):
    assert SEQ // SBLK == NSEL
    nc, ps = k.nc, k.ps
    WW = WINDOW + P
    NPAIR = QT // 2
    masks, s = k.buf(MASKW), k.buf(2, MASKW)
    q, qr, kw = k.buf(4, P), k.buf(4, P), k.buf(WW)
    vw = k.buf(WW // P, P)
    pT, o = k.buf(2, 14, P), k.buf(3, HEADS, HD)
    mx, nb, rs, ri = (k.buf(2, 4) for _ in range(4))
    zero, zeroed, cleared = k.buf(D), k.sem("p_zero_ready"), k.sem("p_rows_cleared")
    masks_loaded, staged = k.sem("p_masks_loaded"), k.sem("p_staged")
    scores_ready, scores_read = k.sem("p_scores_ready"), k.sem("p_scores_read")
    probs_ready = k.sem("p_probs_ready")
    group_turned = [k.sem(f"p_group_turned{g}") for g in range(4)]
    group_copied = [k.sem(f"p_group_copied{g}") for g in range(4)]
    out_summed, out_read, stored = k.sem("p_out_summed"), k.sem("p_out_read"), k.sem("p_stored")
    step_sem = k.sem("p_step")
    PER = 8 * (1 + 2 + 2)

    class Pair:

        def __init__(self, m):
            self.m = m
            self.keys = 2 * (m + 1) * P
            self.first = max(0, WINDOW // P - (2 * m + 1))
            self.window = WW - self.first * P
            lo = self.keys + self.window
            self.cuts = ((0, self.keys, 0), (self.keys, lo, SEQ + self.first * P), (lo, lo + PCMP, SEQ + WW))
            self.blocks = [(0, b, P) for b in range(self.keys // P)] + \
                          [(1, b, P) for b in range(self.window // P)] + [(2, 0, PCMP)]
            self.groups = -(-len(self.blocks) // 4)

    pairs = [Pair(m) for m in range(NPAIR)]
    copies_before = [[sum(16 for p in pairs[:m] if p.groups > g) for g in range(4)] for m in range(NPAIR)]

    def gpsimd(pool):
        nc.gpsimd.memset(zero, 0.0).then_inc(zeroed, 1)

    def sync(sp):
        sp.wait_ge(zeroed, 1)
        with sp.Fori(NE, NB) as b:
            sp.dma_start(d["yb"][tile(b), :], zero).then_inc(cleared, 16)
        with sp.Fori(0, QT) as i:
            sp.wait_ge(stored, 16 * i + 16)
            sp.dma_start(masks, d["prompt_masks"][bass.ds(i, 1)].rearrange("o p n -> (o p) n")
                         ).then_inc(masks_loaded, 16)
        sp.wait_ge(cleared, 16 * NOVER)

    def tensor(pe):
        pe.sem_inc(out_read, 1)
        for pair in pairs:
            with pe.Fori(0, 2) as u:
                tensor_tile(pe, pair, 2 * pair.m + u, 16 * pair.m + 8 * u, u)

    def tensor_tile(pe, pair, i, done, u):
        def scores(h):
            j, r = h % 4, slice(h // 4 * HD, (h // 4 + 1) * HD)
            if h:
                pe.wait_ge(scores_read, done + h)
            for c in range(0, pair.keys, 512):
                n = min(512, pair.keys - c)
                nc.tensor.matmul(ps[:, c // 512, 0:n], qr[r, j], res["ksT"][r, c:c + n], start=True, stop=True)
            for c in range(0, pair.window, 512):
                n = min(512, pair.window - c)
                w = pair.first * P + c
                nc.tensor.matmul(ps[:, 2 + c // 512, 0:n], qr[r, j], kw[r, w:w + n], start=True, stop=True)
            nc.tensor.matmul(ps[:, 3, P:P + PCMP], q[r, j], res["ckT"][r, 0:PCMP], start=True, stop=True
                             ).then_inc(scores_ready, 1)

        pe.wait_ge(staged, 4 * i + 4)
        scores(0)
        before = copies_before[pair.m]
        for h in range(HEADS):
            if h + 1 < HEADS:
                scores(h + 1)
            kv = h // 4 * HD
            pe.wait_ge(probs_ready, done + h + 1)
            for g in range(pair.groups):
                if g == 3:
                    pe.wait_ge(group_copied[0], before[0] + 8 * u + h + 2)
                else:
                    pe.wait_ge(group_copied[g], before[g] + 8 * u + h + 1)
                if g == 0 and pair.groups == 4:
                    pe.wait_ge(group_copied[3], before[3] + 8 * u + h + 1)
                if pair.blocks[4 * g][2] < P:
                    k.pin(pe)
                for m, (br, b, n) in enumerate(pair.blocks[4 * g:4 * g + 4]):
                    col = pair.cuts[br][0] + b * P
                    ins = nc.tensor.transpose(ps[0:n, 4 + g % 3, m * P:(m + 1) * P], s[:, h % 2, col:col + n],
                                              ident)
                ins.then_inc(group_turned[g], 1)
            pe.wait_ge(out_read, done + h + 1)
            for m, (br, b, n) in enumerate(pair.blocks):
                if m % 4 == 0:
                    pe.wait_ge(group_copied[m // 4], before[m // 4] + 8 * u + h + 2)
                v = res["vs"][:, b] if br == 0 else vw[:, pair.first + b] if br == 1 else res["cv"]
                lo, hi, _ = pair.cuts[br]
                ins = nc.tensor.matmul(ps[:, 7, br * HD:(br + 1) * HD], pT[0:n, h % 2, m], v[0:n, kv:kv + HD],
                                       start=(b == 0), stop=((b + 1) * P >= hi - lo))
            ins.then_inc(out_summed, 1)

    def scalar(act):
        for g in range(4):
            act.sem_inc(group_copied[g], 1)
        act.sem_inc(stored, 16)
        for pair in pairs:
            with act.Fori(0, 2) as u:
                scalar_tile(act, pair, 2 * pair.m + u, 16 * pair.m + 8 * u, u)
        act.wait_ge(stored, 16 * QT + 16)

    def scalar_tile(act, pair, i, done, u):
        before = copies_before[pair.m]
        for h in range(HEADS):
            act.wait_ge(scores_read, done + h + 1)
            for br, (lo, hi, _) in enumerate(pair.cuts):
                ins = nc.scalar.activation(s[:, h % 2, lo:hi], s[:, h % 2, lo:hi], ACT.Exp, scale=ATT_SCALE,
                                           bias=nb[:, h % 2, br:br + 1], accum_out=rs[:, h % 2, br:br + 1])
            ins.then_inc(probs_ready, 1)
            for g in range(pair.groups):
                act.wait_ge(group_turned[g], before[g] + 8 * u + h + 1)
                blocks = pair.blocks[4 * g:4 * g + 4]
                full = sum(n == P for _, _, n in blocks)
                bank = ps[:, 4 + g % 3]
                if full:
                    ins = nc.scalar.activation(pT[:, h % 2, 4 * g:4 * g + full].rearrange("p b n -> p (b n)"),
                                               bank[:, 0:full * P], ACT.Copy)
                if full < len(blocks):
                    ins = nc.scalar.activation(pT[0:PCMP, h % 2, 4 * g + full],
                                               bank[0:PCMP, full * P:(full + 1) * P], ACT.Copy)
                ins.then_inc(group_copied[g], 1)
        act.wait_ge(out_read, done + 8 + 1)
        act.dma_start(d["branches"][:, tile(i), :].rearrange("b p n -> p b n"),
                      o.rearrange("p b h n -> p b (h n)")).then_inc(stored, 16)

    def vector(dve):
        for pair in pairs:
            with dve.Fori(0, 2) as u:
                vector_tile(dve, pair, 2 * pair.m + u, 16 * pair.m + 8 * u)

    def vector_tile(dve, pair, i, done):
        step = Steps(dve, step_sem, PER, i)
        dve.wait_ge(stored, 16 * i + 16)
        nc.vector.tensor_copy(q, res["qT"][:, :, tile(i)]).then_inc(staged, 1)
        nc.vector.tensor_copy(qr, res["qrT"][:, :, tile(i)]).then_inc(staged, 1)
        nc.vector.tensor_copy(kw, res["kwT"][:, bass.ds(i * P, WW)]).then_inc(staged, 1)
        nc.vector.tensor_copy(vw, res["vw"][:, bass.ds(i, WW // P), :]).then_inc(staged, 1)
        dve.wait_ge(masks_loaded, 16 * i + 16)

        def maxima(h):
            w = h % 2
            dve.wait_ge(scores_ready, done + h + 1)
            k.pin(dve)
            for br, (lo, hi, at) in enumerate(pair.cuts):
                banks = (ps[:, 0:2], ps[:, 2:4], ps[:, 3:4, P:P + PCMP])[br].rearrange("p b n -> p (b n)")
                ins = nc.vector.tensor_tensor_reduce(s[:, w, lo:hi], banks[:, 0:hi - lo], masks[:, at:at + hi - lo],
                                                     1.0, -3e38, ALU.add, ALU.max, mx[:, w, br:br + 1])
            step(ins)
            nc.vector.tensor_scalar(nb[:, w, 0:3], mx[:, w, 0:3], -ATT_SCALE, None, ALU.mult
                                    ).then_inc(scores_read, 1)

        def outputs(h):
            w = h % 2
            dve.wait_ge(out_summed, done + h + 1)
            step(nc.vector.tensor_scalar(ri[:, w, 0:3], rs[:, w, 0:3], 1e-30, None, ALU.max))
            step(nc.vector.reciprocal(ri[:, w, 0:3], ri[:, w, 0:3]))
            step(nc.vector.tensor_tensor(ri[:, w, 2:3], ri[:, w, 2:3], masks[:, MASKW - 1:MASKW], ALU.mult))
            for br, ob in enumerate((1, 2, 0)):
                ins = nc.vector.tensor_scalar(o[:, ob, h], ps[:, 7, br * HD:(br + 1) * HD], ri[:, w, br:br + 1],
                                              None, ALU.mult)
                if br == 1:
                    step(ins)
            ins.then_inc(out_read, 1)

        maxima(0)
        for h in range(HEADS):
            if h + 1 < HEADS:
                maxima(h + 1)
            outputs(h)
        step.close()

    k.stage(sync=sync, tensor=tensor, scalar=scalar, vector=vector, gpsimd=gpsimd)


def sample_stage(k, d, res, ident):
    nc, ps = k.nc, k.ps
    R = KVH * GRP * NNEW
    NTILE = 2 * CSTR
    xc, xs = k.buf(2, CHW), k.buf(2, CHW)
    xw = k.buf(4, KVW)
    comp_n = 2 * P
    ckT, cv = k.buf(comp_n), k.buf(2 * P)
    comp = Compress(k, d, "scmp", 2, P, ident, ckT, cv)
    kT = comp.xT[:, 0].rearrange("p a b -> p (a b)")
    s = comp.xT[0:R, 1].rearrange("p a b -> p (a b)")
    sn, sw = k.buf(NNEW + 4)[0:R], k.buf(WINDOW + NNEW)[0:R]
    pT = k.buf(NTILE + 1, R)
    wT, pwT = k.buf(WINDOW), k.buf(5, R)
    q, qr = k.buf(R), k.buf(R)
    knew, vnew, wnew = k.buf(2, NNEW), k.buf(P)[0:NNEW], k.buf(P)[0:NNEW]
    pages, lane, chunk_f, chunk = k.buf(NSEQ * 2), k.buf(1), k.buf(NSEQ * 2), k.buf(NSEQ * 2)
    index = k.buf(4)
    p, pcT = k.buf(comp_n)[0:R], k.buf(2, R)
    cover, same, forced, smask = k.buf(2, NBLK), k.buf(R)[0:R], k.buf(2, NBLK)[0:R], k.buf(WINDOW + NNEW)[0:R]
    imp, score, top = k.buf(NBLK)[0:R], k.buf(3, NBLK)[0:R], k.buf(2, 8)[0:R]
    st, mx = k.buf(17)[0:R], k.buf(NBLK)[0:R]
    o = k.buf(3, P)[0:R]
    NKEYS = 9

    sem = lambda what: k.sem(f"s_{what}")
    consts_loaded, chunk_ready = sem("consts_loaded"), sem("chunk_ready")
    xc_loaded, xs_loaded = k.own_sem("s_xc_loaded"), k.own_sem("s_xs_loaded")
    small_loaded, stored, q_ready, dve_step = sem("small_loaded"), sem("stored"), sem("q_ready"), sem("step")
    keys_turned, keys_copied = sem("keys_turned"), sem("keys_copied")
    scores_ready, scores_copied = sem("scores_ready"), sem("scores_copied")
    cmp_scores_ready, cmp_max, cmp_exp = sem("cmp_scores_ready"), sem("cmp_max"), sem("cmp_exp")
    cmp_probs_ready, cmp_turned, pcT_ready = sem("cmp_probs_ready"), sem("cmp_turned"), sem("pcT_ready")
    cmp_out_summed, imp_ready, cmp_out_read = sem("cmp_out_summed"), sem("imp_ready"), sem("cmp_out_read")
    block_scores_ready, block_scores_read = sem("block_scores_ready"), sem("block_scores_read")
    win_max, win_probs_ready = sem("win_max"), sem("win_probs_ready")
    sel_max, sel_masked, sel_probs_ready = sem("sel_max"), sem("sel_masked"), sem("sel_probs_ready")
    probs_turned, act_pT, dve_pT = sem("probs_turned"), sem("act_pT"), sem("dve_pT")
    out_summed, out_ready = sem("out_summed"), sem("out_ready")

    def sync(sp):
        comp.sync_start(sp)
        for to, src in ((cover, d["cover"].rearrange("p (b n) -> p b n", b=2)), (same, d["same"]),
                        (forced, d["forced"].rearrange("p (b n) -> p b n", b=2)), (smask, d["smask"]),
                        (lane, d["lane8"])):
            sp.dma_start(to, src).then_inc(consts_loaded, 16)
        sp.dma_start(pages.bitcast(I32), d["pages"]).then_inc(consts_loaded, 16)
        sp.sem_inc(stored, 96)

        def small(b):
            sp.dma_start(xw, d["cache_win"][bass.ds(b, 1)].rearrange("o (p s) c -> (o p) s c", s=4)
                         ).then_inc(small_loaded, 16)
            sp.dma_start(vnew, d["slc_rows"][bass.ds(b * NNEW + SEQ, NNEW), P:KVW]).then_inc(small_loaded, 16)
            sp.dma_start(wnew, d["win_rows"][bass.ds(b * NNEW + SEQ, NNEW), P:KVW]).then_inc(small_loaded, 16)

        def store(b):
            sp.wait_ge(out_ready, b + 2)
            for br in range(3):
                for h in range(KVH):
                    sp.dma_start(d["branches"][br, bass.ds(b * NNEW + SEQ, NNEW), h * 256:(h + 1) * 256]
                                 .rearrange("t (g n) -> g t n", g=GRP),
                                 o[h * 16:(h + 1) * 16, br, h * HD:(h + 1) * HD]).then_inc(stored, 16)

        small(0)
        with sp.Fori(0, NSEQ - 1) as b:
            sp.wait_ge(out_summed, b + 1)
            small(b + 1)
            store(b)
        store(NSEQ - 1)
        sp.wait_ge(stored, 96 * NSEQ + 96)

    def gpsimd(pool):
        pool.wait_ge(consts_loaded, 16 * 6)
        nc.gpsimd.tensor_copy(chunk_f, pages.bitcast(I32)).then_inc(chunk_ready, 1)
        pool.wait_ge(chunk_ready, 1)
        nc.gpsimd.tensor_scalar(chunk_f, chunk_f, 8.0, lane, ALU.mult, ALU.add).then_inc(chunk_ready, 1)
        pool.wait_ge(chunk_ready, 2)
        nc.gpsimd.tensor_copy(chunk.bitcast(I32), chunk_f).then_inc(chunk_ready, 1)
        pool.wait_ge(chunk_ready, 3)

        def gather(b, n, x, loaded, cache):
            step = Steps(pool, chunk_ready, 2, b)
            step.n = 3 + n
            k.pin(pool)
            step(nc.gpsimd.tensor_copy(index[:, 2 * n:2 * n + 2].bitcast(I32),
                                       chunk.bitcast(I32)[:, bass.ds(2 * b, 2)]))
            k.pin(pool)
            for half in range(2):
                nc.gpsimd.indirect_dma_start(
                    x[:, half], None, d[cache],
                    bass.IndirectOffsetOnAxis(ap=index[:, 2 * n + half:2 * n + half + 1].bitcast(I32), axis=0)
                ).then_inc(loaded, 16)

        gather(0, 0, xc, xc_loaded, "cache_cmp")
        gather(0, 1, xs, xs_loaded, "cache_slc")
        with pool.Fori(0, NSEQ - 1) as b:
            pool.wait_ge(comp.chunks_transposed, 16 * b + 16)
            gather(b + 1, 0, xc, xc_loaded, "cache_cmp")
            pool.wait_ge(out_summed, b + 1)
            gather(b + 1, 1, xs, xs_loaded, "cache_slc")

    def each_sequence(eng, body):
        with eng.Fori(0, NSEQ - 1) as b:
            body(eng, b, True)
        body(eng, NSEQ - 1, False)

    def tensor(pe):
        comp.pe_start(pe)
        pe.wait_ge(consts_loaded, 16 * 6)
        pe.wait_ge(xc_loaded, 32)
        comp.turn(pe, 0, 0, lambda half: xc[:, half])
        comp.hidden(pe, 0, 0)
        each_sequence(pe, tensor_sequence)

    def tensor_sequence(pe, b, more):
        comp.turn(pe, b, 1, lambda half: xc[:, half])
        pe.wait_ge(block_scores_read, b + 1)
        comp.keys_values(pe, b, 0)
        pe.wait_ge(out_ready, b + 1)
        comp.hidden(pe, b, 1)

        pe.wait_ge(xs_loaded, 32 * b + 32)
        pe.wait_ge(q_ready, 6 * b + 6)
        for g in range(NKEYS + 2):
            if g < NKEYS:
                if g >= 4:
                    pe.wait_ge(keys_copied, NKEYS * b + g - 3)
                if g == 8:
                    pe.wait_ge(small_loaded, 48 * b + 48)
                for m in range(4):
                    n = 4 * g + m
                    keys = xw[:, m, 0:P] if g == 8 else xs[:, n // CSTR, n % CSTR * KVW:n % CSTR * KVW + P]
                    ins = nc.tensor.transpose(ps[:, g % 4, m * P:(m + 1) * P], keys, ident)
                ins.then_inc(keys_turned, 1)
            if g >= 2:
                n = g - 2
                pe.wait_ge(keys_copied, NKEYS * b + n + 1)
                if n == 1:
                    pe.wait_ge(comp.cubed, 2 * b + 2)
                if n >= 2:
                    pe.wait_ge(scores_copied, NKEYS * b + n - 1)
                nc.tensor.matmul(ps[0:R, 4 + n % 2], qr, wT if n == 8 else kT[:, n * 512:(n + 1) * 512],
                                 start=True, stop=True).then_inc(scores_ready, 1)

        pe.wait_ge(cmp_out_read, b + 1)
        comp.keys_values(pe, b, 1)
        pe.wait_ge(ckv_now, b + 2)
        pe.wait_ge(scores_copied, NKEYS * b + 8)
        nc.tensor.matmul(ps[0:R, 5, 0:SCMP], q, ckT[:, 0:SCMP], start=True, stop=True)
        nc.tensor.matmul(ps[0:R, 5, P * 2:P * 2 + NNEW], qr, knew[:, 0], start=True, stop=True)
        nc.tensor.matmul(ps[0:R, 5, P * 2 + NNEW:P * 2 + 2 * NNEW], qr, knew[:, 1], start=True, stop=True
                         ).then_inc(cmp_scores_ready, 1)
        if more:
            pe.wait_ge(xc_loaded, 32 * b + 64)
            comp.turn(pe, b + 1, 0, lambda half: xc[:, half])
        pe.wait_ge(cmp_probs_ready, b + 1)
        k.pin(pe)
        nc.tensor.transpose(ps[:, 6, 0:R], p[:, 0:P], ident[0:R, 0:R])
        nc.tensor.transpose(ps[0:SCMP - P, 6, R:2 * R], p[:, P:SCMP], ident[0:R, 0:R]).then_inc(cmp_turned, 1)
        if more:
            pe.wait_ge(scores_copied, NKEYS * b + 9)
            comp.hidden(pe, b + 1, 0, parts=(0,))
        pe.wait_ge(pcT_ready, b + 1)
        for n, rows in enumerate((P, SCMP - P)):
            nc.tensor.matmul(ps[0:R, 7, 0:P], pcT[0:rows, n], cv[0:rows, n * P:(n + 1) * P],
                             start=(n == 0), stop=(n == 1))
        for n, rows in enumerate((P, SCMP - P)):
            ins = nc.tensor.matmul(ps[0:R, 5, 0:NBLK], pcT[0:rows, n], cover[0:rows, n],
                                   start=(n == 0), stop=(n == 1))
        ins.then_inc(cmp_out_summed, 1)
        pe.wait_ge(imp_ready, b + 1)
        k.pin(pe)
        nc.tensor.matmul(ps[0:R, 6, 0:NBLK], same, imp, start=True, stop=True).then_inc(block_scores_ready, 1)
        if more:
            comp.hidden(pe, b + 1, 0, parts=(1,))

        pe.wait_ge(win_probs_ready, b + 1)
        for n in range(NTILE):
            if n % 16 == 0:
                pe.wait_ge(sel_probs_ready, 2 * b + n // 16 + 1)
                k.pin(pe)
            ins = nc.tensor.transpose(ps[:, n // 16, n % 16 * R:(n % 16 + 1) * R], s[:, n * P:(n + 1) * P],
                                      ident[0:R, 0:R])
            if n % 16 == 15:
                ins.then_inc(probs_turned, 1)
        for n in range(4):
            nc.tensor.transpose(ps[:, 2, n * R:(n + 1) * R], sw[:, n * P:(n + 1) * P], ident[0:R, 0:R])
        nc.tensor.transpose(ps[0:NNEW, 2, 4 * R:5 * R], sw[:, WINDOW:], ident[0:R, 0:R])
        nc.tensor.transpose(ps[0:NNEW, 2, 5 * R:6 * R], sn[:, 0:NNEW], ident[0:R, 0:R]).then_inc(probs_turned, 1)
        pe.wait_ge(act_pT, b + 1)
        pe.wait_ge(dve_pT, b + 1)
        for n in range(NTILE):
            nc.tensor.matmul(ps[0:R, 5, 0:P], pT[:, n],
                             xs[:, n // CSTR, n % CSTR * KVW + P:(n % CSTR + 1) * KVW],
                             start=(n == 0), stop=False)
        nc.tensor.matmul(ps[0:R, 5, 0:P], pT[0:NNEW, NTILE], vnew, start=False, stop=True)
        for n in range(4):
            nc.tensor.matmul(ps[0:R, 5, P:2 * P], pwT[:, n], xw[:, n, P:KVW], start=(n == 0), stop=False)
        nc.tensor.matmul(ps[0:R, 5, P:2 * P], pwT[0:NNEW, 4], wnew, start=False, stop=True).then_inc(out_summed, 1)

    def scalar(act):
        comp.act_start(act)
        comp.copies(act, 0, 0, range(0, 8, 2))
        comp.sigmoid(act, 0, 0)
        each_sequence(act, scalar_sequence)

    def scalar_sequence(act, b, more):
        comp.copies(act, b, 1, range(0, 8, 2))
        for g in range(NKEYS + 2):
            if g == 2:
                comp.sigmoid(act, b, 1)
            if g < NKEYS:
                act.wait_ge(keys_turned, NKEYS * b + g + 1)
                nc.scalar.activation(wT if g == 8 else kT[:, g * 512:(g + 1) * 512], ps[:, g % 4], ACT.Copy
                                     ).then_inc(keys_copied, 1)
            if g >= 2:
                n = g - 2
                act.wait_ge(scores_ready, NKEYS * b + n + 1)
                nc.scalar.activation(sw[:, 0:WINDOW] if n == 8 else s[:, n * 512:(n + 1) * 512],
                                     ps[0:R, 4 + n % 2], ACT.Copy).then_inc(scores_copied, 1)
        act.wait_ge(cmp_max, b + 1)
        nc.scalar.activation(p[:, 0:SCMP], p[:, 0:SCMP], ACT.Exp, scale=ATT_SCALE, bias=st[:, 1:2],
                             accum_out=st[:, 2:3]).then_inc(cmp_exp, 1)
        if more:
            comp.copies(act, b + 1, 0, (0,))
        act.wait_ge(win_max, b + 1)
        nc.scalar.activation(sw, sw, ACT.Exp, scale=ATT_SCALE, bias=st[:, 8:9], accum_out=st[:, 9:10]
                             ).then_inc(win_probs_ready, 1)
        if more:
            comp.copies(act, b + 1, 0, (2, 4, 6))
        act.wait_ge(sel_max, b + 1)
        nc.scalar.activation(sn[:, 0:NNEW], sn[:, 0:NNEW], ACT.Exp, scale=ATT_SCALE, bias=st[:, 4:5],
                             accum_out=st[:, 6:7])
        for half in range(2):
            act.wait_ge(sel_masked, 2 * b + half + 1)
            part = s[:, half * 2048:(half + 1) * 2048]
            nc.scalar.activation(part, part, ACT.Exp, scale=ATT_SCALE, bias=st[:, 4:5],
                                 accum_out=st[:, 15 + half:16 + half]).then_inc(sel_probs_ready, 1)
        act.wait_ge(probs_turned, 3 * b + 1)
        nc.scalar.activation(pT[:, 0:16].rearrange("p n r -> p (n r)"), ps[:, 0], ACT.Copy).then_inc(act_pT, 1)
        if more:
            comp.sigmoid(act, b + 1, 0)

    ckv_now = comp.ckv_ready

    def vector(dve):
        comp.dve_start(dve)
        nc.vector.memset(q, 0.0)
        nc.vector.memset(qr, 0.0).then_inc(comp.c0_ready, 1)
        dve.wait_ge(comp.c0_ready, 3)
        dve.wait_ge(consts_loaded, 16 * 6)
        for one_more in (block_scores_read, out_ready, cmp_out_read):
            dve.sem_inc(one_more, 1)
        comp.copies(dve, 0, 0, range(1, 8, 2))
        comp.cube(dve, 0, 0)
        comp.gelu(dve, 0, 0)
        each_sequence(dve, vector_sequence)

    def vector_sequence(dve, b, more):
        step = Steps(dve, dve_step, PER, b)
        for to, src in ((q, res["qT"]), (qr, res["qrT"])):
            for h in range(KVH):
                r = slice(h * HD, (h + 1) * HD)
                nc.vector.tensor_copy(to[r, h * 16:(h + 1) * 16].rearrange("p (g t) -> p g t", g=GRP),
                                      src[r, :, bass.ds(b * NNEW + SEQ, NNEW)]).then_inc(q_ready, 1)
        nc.vector.tensor_copy(knew[:, 0], res["ksT"][:, bass.ds(b * NNEW + SEQ, NNEW)]).then_inc(q_ready, 1)
        nc.vector.tensor_copy(knew[:, 1], res["kwT"][:, bass.ds(b * NNEW + SEQ + WINDOW, NNEW)]).then_inc(q_ready, 1)
        comp.copies(dve, b, 1, range(1, 8, 2))
        comp.cube(dve, b, 1)
        comp.gelu(dve, b, 1)
        comp.biases(dve, b)

        dve.wait_ge(cmp_scores_ready, b + 1)
        nc.vector.tensor_copy(p[:, 0:SCMP], ps[0:R, 5, 0:SCMP])
        step(nc.vector.tensor_reduce(st[:, 0:1], ps[0:R, 5, 0:SCMP], AX.X, ALU.max))
        nc.vector.tensor_scalar(st[:, 1:2], st[:, 0:1], -ATT_SCALE, None, ALU.mult).then_inc(cmp_max, 1)
        nc.vector.tensor_copy(sn[:, 0:NNEW], ps[0:R, 5, P * 2:P * 2 + NNEW])
        step(nc.vector.tensor_copy(sw[:, WINDOW:], ps[0:R, 5, P * 2 + NNEW:P * 2 + 2 * NNEW]))
        dve.wait_ge(scores_copied, NKEYS * b + 9)
        k.pin(dve)
        step(nc.vector.tensor_tensor_reduce(sw, sw, smask, 1.0, -3e38, ALU.add, ALU.max, st[:, 7:8]))
        nc.vector.tensor_scalar(st[:, 8:9], st[:, 7:8], -ATT_SCALE, None, ALU.mult).then_inc(win_max, 1)
        if more:
            comp.copies(dve, b + 1, 0, (1, 3))
        dve.wait_ge(cmp_exp, b + 1)
        step(nc.vector.tensor_scalar(st[:, 2:3], st[:, 2:3], 1e-30, None, ALU.max))
        step(nc.vector.reciprocal(st[:, 2:3], st[:, 2:3]))
        nc.vector.tensor_scalar(p[:, 0:SCMP], p[:, 0:SCMP], st[:, 2:3], None, ALU.mult).then_inc(cmp_probs_ready, 1)
        if more:
            comp.copies(dve, b + 1, 0, (5, 7))
        dve.wait_ge(cmp_turned, b + 1)
        step(nc.vector.tensor_copy(pcT[:, 0], ps[:, 6, 0:R]))
        nc.vector.tensor_copy(pcT[0:SCMP - P, 1], ps[0:SCMP - P, 6, R:2 * R]).then_inc(pcT_ready, 1)
        for half in range(2):
            a = s[:, half * 2048:(half + 1) * 2048].rearrange("p (s a c) -> p a s c", s=CSTR, c=4)
            ins = nc.vector.tensor_reduce(mx[:, half * 32:(half + 1) * 32], a, AX.XY, ALU.max)
        step(ins)
        k.pin(dve)
        step(nc.vector.tensor_tensor_reduce(sn[:, 0:NNEW], sn[:, 0:NNEW], smask[:, WINDOW:], 1.0, -3e38, ALU.add,
                                            ALU.max, mx[:, NBLK - 1:NBLK]))
        dve.wait_ge(cmp_out_summed, b + 1)
        nc.vector.tensor_copy(imp, ps[0:R, 5, 0:NBLK]).then_inc(imp_ready, 1)
        dve.wait_ge(stored, 96 * b + 96)
        nc.vector.tensor_copy(o[:, 0], ps[0:R, 7, 0:P]).then_inc(cmp_out_read, 1)
        dve.wait_ge(block_scores_ready, b + 1)
        nc.vector.tensor_tensor(score[:, 0], ps[0:R, 6, 0:NBLK], forced[:, 0], ALU.mult
                                ).then_inc(block_scores_read, 1)
        dve.wait_ge(block_scores_read, b + 2)
        step(nc.vector.tensor_tensor(score[:, 0], score[:, 0], forced[:, 1], ALU.add))
        for n in range(NSEL // 8):
            k.pin(dve)
            step(nc.vector.max(top[:, n], score[:, n]))
            k.pin(dve)
            step(nc.vector.match_replace(score[:, n + 1], top[:, n], score[:, n], -3e38))
        step(nc.vector.tensor_scalar(score[:, 0], score[:, 2], -3e38, NEG, ALU.not_equal, ALU.mult))
        step(nc.vector.tensor_tensor(mx[:, 0:NBLK - 1], mx[:, 0:NBLK - 1], score[:, 0, 0:NBLK - 1], ALU.add))
        step(nc.vector.tensor_reduce(st[:, 3:4], mx, AX.X, ALU.max))
        nc.vector.tensor_scalar(st[:, 4:5], st[:, 3:4], -ATT_SCALE, None, ALU.mult).then_inc(sel_max, 1)
        for half in range(2):
            a = s[:, half * 2048:(half + 1) * 2048].rearrange("p (s a c) -> p s a c", s=CSTR, c=4)
            block = bc(bc(score[:, 0, half * 32:(half + 1) * 32], 2, 4), 1, CSTR)
            nc.vector.tensor_tensor(a, a, block, ALU.add).then_inc(sel_masked, 1)
        if more:
            comp.cube(dve, b + 1, 0)
        dve.wait_ge(probs_turned, 3 * b + 2)
        nc.vector.tensor_copy(pT[:, 16:32].rearrange("p n r -> p (n r)"), ps[:, 1])
        dve.wait_ge(probs_turned, 3 * b + 3)
        nc.vector.tensor_copy(pT[0:NNEW, 32], ps[0:NNEW, 2, 5 * R:6 * R])
        nc.vector.tensor_copy(pwT[:, 0:4].rearrange("p n r -> p (n r)"), ps[:, 2, 0:4 * R])
        nc.vector.tensor_copy(pwT[0:NNEW, 4], ps[0:NNEW, 2, 4 * R:5 * R]).then_inc(dve_pT, 1)
        if more:
            comp.gelu(dve, b + 1, 0)
        step(nc.vector.tensor_tensor(st[:, 5:6], st[:, 15:16], st[:, 16:17], ALU.add))
        step(nc.vector.tensor_tensor(st[:, 10:11], st[:, 5:6], st[:, 6:7], ALU.add))
        step(nc.vector.tensor_copy(st[:, 11:12], st[:, 9:10]))
        step(nc.vector.tensor_scalar(st[:, 10:12], st[:, 10:12], 1e-30, None, ALU.max))
        step(nc.vector.reciprocal(st[:, 12:14], st[:, 10:12]))
        dve.wait_ge(out_summed, b + 1)
        step(nc.vector.tensor_scalar(o[:, 1], ps[0:R, 5, 0:P], st[:, 12:13], None, ALU.mult))
        nc.vector.tensor_scalar(o[:, 2], ps[0:R, 5, P:2 * P], st[:, 13:14], None, ALU.mult).then_inc(out_ready, 1)
        step.close()

    PER = 22

    k.stage(sync=sync, tensor=tensor, scalar=scalar, vector=vector, gpsimd=gpsimd)




class Lower:

    def __init__(self, k, d, name):
        self.k, self.d = k, d
        self.logits, self.lb, self.lbc = k.buf(2, HH), k.buf(HH), k.buf(HH)
        self.loaded, self.exp, self.diff = (k.sem(f"{name}_lb_{w}") for w in ("loaded", "exp", "step"))

    def sync(self, sp):
        sp.dma_start(self.logits, self.d["lb_logits"].rearrange("p (a h) -> p a h", a=2)).then_inc(self.loaded, 16)

    def scalar(self, act):
        act.wait_ge(self.diff, 1)
        self.k.nc.scalar.activation(self.lb, self.lb, ACT.Sigmoid).then_inc(self.exp, 1)

    def vector(self, dve):
        nc = self.k.nc
        dve.wait_ge(self.loaded, 16)
        nc.vector.tensor_tensor(self.lb, self.logits[:, 0], self.logits[:, 1], ALU.subtract).then_inc(self.diff, 1)
        dve.wait_ge(self.exp, 1)
        nc.vector.tensor_scalar(self.lbc, self.lb, -1.0, 1.0, ALU.mult, ALU.add).then_inc(self.diff, 1)
        dve.wait_ge(self.diff, 2)


def hgrn_prompt_stage(k, d, ident):
    nc, ps = k.nc, k.ps
    NS = P // SUB
    W = HH * P
    lower = Lower(k, d, "hp")
    hq, hf, v, hg = k.buf(HH, P), k.buf(HH, P), k.buf(W), k.buf(W)
    sq, f, key, cum, ecum, qe, qh = (k.buf(HH, P) for _ in range(7))
    kh = k.buf(HH, NS, P)
    kl, klT, att, S = (k.buf(HH, P) for _ in range(4))
    reset, tri, gn = k.buf(W), k.buf(P), k.buf(P)
    o, osq, sg = k.buf(HH, P), k.buf(HH, P), k.buf(HH, P)
    ss = k.buf(3, HH)
    loaded, consts, act_done, pe_done, dve_out, step_sem, done, state_out = (
        k.sem(f"hp_{w}") for w in ("loaded", "consts_loaded", "act_done", "pe_done", "dve_out", "step", "done",
                                   "state_stored"))
    flat = lambda a: a.rearrange("p h n -> p (h n)")

    def sync(sp):
        lower.sync(sp)
        for to, src in ((reset, d["reset"]), (tri, d["tri"]),
                        (gn, d["gnorm"].partition_broadcast(P).rearrange("p o n -> p (o n)"))):
            sp.dma_start(to, src).then_inc(consts, 16)
        with sp.Fori(0, QT) as i:
            sp.wait_ge(done, 16 * i + 16)
            sp.dma_start(hq, d["zT"][0:HH, :, tile(i)].rearrange("h p n -> p h n")).then_inc(loaded, 16)
            sp.dma_start(hf, d["zT"][HH:2 * HH, :, tile(i)].rearrange("h p n -> p h n")).then_inc(loaded, 16)
            sp.dma_start(v, d["zh"][tile(i), 0:W]).then_inc(loaded, 16)
            sp.dma_start(hg, d["zh"][tile(i), W:2 * W]).then_inc(loaded, 16)
        sp.wait_ge(done, 16 * QT + 16)
        sp.dma_start(d["hgrn_p"].rearrange("h p n -> p h n"), S).then_inc(state_out, 16)
        sp.wait_ge(state_out, 16)

    def scalar(act):
        lower.scalar(act)
        act.sem_inc(done, 16)
        with act.Fori(0, QT) as i:
            act.wait_ge(loaded, 64 * i + 64)
            nc.scalar.activation(flat(f), flat(hf), ACT.Sigmoid).then_inc(act_done, 1)
            nc.scalar.activation(flat(sq), flat(hq), ACT.Sigmoid).then_inc(act_done, 1)
            nc.scalar.activation(flat(sg), hg, ACT.Sigmoid).then_inc(act_done, 1)
            act.wait_ge(dve_out, 7 * i + 1)
            nc.scalar.activation(flat(f), flat(f), ACT.Ln).then_inc(act_done, 1)
            act.wait_ge(dve_out, 7 * i + 2)
            nc.scalar.activation(flat(ecum), flat(cum), ACT.Exp).then_inc(act_done, 1)
            act.wait_ge(dve_out, 7 * i + 3)
            nc.scalar.activation(flat(qh), flat(qh), ACT.Exp).then_inc(act_done, 1)
            for h in range(HH):
                ins = nc.scalar.activation(kl[:, h], cum[:, h], ACT.Exp, scale=-1.0, bias=cum[:, h, P - 1:P])
            ins.then_inc(act_done, 1)
            for h in range(HH):
                for n in range(NS):
                    m = SUB * n + SUB // 2 - 1
                    ins = nc.scalar.activation(kh[:, h, n, 0:SUB * (n + 1)], cum[:, h, 0:SUB * (n + 1)], ACT.Exp,
                                               scale=-1.0, bias=cum[:, h, m:m + 1])
                ins.then_inc(act_done, 1)
            act.wait_ge(pe_done, 7 * i + 5)
            nc.scalar.activation(flat(klT), ps[:, 1], ACT.Copy).then_inc(act_done, 1)
            act.wait_ge(dve_out, 7 * i + 6)
            nc.scalar.activation(ss[:, 1], ss[:, 0], ACT.Sqrt, scale=1.0 / DK, bias=k.eps).then_inc(act_done, 1)
            act.wait_ge(dve_out, 7 * i + 7)
            act.dma_start(d["ob"][tile(i), :], flat(o)).then_inc(done, 16)

    A = 13

    def tensor(pe):
        with pe.Fori(0, QT) as i:
            for h in range(HH):
                pe.wait_ge(q_keys, HH * i + h + 1)
                for n in range(NS):
                    ins = nc.tensor.matmul(ps[:, 0, h * P + SUB * n:h * P + SUB * (n + 1)], kh[:, h, n],
                                           qh[:, h, SUB * n:SUB * (n + 1)], start=True, stop=True)
                ins.then_inc(pe_done, 1)
            pe.wait_ge(dve_out, 7 * i + 4)
            for h in range(HH):
                ins = nc.tensor.transpose(ps[:, 1, h * P:(h + 1) * P], kl[:, h], ident)
            ins.then_inc(pe_done, 1)
            pe.wait_ge(dve_out, 7 * i + 5)
            for h in range(HH):
                c = slice(h * P, (h + 1) * P)
                nc.tensor.matmul(ps[:, 2, c], att[:, h], v[:, c], start=True, stop=False)
                ins = nc.tensor.matmul(ps[:, 2, c], qe[:, h], S[:, h], start=False, stop=True)
            ins.then_inc(pe_done, 1)
            pe.wait_ge(act_done, A * i + 12)
            for h in range(HH):
                c = slice(h * P, (h + 1) * P)
                ins = nc.tensor.matmul(ps[:, 3, c], klT[:, h], v[:, c], start=True, stop=True)
            ins.then_inc(pe_done, 1)

    q_keys = k.sem("hp_q_keys_ready")

    def vector(dve):
        lower.vector(dve)
        dve.wait_ge(consts, 48)
        nc.vector.memset(S.rearrange("p h n -> p (h n)"), 0.0)
        nc.vector.memset(kh.rearrange("p h s n -> p (h s n)"), 0.0).then_inc(q_start, 1)
        dve.wait_ge(q_start, 1)
        with dve.Fori(0, QT) as i:
            step = Steps(dve, step_sem, 11, i)
            dve.wait_ge(done, 16 * i + 16)
            dve.wait_ge(act_done, A * i + 1)
            for h in range(HH):
                ins = nc.vector.tensor_scalar(f[:, h], f[:, h], lower.lbc[:, h:h + 1], lower.lb[:, h:h + 1],
                                              ALU.mult, ALU.add)
            step(ins)
            nc.vector.tensor_scalar(flat(key), flat(f), -1.0, 1.0, ALU.mult, ALU.add).then_inc(dve_out, 1)
            dve.wait_ge(act_done, A * i + 4)
            nc.vector.tensor_tensor_scan(flat(cum), reset, flat(f), 0.0, ALU.mult, ALU.add).then_inc(dve_out, 1)
            dve.wait_ge(dve_out, 7 * i + 2)
            c4 = flat(cum).rearrange("p (g s) -> p g s", s=SUB)
            nc.vector.tensor_tensor(flat(qh).rearrange("p (g s) -> p g s", s=SUB), c4,
                                    c4[:, :, SUB // 2 - 1:SUB // 2].broadcast_to([P, HH * NS, SUB]), ALU.subtract
                                    ).then_inc(dve_out, 1)
            step(nc.vector.scalar_tensor_tensor(out=flat(sq), in0=flat(sq), scalar=DK ** -0.5, in1=flat(hq),
                                                op0=ALU.mult, op1=ALU.mult))
            dve.wait_ge(act_done, A * i + 6)
            step(nc.vector.tensor_tensor(flat(qe), flat(sq), flat(ecum), ALU.mult))
            step(nc.vector.tensor_tensor(flat(qh), flat(sq), flat(qh), ALU.mult))
            dve.wait_ge(act_done, A * i + 7)
            nc.vector.tensor_tensor(flat(kl), flat(kl), flat(key), ALU.mult).then_inc(dve_out, 1)
            for h in range(HH):
                dve.wait_ge(act_done, A * i + 8 + h)
                nc.vector.tensor_tensor(kh[:, h], kh[:, h], bc(key[:, h], 1, NS), ALU.mult).then_inc(q_keys, 1)
            dve.wait_ge(pe_done, 7 * i + 4)
            nc.vector.tensor_tensor(att, ps[:, 0].rearrange("p (h n) -> p h n", h=HH), bc(tri, 1, HH), ALU.mult
                                    ).then_inc(dve_out, 1)
            step(nc.vector.tensor_tensor(flat(sg), flat(sg), hg, ALU.mult))
            step(nc.vector.tensor_tensor(sg, sg, bc(gn, 1, HH), ALU.mult))
            dve.wait_ge(pe_done, 7 * i + 6)
            step(nc.vector.tensor_copy(flat(o), ps[:, 2]))
            step(nc.vector.tensor_tensor(flat(osq), flat(o), flat(o), ALU.mult))
            nc.vector.tensor_reduce(ss[:, 0], osq, AX.X, ALU.add).then_inc(dve_out, 1)
            dve.wait_ge(pe_done, 7 * i + 7)
            for h in range(HH):
                ins = nc.vector.scalar_tensor_tensor(out=S[:, h], in0=S[:, h], scalar=ecum[:, h, P - 1:P],
                                                     in1=ps[:, 3, h * P:(h + 1) * P], op0=ALU.mult, op1=ALU.add)
            step(ins)
            dve.wait_ge(act_done, A * i + 13)
            step(nc.vector.reciprocal(ss[:, 2], ss[:, 1]))
            step(nc.vector.tensor_tensor(o, o, ss[:, 2].unsqueeze(2).broadcast_to([P, HH, P]), ALU.mult))
            nc.vector.tensor_tensor(flat(o), flat(o), flat(sg), ALU.mult).then_inc(dve_out, 1)
            step.close()

    q_start = k.sem("hp_zeroed")
    k.stage(sync=sync, tensor=tensor, scalar=scalar, vector=vector)


def hgrn_sample_stage(k, d, ident):
    nc, ps = k.nc, k.ps
    N = NSMP
    lower = Lower(k, d, "hs")
    hq, hf, sq, f, key, cum, ecum, qe, qh, kh, kl = (k.buf(HH, N) for _ in range(11))
    v, hg, sg, o, osq = (k.buf(HH, DK)[0:N] for _ in range(5))
    klT, oT = k.buf(HH, DK)[0:N], k.buf(HH, N)
    att = k.buf(HH, N)[0:N]
    vm = k.buf(HH, NSEQ, DK)[0:N]
    S = k.buf(HH, NSEQ, DK)
    reset, tri, seqmask, gn = k.buf(HH * N), k.buf(N)[0:N], k.buf(NSEQ)[0:N], k.buf(DK)[0:N]
    ss = k.buf(3, HH)[0:N]
    loaded, act_done, pe_done, dve_out, step_sem, stored = (
        k.sem(f"hs_{w}") for w in ("loaded", "act_done", "pe_done", "dve_out", "step", "stored"))
    flat = lambda a: a.rearrange("p h n -> p (h n)")
    rows = slice(SEQ, SEQ + N)

    def sync(sp):
        lower.sync(sp)
        for to, src in ((hq, d["zT"][0:HH, :, rows].rearrange("h p n -> p h n")),
                        (hf, d["zT"][HH:2 * HH, :, rows].rearrange("h p n -> p h n")),
                        (flat(v), d["zh"][rows, 0:512]), (flat(hg), d["zh"][rows, 512:1024]),
                        (reset, d["reset4"]), (tri, d["blocktri"]), (seqmask, d["seqmask"]),
                        (gn, d["gnorm"].partition_broadcast(N).rearrange("p o n -> p (o n)"))):
            sp.dma_start(to, src).then_inc(loaded, 16)
        for h in range(HH):
            sp.dma_start(S[:, h], d["state"][:, h].rearrange("b p n -> p b n")).then_inc(loaded, 16)
        sp.wait_ge(dve_out, 10)
        for h in range(HH):
            sp.dma_start(d["hgrn_s"][:, h].rearrange("b p n -> p b n"), S[:, h]).then_inc(stored, 16)
        sp.dma_start(d["ob"][rows, :], flat(o)).then_inc(stored, 16)
        sp.wait_ge(stored, 80)

    def scalar(act):
        lower.scalar(act)
        act.wait_ge(loaded, 192)
        nc.scalar.activation(flat(f), flat(hf), ACT.Sigmoid).then_inc(act_done, 1)
        nc.scalar.activation(flat(sq), flat(hq), ACT.Sigmoid).then_inc(act_done, 1)
        nc.scalar.activation(flat(sg), flat(hg), ACT.Sigmoid).then_inc(act_done, 1)
        act.wait_ge(dve_out, 1)
        nc.scalar.activation(flat(f), flat(f), ACT.Ln).then_inc(act_done, 1)
        act.wait_ge(dve_out, 2)
        nc.scalar.activation(flat(ecum), flat(cum), ACT.Exp).then_inc(act_done, 1)
        act.wait_ge(dve_out, 3)
        nc.scalar.activation(flat(kh), flat(qh), ACT.Exp, scale=-1.0).then_inc(act_done, 1)
        act.wait_ge(act_done, 6)
        nc.scalar.activation(flat(qh), flat(qh), ACT.Exp).then_inc(act_done, 1)
        nc.scalar.activation(flat(kl), flat(kl), ACT.Exp).then_inc(act_done, 1)
        act.wait_ge(dve_out, 8)
        nc.scalar.activation(ss[:, 1], ss[:, 0], ACT.Sqrt, scale=1.0 / DK, bias=k.eps[0:N]).then_inc(act_done, 1)

    def tensor(pe):
        pe.wait_ge(dve_out, 5)
        for h in range(HH):
            nc.tensor.matmul(ps[0:N, 0, h * N:(h + 1) * N], kh[:, h], qh[:, h], start=True, stop=True)
            ins = nc.tensor.transpose(ps[0:N, 1, h * DK:(h + 1) * DK], kl[:, h], ident)
        ins.then_inc(pe_done, 1)
        pe.wait_ge(dve_out, 6)
        for h in range(HH):
            nc.tensor.matmul(ps[:, 2, h * N:(h + 1) * N], v[:, h], att[:, h], start=True, stop=False)
            for b in range(NSEQ):
                c = b * NNEW
                ins = nc.tensor.matmul(ps[:, 2, h * N + c:h * N + c + NNEW], S[:, h, b], qe[:, h, c:c + NNEW],
                                       start=False, stop=(b == NSEQ - 1))
        ins.then_inc(pe_done, 1)
        pe.wait_ge(dve_out, 7)
        for h in range(HH):
            ins = nc.tensor.transpose(ps[0:N, 3, h * DK:(h + 1) * DK], oT[:, h], ident)
        ins.then_inc(pe_done, 1)
        for h in range(HH):
            if h >= 2:
                pe.wait_ge(states, h - 1)
            for half in range(2):
                ins = nc.tensor.matmul(ps[:, 4 + 2 * (h % 2) + half], klT[:, h],
                                       vm[:, h, 4 * half:4 * half + 4].rearrange("p b n -> p (b n)"),
                                       start=True, stop=True)
            ins.then_inc(pe_done, 1)

    states = k.sem("hs_states_updated")

    def vector(dve):
        lower.vector(dve)
        step = Steps(dve, step_sem)
        dve.wait_ge(act_done, 1)
        for h in range(HH):
            ins = nc.vector.tensor_scalar(f[:, h], f[:, h], lower.lbc[:, h:h + 1], lower.lb[:, h:h + 1],
                                          ALU.mult, ALU.add)
        step(ins)
        nc.vector.tensor_scalar(flat(key), flat(f), -1.0, 1.0, ALU.mult, ALU.add).then_inc(dve_out, 1)
        dve.wait_ge(act_done, 4)
        nc.vector.tensor_tensor_scan(flat(cum), reset, flat(f), 0.0, ALU.mult, ALU.add).then_inc(dve_out, 1)
        dve.wait_ge(dve_out, 2)
        c4, q4, l4 = (flat(a).rearrange("p (g s) -> p g s", s=NNEW) for a in (cum, qh, kl))
        n4 = [P, HH * NSEQ, NNEW]
        step(nc.vector.tensor_tensor(l4, c4[:, :, NNEW - 1:NNEW].broadcast_to(n4), c4, ALU.subtract))
        nc.vector.tensor_tensor(q4, c4, c4[:, :, 1:2].broadcast_to(n4), ALU.subtract).then_inc(dve_out, 1)
        step(nc.vector.scalar_tensor_tensor(out=flat(sq), in0=flat(sq), scalar=DK ** -0.5, in1=flat(hq),
                                            op0=ALU.mult, op1=ALU.mult))
        dve.wait_ge(act_done, 8)
        step(nc.vector.tensor_tensor(flat(qe), flat(sq), flat(ecum), ALU.mult))
        step(nc.vector.tensor_tensor(flat(qh), flat(sq), flat(qh), ALU.mult))
        nc.vector.tensor_tensor(flat(kh), flat(kh), flat(key), ALU.mult).then_inc(dve_out, 1)
        nc.vector.tensor_tensor(flat(kl), flat(kl), flat(key), ALU.mult).then_inc(dve_out, 1)
        for h in range(HH):
            ins = nc.vector.tensor_tensor(vm[:, h], bc(v[:, h], 1, NSEQ),
                                          seqmask.unsqueeze(2).broadcast_to([N, NSEQ, DK]), ALU.mult)
        dve.wait_ge(pe_done, 1)
        step(nc.vector.tensor_copy(flat(klT), ps[0:N, 1]))
        nc.vector.tensor_tensor(att, ps[0:N, 0, 0:HH * N].rearrange("p (h n) -> p h n", h=HH), bc(tri, 1, HH),
                                ALU.mult).then_inc(dve_out, 1)
        dve.wait_ge(pe_done, 2)
        nc.vector.tensor_copy(flat(oT), ps[:, 2, 0:HH * N]).then_inc(dve_out, 1)
        dve.wait_ge(pe_done, 3)
        step(nc.vector.tensor_copy(flat(o), ps[0:N, 3]))
        step(nc.vector.tensor_tensor(flat(osq), flat(o), flat(o), ALU.mult))
        nc.vector.tensor_reduce(ss[:, 0], osq, AX.X, ALU.add).then_inc(dve_out, 1)
        for h in range(HH):
            dve.wait_ge(pe_done, 4 + h)
            last = ecum[:, h].rearrange("p (b t) -> p b t", t=NNEW)[:, :, NNEW - 1:NNEW]
            step(nc.vector.tensor_tensor(S[:, h], S[:, h], last.broadcast_to([P, NSEQ, DK]), ALU.mult))
            for half in range(2):
                g = S[:, h, 4 * half:4 * half + 4].rearrange("p b n -> p (b n)")
                ins = nc.vector.tensor_tensor(g, g, ps[:, 4 + 2 * (h % 2) + half], ALU.add)
            ins.then_inc(states, 1)
        step(nc.vector.tensor_tensor(flat(sg), flat(sg), flat(hg), ALU.mult))
        step(nc.vector.tensor_tensor(sg, sg, bc(gn, 1, HH), ALU.mult))
        dve.wait_ge(act_done, 9)
        step(nc.vector.reciprocal(ss[:, 2], ss[:, 1]))
        step(nc.vector.tensor_tensor(o, o, ss[:, 2].unsqueeze(2).broadcast_to([N, HH, DK]), ALU.mult))
        dve.wait_ge(states, HH)
        nc.vector.tensor_tensor(flat(o), flat(o), flat(sg), ALU.mult).then_inc(dve_out, 2)

    k.stage(sync=sync, tensor=tensor, scalar=scalar, vector=vector)


def merge_stage(k, d, ident, route):
    nc, ps = k.nc, k.ps
    W3 = TPAD // 3
    assert NT % 3 == 0 and NT % 2 == 1
    oT, mT = k.buf(2, 4, TPAD), k.buf(KD, TPAD)
    wo, wr, br_, g2, iota = k.buf(KD, D), k.buf(KD, NG + NE), k.buf(NG + NE), k.buf(D), k.buf(NE)
    w, m, tmp = k.buf(2, 2, 4, P), k.buf(2, 2, TPAD), k.buf(3, 2, W3)
    lg, sel = k.buf(NG + NE), k.buf(NG, EPG)
    g8, e8, top, idx, idf = k.buf(8), k.buf(8), k.buf(2, 8), k.buf(2, 8), k.buf(2, 8)
    st, hot = k.buf(16), k.buf(NG)
    low = k.low
    bo, ob, oa, t3, gates = k.buf(3, 3, 512), k.buf(3, 512), k.buf(3, 512), k.buf(3, 3, 512), k.buf(NT, 24)
    k.low = low
    x, x2, h2, sq, h2T = k.buf(D), k.buf(D), k.buf(D), k.buf(D), k.buf(KD, P)
    mg = k.buf(2, KD, P)
    sem = lambda what: k.sem(f"m_{what}")
    weights, padded, gates_loaded, gates_ready = (sem(n) for n in ("weights_loaded", "pads_zeroed", "gates_loaded",
                                                                   "gates_ready"))
    rows_loaded, rows_turned = [sem(f"rows_loaded{u}") for u in range(3)], [sem(f"rows_turned{u}") for u in range(3)]
    oa_ready, transposed = sem("oa_ready"), sem("transposed")
    block_loaded = [sem(f"block_loaded{u}") for u in range(2)]
    sigmoid_ready, products_ready, merged = sem("sigmoid_ready"), sem("products_ready"), sem("merged")
    mg_ready, projected, x_loaded, x2_ready = sem("mg_ready"), sem("projected"), sem("x_loaded"), sem("x2_ready")
    squared, root_ready, h2_ready, h2_turned = sem("squared"), sem("root_ready"), sem("h2_ready"), sem("h2_turned")
    h2T_ready, logits_ready, logits_read = sem("h2T_ready"), sem("logits_ready"), sem("logits_read")
    group_max, group_exp, two_max, two_exp = sem("group_max"), sem("group_exp"), sem("two_max"), sem("two_exp")
    x2_stored, h2_stored = sem("x2_stored"), sem("h2_stored")
    sum_step, merge_step, norm_step, route_step = sem("sum_step"), sem("merge_step"), sem("norm_step"), sem("route_step")

    def sync(sp):
        pad = slice(SEQ + NSMP, TPAD)
        for n in range(3):
            sp.dma_start(d["branches"][n, pad, :], d["x_all"][pad, 0:512]).then_inc(padded, 16)
        sp.dma_start(d["ob"][pad, :], d["x_all"][pad, 0:512]).then_inc(padded, 16)
        sp.dma_start(gates, d["zn"].rearrange("(t p) c -> p t c", p=P)[:, :, ZC - 24:ZC]).then_inc(gates_loaded, 16)
        sp.wait_ge(padded, 64)
        with sp.Fori(0, NT // 3) as i:
            for u in range(3):
                sp.wait_ge(rows_turned[u], i + 1)
                t = tile(3 * i + u)
                sp.dma_start(bo[:, u], d["branches"][:, t, :].rearrange("b p n -> p b n")
                             ).then_inc(rows_loaded[u], 16)
                sp.dma_start(ob[:, u], d["ob"][t, :]).then_inc(rows_loaded[u], 16)
        with sp.Fori(0, KD // 2) as i:
            for u in range(2):
                b = 2 * i + u
                sp.wait_ge(merged, 3 * b + 3)
                for n, name in enumerate(("w_pa", "w_pb")):
                    sp.dma_start(w[:, u, n], d[name].rearrange("p (c n) -> p c n", c=4)[:, :, tile(b)]
                                 ).then_inc(block_loaded[u], 16)
                sp.dma_start(m[:, u], d["zT"][2 * HH:24].rearrange("(s b) p n -> b p s n", s=2)[bass.ds(b, 1)]
                             .rearrange("o p s n -> (o p) s n")).then_inc(block_loaded[u], 16)
        sp.sem_inc(x2_stored, 16)
        sp.sem_inc(h2_stored, 16)
        with sp.Fori(0, NT) as t:
            sp.wait_ge(x2_ready, t + 2)
            sp.dma_start(x, d["x_all"][tile(t), :]).then_inc(x_loaded, 16)
            sp.wait_ge(x2_ready, t + 3)
            sp.dma_start(d["x2"][tile(t), :], x2).then_inc(x2_stored, 16)
            sp.wait_ge(h2_ready, t + 1)
            sp.dma_start(d["h2"][tile(t), :], h2).then_inc(h2_stored, 16)
        sp.wait_ge(x2_stored, 16 * NT + 16)
        sp.wait_ge(h2_stored, 16 * NT + 16)

    def gpsimd(pool):
        pool.wait_ge(merged, 3 * KD + 6)

        def stage(t, u):
            pool.wait_ge(projected, 2 * t + 2)
            nc.gpsimd.tensor_copy(mg[:, u], mT[:, :, tile(t)]).then_inc(mg_ready, 1)

        with pool.Fori(0, NT // 2) as i:
            for u in range(2):
                stage(2 * i + u, u)
        stage(NT - 1, 0)

    def scalar(act):
        for to, src in ((wo, d["w_out"].rearrange("p (c n) -> p c n", c=KD)),
                        (wr, d["w_router"].rearrange("p (c n) -> p c n", c=KD)),
                        (br_, d["b_router"].partition_broadcast(P).rearrange("p o n -> p (o n)")),
                        (g2, d["norm2"].partition_broadcast(P).rearrange("p o n -> p (o n)")),
                        (iota, d["iota"][:, 0:NE])):
            act.dma_start(to, src).then_inc(weights, 16)
        for u in range(3):
            act.sem_inc(rows_turned[u], 1)
        act.wait_ge(gates_loaded, 16)
        nc.scalar.activation(gates, gates, ACT.Sigmoid).then_inc(gates_ready, 1)
        with act.Fori(0, NT // 3) as i:
            for u in range(3):
                t = 3 * i + u
                act.wait_ge(transposed, t + 1)
                for n in range(2):
                    ins = nc.scalar.activation(oT[:, n, :, tile(t)], ps[:, 2 * u + n].rearrange("p (c n) -> p c n", c=4),
                                               ACT.Copy)
                ins.then_inc(rows_turned[u], 1)
        with act.Fori(0, KD // 2) as i:
            for u in range(2):
                act.wait_ge(block_loaded[u], 48 * i + 48)
                mf = m[:, u].rearrange("p s n -> p (s n)")
                nc.scalar.activation(mf, mf, ACT.Sigmoid).then_inc(sigmoid_ready, 1)
        act.sem_inc(h2T_ready, 1)

        def norm(t):
            act.wait_ge(x2_ready, t + 3)
            nc.scalar.activation(sq, x2, ACT.Square, accum_out=st[:, 0:1]).then_inc(squared, 1)
            act.wait_ge(squared, t + 1)
            nc.scalar.activation(st[:, 1:2], st[:, 0:1], ACT.Sqrt, scale=1.0 / D, bias=k.eps).then_inc(root_ready, 1)
            act.wait_ge(h2_turned, t + 2)
            for n in range(2):
                ins = nc.scalar.activation(h2T[:, 4 * n:4 * n + 4].rearrange("p c n -> p (c n)"), ps[:, n], ACT.Copy)
            ins.then_inc(h2T_ready, 1)

        def router(t):
            act.wait_ge(group_max, t + 1)
            nc.scalar.activation(hot, lg[:, 0:NG], ACT.Exp, bias=st[:, 3:4], accum_out=st[:, 4:5]
                                 ).then_inc(group_exp, 1)
            act.wait_ge(two_max, t + 1)
            nc.scalar.activation(st[:, 5:6], top[:, 1, 1:2], ACT.Exp, bias=st[:, 6:7]).then_inc(two_exp, 1)

        norm(0)
        with act.Fori(0, NT - 1) as t:
            norm(t + 1)
            router(t)
        router(NT - 1)

    def tensor(pe):
        with pe.Fori(0, NT // 3) as i:
            for u in range(3):
                pe.wait_ge(oa_ready, 3 * i + u + 1)
                for c in range(4):
                    nc.tensor.transpose(ps[:, 2 * u, c * P:(c + 1) * P], oa[:, u, c * P:(c + 1) * P], ident)
                    ins = nc.tensor.transpose(ps[:, 2 * u + 1, c * P:(c + 1) * P], ob[:, u, c * P:(c + 1) * P], ident)
                ins.then_inc(transposed, 1)
        for u in range(3):
            pe.wait_ge(rows_turned[u], NT // 3 + 1)
        with pe.Fori(0, KD // 2) as i:
            for u in range(2):
                pe.wait_ge(block_loaded[u], 48 * i + 48)
                for g in range(3):
                    pe.wait_ge(merged, 3 * (2 * i + u) + g + 4)
                    for n in range(2):
                        for c in range(4):
                            ins = nc.tensor.matmul(ps[:, 2 * g + n, 0:W3], w[:, u, n, c],
                                                   oT[:, n, c, g * W3:(g + 1) * W3], start=(c == 0), stop=(c == 3))
                    ins.then_inc(products_ready, 1)
        pe.wait_ge(weights, 80)
        pe.sem_inc(projected, 4)
        pe.sem_inc(h2_turned, 1)

        def project(t, u, half):
            if half == 0:
                pe.wait_ge(mg_ready, t + 1)
                pe.wait_ge(x2_ready, t + 1)
            for c in range(KD):
                ins = nc.tensor.matmul(ps[:, 4 + 2 * u + half], mg[:, u, c], wo[:, c, half * 512:(half + 1) * 512],
                                       start=(c == 0), stop=(c == KD - 1))
            ins.then_inc(projected, 1)

        def turn(t):
            pe.wait_ge(h2_ready, t + 1)
            pe.wait_ge(h2T_ready, t + 1)
            for c in range(KD):
                ins = nc.tensor.transpose(ps[:, c // 4, c % 4 * P:(c % 4 + 1) * P], h2[:, c * P:(c + 1) * P], ident)
            ins.then_inc(h2_turned, 1)

        def logits(t):
            pe.wait_ge(h2T_ready, t + 2)
            pe.wait_ge(logits_read, t + 1)
            for c in range(KD):
                ins = nc.tensor.matmul(ps[:, 2, 0:NG + NE], h2T[:, c], wr[:, c], start=(c == 0), stop=(c == KD - 1))
            ins.then_inc(logits_ready, 1)

        for half in range(2):
            project(0, 0, half)
        with pe.Fori(0, NT // 2) as i:
            for u in range(2):
                t = 2 * i + u
                project(t + 1, 1 - u, 0)
                turn(t)
                project(t + 1, 1 - u, 1)
                logits(t)
        turn(NT - 1)
        logits(NT - 1)

    def vector(dve):
        dve.wait_ge(gates_ready, 1)
        with dve.Fori(0, NT // 3) as i:
            step = Steps(dve, sum_step, 6, i)
            for u in range(3):
                dve.wait_ge(rows_loaded[u], 32 * i + 32)
                g = gates[:, bass.ds(3 * i + u, 1), :].rearrange("p o (h n) -> p (o h) n", n=3)
                for n in range(3):
                    ins = nc.vector.tensor_tensor(t3[:, u, n].rearrange("p (h n) -> p h n", h=HEADS),
                                                  bo[:, u, n].rearrange("p (h n) -> p h n", h=HEADS),
                                                  g[:, :, n:n + 1].broadcast_to([P, HEADS, HD]), ALU.mult)
                step(ins)
                step(nc.vector.tensor_tensor(t3[:, u, 0], t3[:, u, 0], t3[:, u, 1], ALU.add))
                nc.vector.tensor_tensor(oa[:, u], t3[:, u, 0], t3[:, u, 2], ALU.add).then_inc(oa_ready, 1)
            step.close()
        dve.sem_inc(merged, 6)
        with dve.Fori(0, KD // 2) as i:
            step = Steps(dve, merge_step, 6, i)
            for u in range(2):
                b = 2 * i + u
                dve.wait_ge(sigmoid_ready, b + 1)
                for g in range(3):
                    c = slice(g * W3, (g + 1) * W3)
                    dve.wait_ge(products_ready, 3 * b + g + 1)
                    for n in range(2):
                        ins = nc.vector.tensor_tensor(tmp[:, g, n], ps[:, 2 * g + n, 0:W3], m[:, u, n, c], ALU.mult)
                    step(ins)
                    nc.vector.tensor_tensor(mT[:, bass.ds(b, 1), c], tmp[:, g, 0:1], tmp[:, g, 1:2], ALU.add
                                            ).then_inc(merged, 1)
            step.close()
        dve.wait_ge(weights, 80)
        dve.sem_inc(x2_ready, 2)
        dve.sem_inc(logits_read, 1)

        def norm(t, u):
            step = Steps(dve, norm_step, 1, t)
            dve.wait_ge(x_loaded, 16 * t + 16)
            dve.wait_ge(x2_stored, 16 * t + 16)
            for half in range(2):
                c = slice(512 * half, 512 * half + 512)
                dve.wait_ge(projected, 2 * t + 5 + half)
                ins = nc.vector.tensor_tensor(x2[:, c], ps[:, 4 + 2 * u + half], x[:, c], ALU.add)
            ins.then_inc(x2_ready, 1)
            dve.wait_ge(root_ready, t + 1)
            step(nc.vector.reciprocal(st[:, 2:3], st[:, 1:2]))
            dve.wait_ge(h2_stored, 16 * t + 16)
            dve.wait_ge(h2_turned, t + 1)
            nc.vector.scalar_tensor_tensor(out=h2, in0=x2, scalar=st[:, 2:3], in1=g2, op0=ALU.mult, op1=ALU.mult
                                           ).then_inc(h2_ready, 1)

        def router(t):
            step = Steps(dve, route_step, 15, t)
            dve.wait_ge(logits_ready, t + 1)
            step(nc.vector.memset(g8, -3e38))
            nc.vector.tensor_tensor(lg, ps[:, 2, 0:NG + NE], br_, ALU.add).then_inc(logits_read, 1)
            dve.wait_ge(logits_read, t + 2)
            step(nc.vector.tensor_copy(g8[:, 0:NG], lg[:, 0:NG]))
            k.pin(dve)
            step(nc.vector.max(top[:, 0], g8))
            k.pin(dve)
            step(nc.vector.max_index(idx[:, 0].bitcast(U32), top[:, 0], g8))
            nc.vector.tensor_scalar(st[:, 3:4], top[:, 0, 0:1], -1.0, None, ALU.mult).then_inc(group_max, 1)
            step(nc.vector.tensor_copy(idf[:, 0], idx[:, 0].bitcast(U32)))
            dve.wait_ge(group_exp, t + 1)
            step(nc.vector.tensor_scalar(hot, iota[:, 0:NG], idf[:, 0, 0:1], None, ALU.is_equal))
            step(nc.vector.tensor_tensor(sel, lg[:, NG:].rearrange("p (g e) -> p g e", g=NG),
                                         hot.unsqueeze(2).broadcast_to([P, NG, EPG]), ALU.mult))
            step(nc.vector.tensor_reduce(e8, sel.rearrange("p g e -> p e g"), AX.X, ALU.add))
            k.pin(dve)
            step(nc.vector.max(top[:, 1], e8))
            k.pin(dve)
            step(nc.vector.max_index(idx[:, 1].bitcast(U32), top[:, 1], e8))
            nc.vector.tensor_scalar(st[:, 6:7], top[:, 1, 0:1], -1.0, None, ALU.mult).then_inc(two_max, 1)
            step(nc.vector.tensor_copy(idf[:, 1], idx[:, 1].bitcast(U32)))
            dve.wait_ge(two_exp, t + 1)
            step(nc.vector.scalar_tensor_tensor(out=st[:, 7:8], in0=st[:, 5:6], scalar=1.0, in1=st[:, 4:5],
                                                op0=ALU.add, op1=ALU.mult))
            step(nc.vector.reciprocal(st[:, 10:11], st[:, 7:8]))
            step(nc.vector.tensor_tensor(st[:, 11:12], st[:, 10:11], st[:, 5:6], ALU.mult))
            step(nc.vector.scalar_tensor_tensor(out=st[:, 8:10], in0=idf[:, 0, 0:1].broadcast_to([P, 2]),
                                                scalar=float(EPG), in1=idf[:, 1, 0:2], op0=ALU.mult, op1=ALU.add))
            nc.vector.tensor_copy(route[:, bass.ds(t, 1), :], st[:, 8:12].unsqueeze(1))
            step.close()

        norm(0, 0)
        with dve.Fori(0, NT // 2) as i:
            for u in range(2):
                norm(2 * i + u + 1, 1 - u)
                router(2 * i + u)
        router(NT - 1)

    k.stage(sync=sync, tensor=tensor, scalar=scalar, vector=vector, gpsimd=gpsimd)


def dispatch_stage(k, d, route, gather, blocks):
    nc, ps = k.nc, k.ps
    iota, valid, before, ones = k.buf(NE), k.buf(NT), k.buf(P), k.buf(P)
    hot, a, rank, cnt = k.buf(2, NT, NE), k.buf(NT, NE), k.buf(NT, NE), k.buf(NE)
    tmp, r, lim = k.buf(2, NT, NE), k.buf(2, NT), k.buf(EPG)
    more, upto, start, one = k.buf(NE), k.buf(NE), k.buf(NE), k.buf(NE)
    cmp_e, cmp_r, cmp_b = k.buf(NE, 8), k.buf(2, NT, 8), k.buf(NOVER, NE)
    rb, blk, alt, scat = k.buf(2, NT), k.buf(2, NT), k.buf(2, NT), k.buf(2, NT)
    tbl, fill, token = k.buf(NB + 2), k.buf((NB + 1)), k.buf(NT)
    base = k.buf(NT + 1, NE)
    scat_i = k.buf(2, NT)
    consts, step_sem, pe_done, prefix_ready, filled, table = (
        k.sem(f"d_{w}") for w in ("consts_loaded", "step", "pe_done", "hot_ready", "filled", "dest_ready"))
    scattered = k.own_sem("d_scattered")

    def sync(sp):
        for to, src in ((iota, d["iota"][:, 0:NE]), (valid, d["valid"]), (before, d["before"]), (lim, d["limits"]),
                        (tbl, d["block_ids"]), (token, d["token_ids"])):
            sp.dma_start(to if to is not token else to.bitcast(I32), src).then_inc(consts, 16)
        sp.wait_ge(table, 1)
        sp.dma_start(d["source"].rearrange("(p n) o -> p (n o)", p=P), fill.bitcast(I32)).then_inc(filled, 16)

    def gpsimd(pool):
        pool.wait_ge(filled, 16)
        pool.wait_ge(table, 2)
        for t in range(NT):
            parts = P if t < QT else NSMP
            for n in range(2):
                nc.gpsimd.indirect_dma_start(
                    d["source"], bass.IndirectOffsetOnAxis(ap=scat_i[0:parts, n, t:t + 1].bitcast(I32), axis=0),
                    token[0:parts, t:t + 1].bitcast(I32), None).then_inc(scattered, 16)
        pool.wait_ge(scattered, 16 * 2 * NT)

    def tensor(pe):
        pe.wait_ge(prefix_ready, 1)
        flat = a.rearrange("p t e -> p (t e)")
        nc.tensor.matmul(ps[:, 0, 0:NT * NE], before, flat, start=True, stop=True)
        nc.tensor.matmul(ps[:, 1, 0:NT * NE], ones, flat, start=True, stop=True).then_inc(pe_done, 1)

    def vector(dve):
        step = Steps(dve, step_sem)
        step(nc.vector.memset(fill.bitcast(I32), SEQ + NSMP))
        nc.vector.memset(ones, 1.0)
        nc.vector.memset(one, 1.0)
        step(nc.vector.memset(base[:, 0], 0.0))
        nc.vector.memset(r, 0.0).then_inc(table, 1)
        dve.wait_ge(consts, 96)
        shape = [P, NT, NE]
        for n in range(2):
            ins = nc.vector.tensor_tensor(hot[:, n], bc(iota, 1, NT), route[:, :, n:n + 1].broadcast_to(shape),
                                          ALU.is_equal)
        step(ins)
        for n in range(2):
            ins = nc.vector.tensor_tensor(hot[:, n], hot[:, n], valid.unsqueeze(2).broadcast_to(shape), ALU.mult)
        step(ins)
        nc.vector.tensor_tensor(a, hot[:, 0], hot[:, 1], ALU.add).then_inc(prefix_ready, 1)
        dve.wait_ge(pe_done, 1)
        total = ps[:, 1, 0:NT * NE].rearrange("p (t e) -> p t e", t=NT)
        for t in range(NT):
            step(nc.vector.tensor_tensor(base[:, t + 1], base[:, t], total[:, t], ALU.add))
        count = base[:, NT]
        step(nc.vector.tensor_tensor(rank, ps[:, 0, 0:NT * NE].rearrange("p (t e) -> p t e", t=NT), base[:, 0:NT],
                                     ALU.add))
        for n in range(2):
            ins = nc.vector.tensor_tensor(tmp[:, n], hot[:, n], rank, ALU.mult)
        step(ins)
        step(nc.vector.tensor_reduce(r, tmp, AX.X, ALU.add))
        step(nc.vector.tensor_tensor(cmp_e, count.unsqueeze(2).broadcast_to([P, NE, 8]), bc(lim, 1, NE), ALU.is_gt))
        step(nc.vector.tensor_reduce(more, cmp_e, AX.X, ALU.add))
        step(nc.vector.tensor_tensor_scan(upto, one, more, 0.0, ALU.mult, ALU.add))
        step(nc.vector.tensor_tensor(start, upto, more, ALU.subtract))
        step(nc.vector.tensor_tensor(cmp_b, bc(upto, 1, NOVER), iota[:, 0:NOVER].unsqueeze(2)
                                     .broadcast_to([P, NOVER, NE]), ALU.is_le))
        step(nc.vector.tensor_reduce(tbl[:, NE:NB], cmp_b, AX.X, ALU.add))
        step(nc.vector.tensor_scalar(tbl[:, NE:NB], tbl[:, NE:NB], float(NE - 1), None, ALU.min))
        step(nc.vector.tensor_scalar(tbl[:, NB:NB + 1], upto[:, NE - 1:NE], 0.5, NE / 2 + 0.25, ALU.mult, ALU.add))
        step(nc.vector.tensor_copy(blocks.bitcast(I32), tbl))
        for n in range(2):
            ins = nc.vector.tensor_tensor(cmp_r[:, n], r[:, n].unsqueeze(2).broadcast_to([P, NT, 8]), bc(lim, 1, NT),
                                          ALU.is_ge)
        step(ins)
        step(nc.vector.tensor_reduce(rb, cmp_r, AX.X, ALU.add))
        for n in range(2):
            ins = nc.vector.tensor_tensor(tmp[:, n], hot[:, n], bc(start, 1, NT), ALU.mult)
        step(ins)
        step(nc.vector.tensor_reduce(alt, tmp, AX.X, ALU.add))
        step(nc.vector.tensor_tensor(alt, alt, rb, ALU.add))
        step(nc.vector.tensor_scalar(alt, alt, float(NE - 1), None, ALU.add))
        step(nc.vector.tensor_scalar(scat, rb, 0.0, None, ALU.is_gt))
        for n in range(2):
            eid = route[:, :, n:n + 1].rearrange("p t o -> p (t o)")
            ins = nc.vector.tensor_tensor(blk[:, n], alt[:, n], eid, ALU.subtract)
        step(ins)
        step(nc.vector.tensor_tensor(blk, blk, scat, ALU.mult))
        for n in range(2):
            eid = route[:, :, n:n + 1].rearrange("p t o -> p (t o)")
            ins = nc.vector.tensor_tensor(blk[:, n], blk[:, n], eid, ALU.add)
        step(ins)
        step(nc.vector.scalar_tensor_tensor(out=r, in0=rb, scalar=-float(P), in1=r, op0=ALU.mult, op1=ALU.add))
        step(nc.vector.scalar_tensor_tensor(out=alt, in0=blk, scalar=float(P), in1=r, op0=ALU.mult, op1=ALU.add))
        step(nc.vector.scalar_tensor_tensor(out=scat, in0=r, scalar=float(NB + 1), in1=blk, op0=ALU.mult,
                                            op1=ALU.add))
        for n in range(2):
            ins = nc.vector.tensor_tensor(alt[:, n], alt[:, n], valid, ALU.mult)
        step(ins)
        step(nc.vector.tensor_copy(gather.bitcast(I32), alt))
        nc.vector.tensor_copy(scat_i.bitcast(I32), scat).then_inc(table, 1)

    k.stage(sync=sync, tensor=tensor, vector=vector, gpsimd=gpsimd)


def experts_stage(k, d, ident, blocks):
    nc, ps = k.nc, k.ps
    FJ = DE // P
    wg, wu, wd = k.buf(2, KD, DE), k.buf(2, KD, DE), k.buf(2, FJ, D)
    x, xT, y = k.buf(2, D), k.buf(2, KD, P), k.buf(2, D)
    sg, hid = k.buf(2, FJ * P), k.buf(2, FJ, P)
    src, index = k.buf(NB + 1), k.buf(2)
    up_loaded = [k.sem(f"e_up_loaded{u}") for u in (0, 1)]
    down_loaded = [k.sem(f"e_down_loaded{u}") for u in (0, 1)]
    up_used, down_used = k.sem("e_up_used"), k.sem("e_down_used")
    src_loaded, index_ready = k.sem("e_src_loaded"), k.sem("e_index_ready")
    x_loaded = [k.own_sem(f"e_x_loaded{u}") for u in (0, 1)]
    x_turned, act_xT, dve_xT = k.sem("e_x_turned"), k.sem("e_act_xT"), k.sem("e_dve_xT")
    gate_ready, up_ready, sig_ready, hid_ready = (k.sem(f"e_{w}") for w in
                                                  ("gate_ready", "up_ready", "sigmoid_ready", "hid_ready"))
    y_summed, act_y, dve_y = k.sem("e_y_summed"), k.sem("e_act_y"), k.sem("e_dve_y")
    stored = [k.sem(f"e_stored{u}") for u in (0, 1)]
    step_sem = k.sem("e_step")

    def rounds(eng):
        return eng.value_load(blocks[0:1, NB:NB + 1].bitcast(I32), min_val=NE // 2, max_val=NB // 2)

    def sync(sp):
        sp.dma_start(src.bitcast(I32), d["source"].rearrange("(p n) o -> p (n o)", p=P)).then_inc(src_loaded, 16)
        with sp.Fori(0, rounds(sp)) as i:
            for u in range(2):
                e = sp.value_load(blocks[0:1, bass.ds(2 * i + u, 1)].bitcast(I32), min_val=0, max_val=NE - 1)
                sp.wait_ge(up_used, 2 * i + u + 1)
                for to, w in ((wg, "w_gate"), (wu, "w_up")):
                    sp.dma_start(to[:, u], d[w][bass.ds(e, 1)].rearrange("o (p c) n -> (o p) c n", p=P)
                                 ).then_inc(up_loaded[u], 16)
                sp.wait_ge(down_used, 2 * i + u + 1)
                sp.dma_start(wd[:, u], d["w_down"][bass.ds(e, 1)].rearrange("o (p j) n -> (o p) j n", p=P)
                             ).then_inc(down_loaded[u], 16)

    def gpsimd(pool):
        pool.wait_ge(src_loaded, 16)

        def fetch(u, column, n):
            nc.gpsimd.tensor_copy(index[:, u:u + 1].bitcast(I32), src[:, column].bitcast(I32)
                                  ).then_inc(index_ready, 1)
            pool.wait_ge(index_ready, n + 1)
            k.pin(pool)
            nc.gpsimd.indirect_dma_start(
                x[:, u], None, d["h2"], bass.IndirectOffsetOnAxis(ap=index[:, u:u + 1].bitcast(I32), axis=0)
            ).then_inc(x_loaded[u], 16)

        total = rounds(pool)
        with pool.Fori(0, total) as i:
            for u in range(2):
                pool.wait_ge(x_turned, 2 * i + u + 1)
                fetch(u, bass.ds(2 * i + u, 1), 2 * i + u)
        pool.wait_ge(x_turned, 2 * total + 1)
        k.pin(pool)
        fetch(0, slice(NB, NB + 1), 2 * total)

    def turn(pe, u, i, n):
        pe.wait_ge(x_loaded[u], 16 * i + 16)
        pe.wait_ge(act_xT, n + 1)
        pe.wait_ge(dve_xT, n + 1)
        for c in range(KD):
            ins = nc.tensor.transpose(ps[:, c // 4, c % 4 * P:(c % 4 + 1) * P], x[:, u, c:D:KD], ident)
        ins.then_inc(x_turned, 1)

    def tensor(pe):
        pe.sem_inc(up_used, 2)
        pe.sem_inc(down_used, 2)
        pe.sem_inc(x_turned, 2)
        turn(pe, 0, 0, 0)
        with pe.Fori(0, rounds(pe)) as i:
            for u in range(2):
                n = 2 * i + u
                pe.wait_ge(act_xT, n + 2)
                pe.wait_ge(dve_xT, n + 2)
                pe.wait_ge(up_loaded[u], 32 * i + 32)
                pe.wait_ge(hid_ready, n + 1)
                for w, bank, ready in ((wg, 2, gate_ready), (wu, 3, up_ready)):
                    for j in range(FJ):
                        for c in range(KD):
                            ins = nc.tensor.matmul(ps[:, bank, j * P:(j + 1) * P], w[:, u, c, j:DE:FJ], xT[:, u, c],
                                                   start=(c == 0), stop=(c == KD - 1))
                    ins.then_inc(ready, 1)
                turn(pe, 1 - u, i + u, n + 1)
                pe.drain().then_inc(up_used, 1)
                pe.wait_ge(hid_ready, n + 2)
                pe.wait_ge(down_loaded[u], 16 * i + 16)
                pe.wait_ge(act_y, n + 1)
                pe.wait_ge(dve_y, n + 1)
                for half in range(2):
                    for j in range(FJ):
                        ins = nc.tensor.matmul(ps[:, 4 + half], hid[:, u, j], wd[:, u, j, half * 512:half * 512 + 512],
                                               start=(j == 0), stop=(j == FJ - 1))
                    ins.then_inc(y_summed, 1)
                pe.drain().then_inc(down_used, 1)

    def scalar(act):
        act.sem_inc(act_xT, 1)
        act.sem_inc(act_y, 1)
        for u in range(2):
            act.sem_inc(stored[u], 16)

        def copy_x(u, n):
            act.wait_ge(x_turned, n + 3)
            nc.scalar.activation(xT[:, u, 0:4].rearrange("p c n -> p (c n)"), ps[:, 0], ACT.Copy).then_inc(act_xT, 1)

        copy_x(0, 0)
        total = rounds(act)
        with act.Fori(0, total) as i:
            for u in range(2):
                n = 2 * i + u
                act.wait_ge(gate_ready, n + 1)
                nc.scalar.activation(sg[:, u], ps[:, 2], ACT.Sigmoid).then_inc(sig_ready, 1)
                copy_x(1 - u, n + 1)
                act.wait_ge(stored[u], 16 * i + 16)
                act.wait_ge(y_summed, 2 * n + 1)
                nc.scalar.activation(y[:, u, 0:512], ps[:, 4], ACT.Copy).then_inc(act_y, 1)
                act.wait_ge(act_y, n + 2)
                act.wait_ge(dve_y, n + 2)
                act.dma_start(d["yb"][bass.ds((2 * i + u) * P, P), :], y[:, u]).then_inc(stored[u], 16)
        for u in range(2):
            act.wait_ge(stored[u], 16 * total + 16)
        k.pin(act)

    def vector(dve):
        dve.sem_inc(dve_xT, 1)
        dve.sem_inc(dve_y, 1)
        dve.sem_inc(hid_ready, 1)

        def copy_x(u, n):
            dve.wait_ge(x_turned, n + 3)
            nc.vector.tensor_copy(xT[:, u, 4:8].rearrange("p c n -> p (c n)"), ps[:, 1]).then_inc(dve_xT, 1)

        copy_x(0, 0)
        with dve.Fori(0, rounds(dve)) as i:
            for u in range(2):
                n = 2 * i + u
                dve.wait_ge(sig_ready, n + 1)
                nc.vector.tensor_tensor(sg[:, u], sg[:, u], ps[:, 2], ALU.mult).then_inc(step_sem, 1)
                dve.wait_ge(step_sem, n + 1)
                dve.wait_ge(up_ready, n + 1)
                nc.vector.tensor_tensor(hid[:, u].rearrange("p j n -> p (j n)"), sg[:, u], ps[:, 3], ALU.mult
                                        ).then_inc(hid_ready, 1)
                copy_x(1 - u, n + 1)
                dve.wait_ge(stored[u], 16 * i + 16)
                dve.wait_ge(y_summed, 2 * n + 2)
                nc.vector.tensor_copy(y[:, u, 512:D], ps[:, 5]).then_inc(dve_y, 1)

    k.stage(sync=sync, tensor=tensor, scalar=scalar, vector=vector, gpsimd=gpsimd)


def combine_stage(k, d, route, gather):
    nc = k.nc
    g = k.buf(D)
    x2, y1, y2, gates, st, index = k.buf(2, D), k.buf(2, D), k.buf(2, D), k.buf(2, 2), k.buf(2, 4), k.buf(2, 2)
    gain, x_loaded, rows = k.sem("f_gain_loaded"), [k.sem(f"f_x_loaded{u}") for u in (0, 1)], \
        [k.own_sem(f"f_rows_loaded{u}") for u in (0, 1)]
    index_ready, step_sem, summed, rooted = (k.sem(f"f_{w}") for w in ("index_ready", "step", "summed", "rooted"))
    y_ready, stored = k.sem("f_y_ready"), [k.sem(f"f_stored{u}") for u in (0, 1)]

    def sync(sp):
        sp.dma_start(g, d["final_norm"].partition_broadcast(P).rearrange("p o n -> p (o n)")).then_inc(gain, 16)
        for t in range(NT):
            if t >= 2:
                sp.wait_ge(stored[t % 2], 16 * (t // 2))
            sp.dma_start(x2[:, t % 2], d["x2"][t * P:(t + 1) * P, :]).then_inc(x_loaded[t % 2], 16)

    def gpsimd(pool):
        for t in range(NT):
            if t >= 2:
                pool.wait_ge(stored[t % 2], 16 * (t // 2))
            for n, to in enumerate((y1, y2)):
                nc.gpsimd.indirect_dma_start(
                    to[:, t % 2], None, d["yb"],
                    bass.IndirectOffsetOnAxis(ap=gather[:, n, t:t + 1].bitcast(I32), axis=0)
                ).then_inc(rows[t % 2], 16)

    def scalar(act):
        for t in range(NT):
            u = t % 2
            act.wait_ge(summed, t + 1)
            nc.scalar.activation(y1[:, u], x2[:, u], ACT.Square, accum_out=st[:, u, 0:1]).then_inc(rooted, 1)
            act.wait_ge(rooted, 2 * t + 1)
            nc.scalar.activation(st[:, u, 1:2], st[:, u, 0:1], ACT.Sqrt, scale=1.0 / D, bias=k.eps
                                 ).then_inc(rooted, 1)
            act.wait_ge(y_ready, t + 1)
            act.dma_start(d["y"][t * P:(t + 1) * P, :], y2[:, u]).then_inc(stored[u], 16)
        for u in range(2):
            act.wait_ge(stored[u], 16 * ((NT + 1 - u) // 2))

    def vector(dve):
        step = Steps(dve, step_sem)
        dve.wait_ge(gain, 16)
        for t in range(NT):
            u = t % 2
            dve.wait_ge(x_loaded[u], 16 * (t // 2 + 1))
            dve.wait_ge(rows[u], 32 * (t // 2 + 1))
            step(nc.vector.scalar_tensor_tensor(out=x2[:, u], in0=y1[:, u], scalar=route[:, t, 2:3], in1=x2[:, u],
                                                op0=ALU.mult, op1=ALU.add))
            nc.vector.scalar_tensor_tensor(out=x2[:, u], in0=y2[:, u], scalar=route[:, t, 3:4], in1=x2[:, u],
                                           op0=ALU.mult, op1=ALU.add).then_inc(summed, 1)
            dve.wait_ge(rooted, 2 * t + 2)
            step(nc.vector.reciprocal(st[:, u, 2:3], st[:, u, 1:2]))
            nc.vector.scalar_tensor_tensor(out=y2[:, u], in0=x2[:, u], scalar=st[:, u, 2:3], in1=g,
                                           op0=ALU.mult, op1=ALU.mult).then_inc(y_ready, 1)

    k.stage(sync=sync, scalar=scalar, vector=vector, gpsimd=gpsimd)


def build(nc, d, upto=99):
    with ExitStack() as ctx:
        k = Kernel(nc, ctx)
        ident = k.keep(P)
        route, gather, blocks = k.keep(NT, 4), k.keep(2, NT), k.keep(NB + 2)

        hT_low = k.high
        res = {"qT": k.keep(4, TPAD), "qrT": k.keep(4, TPAD), "ksT": k.keep(TPAD), "kwT": k.keep(WINDOW + TPAD),
               "vs": k.keep(NT, P), "vw": k.keep(NT + WINDOW // P, P), "ckT": k.keep(PCMP + 1), "cv": k.keep(P)}
        res_high = k.high
        hT = k.keep(KD, TPAD)
        stages = [
            lambda: norm_stage(k, d, hT, ident),
            lambda: project_rows_stage(k, "pr1", hT, d["w_rows1"], d["zn"], ZC // ZCH, ZCH),
            lambda: project_rows_stage(k, "pr2", hT, d["w_rows2"], d["zh"], 2, 512),
            lambda: project_columns_stage(k, hT, d["w_cols"], d["zT"], 24),
            lambda: (release(k, res_high), rotary_stage(k, d, res, ident)),
            lambda: prompt_compress_stage(k, d, res, ident),
            lambda: prompt_stage(k, d, res, ident),
            lambda: sample_stage(k, d, res, ident),
            lambda: (release(k, hT_low), hgrn_prompt_stage(k, d, ident)),
            lambda: hgrn_sample_stage(k, d, ident),
            lambda: merge_stage(k, d, ident, route),
            lambda: dispatch_stage(k, d, route, gather, blocks),
            lambda: experts_stage(k, d, ident, blocks),
            lambda: combine_stage(k, d, route, gather),
        ]
        for s in stages[:upto]:
            s()
        block = ctx.enter_context(nc.Block())
        k.emit(block)


def release(k, high):
    k.high = high


SCRATCH = {
    "zn": (TPAD, ZC), "zh": (TPAD, 1024), "zT": (24, P, TPAD), "slc_rows": (TPAD, KVW), "win_rows": (TPAD, KVW),
    "branches": (3, TPAD, 512), "ob": (TPAD, 512), "x2": (TPAD, D), "h2": (TPAD, D),
    "source": (ROWS + P, 1), "yb": (ROWS, D),
}
OUTPUTS = {
    "y": (TPAD, D), "cmp_p": (SEQ, KVW), "cmp_s": (NSMP, KVW), "slc_p": (SEQ, KVW), "slc_s": (NSMP, KVW),
    "win_p": (WINDOW, KVW), "win_s": (NSEQ, WINDOW, KVW), "hgrn_p": (HH, DK, DK), "hgrn_s": (NSEQ, HH, DK, DK),
}


def shape_constants(np):
    f = np.float32
    p = np.arange(P)[:, None]
    pos = np.concatenate([np.arange(SEQ), np.tile(PAST + np.arange(NNEW), NSEQ), np.zeros(TPAD - SEQ - NSMP)]).astype(f)
    inv = f(10000.0) ** (-np.arange(HD // 2, dtype=f) / f(HD // 2))
    ang = pos[:, None] * inv[None, :].astype(f)
    masks = np.zeros((QT, P, MASKW), f)
    for b in range(QT):
        t = b * P + p
        masks[b, :, 0:SEQ] = np.where(np.arange(SEQ)[None] <= t, 0, NEG)
        kp = b * P - WINDOW + np.arange(WINDOW + P)[None]
        masks[b, :, SEQ:SEQ + WINDOW + P] = np.where((kp >= 0) & (kp <= t) & (kp > t - WINDOW), 0, NEG)
        end = np.arange(PCMP)[None] * CSTR + CBLK - 1
        masks[b, :, SEQ + WINDOW + P:-1] = np.where(end <= t, 0, NEG)
        masks[b, :, -1:] = (t >= CBLK - 1)
    r = np.arange(32)
    smask = np.zeros((32, WINDOW + NNEW), f)
    tok = (r % NNEW)[:, None]
    c = np.arange(WINDOW)[None]
    smask[:, :WINDOW] = np.where((c % P) * 4 + c // P > tok, 0, NEG)
    smask[:, WINDOW:] = np.where(np.arange(NNEW)[None] <= tok, 0, NEG)
    n = np.arange(2 * P)[:, None]
    j = np.arange(NBLK)[None]
    cover = ((n * CSTR < (j + 1) * SBLK) & (n * CSTR + CBLK > j * SBLK) & (n < SCMP)).astype(f)
    same = ((r[:, None] % NNEW == r[None] % NNEW) & (r[:, None] // 16 == r[None] // 16)).astype(f)
    forced = np.zeros((32, 2, NBLK), f)
    forced[:, 0] = 1
    for b in (0, NBLK - 2, NBLK - 1):
        forced[:, 0, b], forced[:, 1, b] = 0, 1e9
    small = np.zeros((P, 2 * NBLK), f)
    small[:] = cover.reshape(2, P, NBLK).transpose(1, 0, 2).reshape(P, -1)
    sub = np.ones((P, HH, P), f)
    sub[:, :, 0] = 0
    reset4 = np.ones((P, HH, 32), f)
    reset4[:, :, ::NNEW] = 0
    s, t = np.arange(P)[:, None], np.arange(P)[None]
    blocktri = ((s <= t) & (s // NNEW == t // NNEW)).astype(f)
    seqmask = (np.arange(32)[:, None] // NNEW == np.arange(NSEQ)[None]).astype(f)
    return {
        "ident": np.eye(P, dtype=f), "rope": np.concatenate([np.cos(ang), np.sin(ang)], 1).astype(f),
        "prompt_masks": masks, "smask": smask, "cover": small, "same": same, "forced": forced.reshape(32, -1),
        "reset": sub.reshape(P, -1), "reset4": reset4.reshape(P, -1), "tri": (s <= t).astype(f),
        "before": (s < t).astype(f), "blocktri": blocktri[:32, :32].copy(), "seqmask": seqmask,
        "iota": np.tile(np.arange(NB, dtype=f), (P, 1)), "limits": np.tile(P * np.arange(1, 9, dtype=f), (P, 1)),
        "valid": ((np.arange(NT) * P)[None] + p < SEQ + NSMP).astype(f),
        "block_ids": np.tile(np.arange(NB + 2, dtype=f), (P, 1)),
        "token_ids": ((np.arange(NT) * P)[None] + p).astype(np.int32),
        "lane8": (np.arange(P)[:, None] % 8).astype(f),
    }


def laid_out(inputs, np):
    a = {n: np.asarray(v) for n, v in inputs.items()}
    x = np.concatenate([a["x_prompt"].reshape(SEQ, D), a["x_sample"].reshape(NSMP, D),
                        np.zeros((TPAD - SEQ - NSMP, D), np.float32)])
    w = a["w_in"][0]
    q = w[:, :512].reshape(D, KVH, GRP, HD).transpose(0, 2, 1, 3).reshape(D, 512)
    rows1 = np.concatenate([q, w[:, 512:ZC]], 1)
    rows2 = w[:, 2328:3352]
    cols = np.concatenate([w[:, ZC:2328], w[:, 3352:5400]], 1)

    def chunked(m, width):
        n = m.shape[1] // width
        return np.ascontiguousarray(m.reshape(KD, P, n, width).transpose(2, 1, 0, 3).reshape(n, P, KD * width))

    def by_k(m):
        return np.ascontiguousarray(m.reshape(-1, P, m.shape[1]).transpose(1, 0, 2).reshape(P, -1))

    router = np.concatenate([a["w_router_group"][0], a["w_router_expert"][0].transpose(1, 0, 2).reshape(D, NE)], 1)
    return {
        "x_all": x, "norm1": a["norm1"], "w_rows1": chunked(rows1, ZCH), "w_rows2": chunked(rows2, 512),
        "w_cols": chunked(cols, P), "cache_cmp": np.ascontiguousarray(a["cache_cmp_kv"].reshape(-1, CSTR, 2 * KVH, HD).transpose(0, 2, 1, 3)
                                          ).reshape(-1, CHW),
        "cache_slc": a["cache_slc_kv"].reshape(-1, CHW), "cache_win": a["cache_win_kv"].reshape(NSEQ, WINDOW, KVW),
        "state": a["state_hgrn"][0], "pages": np.repeat(a["page_table"].reshape(NSEQ, 2, 16).transpose(2, 0, 1).reshape(16, -1), 8, axis=0),
        "pe": np.ascontiguousarray(a["cmp_pe"][0].reshape(2, 16, P).transpose(2, 0, 1).reshape(P, 32)),
        "cmp_w1": np.ascontiguousarray(a["cmp_w1"][0].reshape(2, 16, P, P).transpose(2, 0, 1, 3).reshape(P, -1)),
        "cmp_b1": np.ascontiguousarray(a["cmp_b1"][0].T),
        "cmp_w2": np.ascontiguousarray(a["cmp_w2"][0].transpose(1, 0, 2).reshape(P, P)),
        "cmp_b2k": np.concatenate([a["cmp_b2"][0, 0]] * 2).reshape(P, 1),
        "cmp_b2v": np.concatenate([a["cmp_b2"][0, 1]] * 2).reshape(1, P),
        "lb_logits": np.ascontiguousarray(a["hgrn_lb_logits"].reshape(2, HH, DK).transpose(2, 0, 1).reshape(DK, -1)),
        "gnorm": a["hgrn_gnorm"], "w_pa": by_k(a["w_proj_a"][0]), "w_pb": by_k(a["w_proj_b"][0]),
        "w_out": by_k(a["w_out"][0]), "norm2": a["norm2"], "w_router": by_k(router),
        "b_router": np.concatenate([a["b_router_group"].reshape(1, NG), a["b_router_expert"].reshape(1, NE)], 1),
        "w_gate": a["w_exp_gate"][0], "w_up": a["w_exp_up"][0], "w_down": a["w_exp_down"][0],
        "final_norm": a["final_norm"].reshape(1, D),
    }


def kernel(**inputs):
    import numpy as np
    import concourse.bacc as bacc
    from concourse import mybir
    from concourse.bass_utils import run_bass_kernel_spmd

    nc = bacc.Bacc("TRN2", target_bir_lowering=False, num_devices=1)
    arrays = {n: np.ascontiguousarray(v) for n, v in {**laid_out(inputs, np), **shape_constants(np)}.items()}
    d = {n: nc.dram_tensor(f"in_{n}", v.shape, mybir.dt.from_np(v.dtype), kind="ExternalInput").ap()
         for n, v in arrays.items()}
    for n, shape in SCRATCH.items():
        dt = mybir.dt.int32 if n == "source" else mybir.dt.float32
        d[n] = nc.dram_tensor(f"scratch_{n}", shape, dt, kind="Internal").ap()
    for n, shape in OUTPUTS.items():
        d[n] = nc.dram_tensor(f"out_{n}", shape, mybir.dt.float32, kind="ExternalOutput").ap()
    build(nc, d)
    r = run_bass_kernel_spmd(nc, [{f"in_{n}": v for n, v in arrays.items()}], core_ids=[0]).results[0]
    o = {n: r[f"out_{n}"] for n in OUTPUTS}
    return (o["y"][:SEQ].reshape(1, SEQ, D), o["y"][SEQ:SEQ + NSMP].reshape(NSEQ, NNEW, D),
            o["cmp_p"].reshape(1, 1, SEQ, 2, KVH, HD), o["cmp_s"].reshape(1, NSEQ, NNEW, 2, KVH, HD),
            o["slc_p"].reshape(1, 1, SEQ, 2, KVH, HD), o["slc_s"].reshape(1, NSEQ, NNEW, 2, KVH, HD),
            o["win_p"].reshape(1, 1, WINDOW, 2, KVH, HD), o["win_s"].reshape(1, NSEQ, WINDOW, 2, KVH, HD),
            o["hgrn_p"].reshape(1, 1, HH, DK, DK), o["hgrn_s"].reshape(1, NSEQ, HH, DK, DK))
```

```python
import math
from contextlib import ExitStack

import numpy as np

import concourse.bass as bass
from concourse import mybir
from concourse.alu_op_type import AluOpType as ALU

ACT = mybir.ActivationFunctionType
AX = mybir.AxisListType
F32 = mybir.dt.float32
I32 = mybir.dt.int32
U32 = mybir.dt.uint32
F32R = mybir.dt.float32r

P = 128
D = 1024
KD = D // P
SEQ = 1024
NSEQ, NNEW = 8, 4
NSMP = NSEQ * NNEW
QT = SEQ // P
NT = QT + 1
TPAD = NT * P
HD = 64
HEADS, KVH, GRP = 8, 2, 4
KVW = 2 * KVH * HD
PAST, PAGE = 4096, 128
WINDOW = 512
SBLK, NSEL = 64, 16
CBLK, CSTR = 32, 16
PCMP = SEQ // CSTR - 1
SCMP = PAST // CSTR - 1
CHW = CSTR * KVW
NBLK = PAST // SBLK + 1
HH, DK = 4, 128
SUB = 16
ZC = 1304
ZCH = 326
NE, NG, EPG, DE = 32, 4, 8, 512
NOVER = (2 * (SEQ + NSMP)) // (P + 1)
NB = NE + NOVER
ROWS = NB * P
EPS = 1e-6
NEG = -1e9
ATT_SCALE = HD ** -0.5
ATTENDED = 2 * (SEQ + WINDOW + P + 4 * P)
PROJECTED = 2 * KD * TPAD + 3 * 2 * KD * ZCH
MASKW = SEQ + WINDOW + P + PCMP + 1


class Kernel:

    def __init__(self, nc, ctx):
        self.nc, self.ctx = nc, ctx
        self.words = 53120
        self.projected, self.attended = {}, {}
        with ExitStack() as places:
            for name, words in (("ks", SEQ), ("kw", WINDOW + P), ("qr", 4 * P)):
                for part in ("high", "low"):
                    self.attended[name, part] = places.enter_context(
                        nc.sbuf_tensor(f"{name}_{part}", [P, words], F32R))
        with ExitStack() as places:
            for name, words, dtype in (("h_high", KD * TPAD, F32R), ("h_low", KD * TPAD, F32R),
                                       ("w_high", 2 * KD * ZCH, F32R), ("w_low", 2 * KD * ZCH, F32R),
                                       ("w_loaded", 2 * KD * ZCH, F32)):
                self.projected[name] = places.enter_context(nc.sbuf_tensor(name, [P, words], dtype))
        self.arena = ctx.enter_context(nc.sbuf_tensor("arena", [P, self.words], F32))
        self.ps = ctx.enter_context(nc.psum_tensor("ps", [P, 8, 512], F32))
        self.low, self.high = 0, self.words
        self.programs = {e: [] for e in ("sync", "tensor", "scalar", "vector", "gpsimd")}
        self.pinned = ctx.enter_context(nc.semaphore("pinned"))
        self.stages = self.taken = 0
        self.sems, self.used = ([], []), []
        self.eps = self.keep(1)

    def buf(self, *shape, parts=P):
        n = math.prod(shape)
        a = self.arena[0:parts, self.low:self.low + n]
        self.low += n
        assert self.low <= self.high, (self.low, self.high)
        return shaped(a, shape)

    def keep(self, *shape):
        n = math.prod(shape)
        self.high -= n
        assert self.low <= self.high
        return shaped(self.arena[:, self.high:self.high + n], shape)

    def sem(self, name):
        group = self.sems[self.stages % 2]
        if self.taken == len(group):
            group.append(self.ctx.enter_context(self.nc.semaphore(name)))
        self.taken += 1
        return group[self.taken - 1]

    def pin(self, eng):
        eng.sem_inc(self.pinned, 1)

    def own_sem(self, name):
        return self.ctx.enter_context(self.nc.semaphore(name))

    def stage(self, **programs):
        for e in self.programs:
            self.programs[e].append(programs.get(e))
        self.used.append(self.sems[self.stages % 2][:self.taken])
        self.low = self.taken = 0
        self.stages += 1

    def emit(self, block):
        over = self.ctx.enter_context(self.nc.semaphore("stage_over"))
        cleared = self.ctx.enter_context(self.nc.semaphore("stage_cleared"))

        def run(eng, name):
            for n, program in enumerate(self.programs[name]):
                if name == "vector" and n:
                    for s in self.used[n - 1]:
                        ins = eng.sem_clear(s)
                    ins.then_inc(cleared, 1)
                    eng.wait_ge(cleared, n)
                if program:
                    program(eng)
                eng.drain().then_inc(over, 1)
                eng.wait_ge(over, len(self.programs) * (n + 1))
                eng.drain()

        @block.sync
        def _(sp):
            run(sp, "sync")

        @block.tensor
        def _(pe):
            run(pe, "tensor")

        @block.scalar
        def _(act):
            run(act, "scalar")

        @block.vector
        def _(dve):
            run(dve, "vector")

        @block.gpsimd
        def _(pool):
            run(pool, "gpsimd")


def shaped(a, shape):
    if len(shape) == 1:
        return a
    names = "abcde"[:len(shape)]
    return a.rearrange(f"p ({' '.join(names)}) -> p {' '.join(names)}", **dict(zip(names, shape)))


class Steps:

    def __init__(self, eng, sem, per=0, i=0):
        self.eng, self.sem, self.per, self.i, self.n = eng, sem, per, i, 0

    def __call__(self, ins):
        self.n += 1
        ins.then_inc(self.sem, 1)
        self.eng.wait_ge(self.sem, self.i * self.per + self.n)

    def close(self):
        assert not self.per or self.n == self.per, (self.n, self.per)


def tile(i):
    return bass.ds(i * P, P)


def bc(a, axis, n):
    u = a.unsqueeze(axis)
    shape = list(u.shape)
    shape[axis] = n
    return u.broadcast_to(shape)


def split_matmul(nc, out, stationary, moving, start, stop):
    (ah, al), (bh, bl) = stationary, moving
    nc.tensor.matmul(out, ah, bh, start=start, stop=False)
    nc.tensor.matmul(out, ah, bl, start=False, stop=False)
    return nc.tensor.matmul(out, al, bh, start=False, stop=stop)


def norm(k, d, hT, ident):
    nc = k.nc
    x, h, g = k.buf(2, D), k.buf(2, D), k.buf(D)
    ss = k.buf(2, 4)
    eps_ready = k.sem("n_eps_ready")
    gain_loaded, x_loaded = k.sem("n_gain_loaded"), [k.sem(f"n_x_loaded{u}") for u in (0, 1)]
    squared, h_ready = k.sem("n_squared"), k.sem("n_h_ready")
    transposed, copied = k.sem("n_transposed"), k.sem("n_copied")
    step_sem = k.sem("n_step")

    def sync(sp):
        sp.dma_start(ident, d["ident"]).then_inc(gain_loaded, 16)
        sp.dma_start(g, d["norm1"].partition_broadcast(P).rearrange("p o n -> p (o n)")).then_inc(gain_loaded, 16)
        for t in range(NT):
            if t >= 2:
                sp.wait_ge(h_ready, t - 1)
            sp.dma_start(x[:, t % 2], d["x_all"][t * P:(t + 1) * P, :]).then_inc(x_loaded[t % 2], 16)

    def scalar(act):
        for t in range(NT):
            act.wait_ge(x_loaded[t % 2], 16 * (t // 2 + 1))
            if t >= 2:
                act.wait_ge(transposed, t - 1)
            nc.scalar.activation(h[:, t % 2], x[:, t % 2], ACT.Square,
                                 accum_out=ss[:, t % 2, 0:1]).then_inc(squared, 1)
            if t == 0:
                act.wait_ge(eps_ready, 1)
            act.wait_ge(squared, 2 * t + 1)
            nc.scalar.activation(ss[:, t % 2, 1:2], ss[:, t % 2, 0:1], ACT.Sqrt, scale=1.0 / D, bias=k.eps
                                 ).then_inc(squared, 1)

    def vector(dve):
        step = Steps(dve, step_sem)
        nc.vector.memset(k.eps, EPS).then_inc(eps_ready, 1)
        dve.wait_ge(gain_loaded, 32)
        for t in range(NT):
            dve.wait_ge(squared, 2 * t + 2)
            s = ss[:, t % 2]
            step(nc.vector.reciprocal(s[:, 2:3], s[:, 1:2]))
            nc.vector.scalar_tensor_tensor(out=h[:, t % 2], in0=x[:, t % 2], scalar=s[:, 2:3], in1=g,
                                           op0=ALU.mult, op1=ALU.mult).then_inc(h_ready, 1)
            dve.wait_ge(transposed, t + 1)
            places = [[part[:, 4 * b:4 * b + 4, t * P:(t + 1) * P] for part in hT] for b in range(2)]
            banks = [k.ps[:, 2 * (t % 2) + b].rearrange("p (c n) -> p c n", c=4) for b in range(2)]
            for (high, _), bank in zip(places, banks):
                ins = nc.vector.tensor_copy(high, bank)
            step(ins)
            for (high, low), bank in zip(places, banks):
                ins = nc.vector.tensor_tensor(low, bank, high.bitcast(F32), ALU.subtract)
            ins.then_inc(copied, 1)

    def tensor(pe):
        for t in range(NT):
            pe.wait_ge(h_ready, t + 1)
            if t >= 2:
                pe.wait_ge(copied, t - 1)
            for c in range(KD):
                ins = nc.tensor.transpose(k.ps[:, 2 * (t % 2) + c // 4, (c % 4) * P:(c % 4 + 1) * P],
                                          h[:, t % 2, c * P:(c + 1) * P], ident)
            ins.then_inc(transposed, 1)

    def banks_read(eng):
        eng.wait_ge(copied, NT)

    nothing = lambda eng, u: None
    return dict(sync=sync, scalar=scalar, vector=vector, tensor=tensor), Before(banks_read, nothing, nothing, nothing)


class Before:

    def __init__(self, banks_read, weights_split, weights_used, rows_stored):
        self.banks_read, self.weights_split = banks_read, weights_split
        self.weights_used, self.rows_stored = weights_used, rows_stored


def project(k, name, hT, w, out, chunks, width, transposed, wbuf, wsplit, z, before):
    nc = k.nc
    W3 = TPAD // 3
    N = 3 if transposed else NT
    BANKS = 6 if transposed else 3
    assert (2 * N) % BANKS == 0
    columns = W3 if transposed else width
    rounds = chunks // 2
    wbuf = wbuf[:, :, 0:KD * width].rearrange("p u (c n) -> p u c n", c=KD)
    high, low = (part[:, :, 0:KD * width].rearrange("p u (c n) -> p u c n", c=KD) for part in wsplit)
    z = z[:, :, 0:N * columns].rearrange("p u (t n) -> p u t n", t=N)
    s = lambda what: k.sem(f"{name}_{what}")
    w_loaded, stored = [s(f"w_loaded{u}") for u in (0, 1)], [s(f"stored{u}") for u in (0, 1)]
    w_high, w_split, multiplied, copied = s("w_high"), s("w_split"), s("multiplied"), s("copied")

    def bank(u, t):
        return (u * N + t) % BANKS

    def sync(sp):
        with sp.Fori(0, rounds) as i:
            for u in range(2):
                before.weights_split(sp, u)
                sp.wait_ge(w_split, 2 * i + u + 1)
                sp.dma_start(wbuf[:, u], w[bass.ds(2 * i + u, 1)].rearrange("o p (c n) -> (o p) c n", c=KD)
                             ).then_inc(w_loaded[u], 16)

    def vector(dve):
        dve.sem_inc(w_split, 2)
        with dve.Fori(0, rounds) as i:
            for u in range(2):
                n = 2 * i + u
                dve.wait_ge(w_loaded[u], 16 * i + 16)
                before.weights_used(dve, u)
                dve.wait_ge(multiplied, N * (n + 1))
                nc.vector.tensor_copy(high[:, u], wbuf[:, u]).then_inc(w_high, 1)
                dve.wait_ge(w_high, n + 1)
                nc.vector.tensor_tensor(low[:, u], wbuf[:, u], high[:, u].bitcast(F32), ALU.subtract
                                        ).then_inc(w_split, 1)

    def tensor(pe):
        pe.sem_inc(multiplied, 2 * N)
        before.banks_read(pe)
        with pe.Fori(0, rounds) as i:
            for u in range(2):
                n = 2 * i + u
                pe.wait_ge(w_split, n + 3)
                for t in range(N):
                    pe.wait_ge(copied, N * n + t + 1)
                    for c in range(KD):
                        a = [part[:, c, t * P:(t + 1) * P] for part in hT]
                        b = high[:, u, c], low[:, u, c]
                        if transposed:
                            a, b = b, [part[:, c, t * W3:(t + 1) * W3] for part in hT]
                        ins = split_matmul(nc, k.ps[:, bank(u, t), 0:columns], a, b, start=(c == 0),
                                           stop=(c == KD - 1))
                    ins.then_inc(multiplied, 1)

    def scalar(act):
        act.sem_inc(copied, BANKS)
        for u in range(2):
            act.sem_inc(stored[u], 16)
        with act.Fori(0, rounds) as i:
            for u in range(2):
                n = 2 * i + u
                before.rows_stored(act, u)
                act.wait_ge(stored[u], 16 * i + 16)
                for t in range(N):
                    act.wait_ge(multiplied, N * (n + 2) + t + 1)
                    nc.scalar.activation(z[:, u, t], k.ps[:, bank(u, t), 0:columns], ACT.Copy).then_inc(copied, 1)
                act.wait_ge(copied, N * (n + 1) + BANKS)
                chunk = bass.ds(n, 1)
                if transposed:
                    act.dma_start(out[chunk].rearrange("o p (t n) -> (o p) t n", t=N), z[:, u]
                                  ).then_inc(stored[u], 16)
                else:
                    act.dma_start(out.rearrange("(t p) (c n) -> p t c n", p=P, n=width)[:, :, chunk, :]
                                  .rearrange("p t o n -> p t (o n)"), z[:, u]).then_inc(stored[u], 16)

    def banks_read(eng):
        eng.wait_ge(copied, N * chunks + BANKS)

    def weights_split(eng, u):
        eng.wait_ge(w_split, chunks + u + 1)

    def weights_used(eng, u):
        eng.wait_ge(multiplied, N * (chunks + u + 1))

    def rows_stored(eng, u):
        eng.wait_ge(stored[u], 16 * rounds + 16)

    return (dict(sync=sync, tensor=tensor, scalar=scalar, vector=vector),
            Before(banks_read, weights_split, weights_used, rows_stored))


def projections_stage(k, d, ident):
    places = k.projected
    hT = [shaped(places[name][:, :], (KD, TPAD)) for name in ("h_high", "h_low")]
    wsplit = [shaped(places[name][:, :], (2, KD * ZCH)) for name in ("w_high", "w_low")]
    wbuf = shaped(places["w_loaded"][:, :], (2, KD * ZCH))
    k.low = PROJECTED
    z = k.buf(2, NT * ZCH)
    parts = [norm(k, d, hT, ident)]
    for name, w, out, chunks, width, transposed in (("rows1", "w_rows1", "zn", ZC // ZCH, ZCH, False),
                                                    ("rows2", "w_rows2", "zh", 1024 // 256, 256, False),
                                                    ("cols", "w_cols", "zT", 24, P, True)):
        parts.append(project(k, name, hT, d[w], d[out], chunks, width, transposed, wbuf, wsplit, z, parts[-1][1]))

    def run(name):
        def program(eng):
            for programs, _ in parts:
                programs[name](eng)
            if name == "scalar":
                for u in range(2):
                    for _, part in parts[1:]:
                        part.rows_stored(eng, u)
        return program

    k.stage(**{name: run(name) for name in ("sync", "tensor", "scalar", "vector")})


def rotary_stage(k, d, res, ident, rows_out):
    nc = k.nc
    NR = HEADS + 2 * KVH
    z, tab = k.buf(3, ZC), k.buf(3, HD)
    rin, ro, t4 = k.buf(3, NR, HD), k.buf(3, NR, HD), k.buf(3, 4, NR, HD // 2)
    skv, wkv = k.buf(3, KVW), k.buf(3, KVW)
    z_loaded, stored = [k.sem(f"r_z_loaded{u}") for u in range(3)], [k.sem(f"r_stored{u}") for u in range(3)]
    gathered, multiplied, turned = k.sem("r_gathered"), k.sem("r_multiplied"), k.sem("r_turned")
    transposed, act_copied, rows_ready = k.sem("r_transposed"), k.sem("r_act_copied"), k.sem("r_rows_ready")
    zeroed = k.sem("r_zeroed")
    H2 = HD // 2

    def sync(sp):
        sp.dma_start(d["win_s"][:, 0:WINDOW - NNEW, :], d["cache_win"][:, NNEW:WINDOW, :]).then_inc(rows_out, 16)
        with sp.Fori(0, NT // 3) as i:
            for u in range(3):
                sp.wait_ge(stored[u], 32 * i + 32)
                sp.dma_start(z[:, u], d["zn"][tile(3 * i + u), :]).then_inc(z_loaded[u], 16)
                sp.dma_start(tab[:, u], d["rope"][tile(3 * i + u), :]).then_inc(z_loaded[u], 16)
        for u in range(3):
            sp.wait_ge(stored[u], 32 * (NT // 3) + 32)
        for src, new_p, new_s in ((d["zn"][:, 512:512 + KVW], "cmp_p", "cmp_s"), (d["slc_rows"], "slc_p", "slc_s")):
            sp.dma_start(d[new_p], src[0:SEQ, :]).then_inc(rows_out, 16)
            sp.dma_start(d[new_s], src[SEQ:SEQ + NSMP, :]).then_inc(rows_out, 16)
        sp.dma_start(d["win_p"], d["win_rows"][SEQ - WINDOW:SEQ, :]).then_inc(rows_out, 16)
        sp.dma_start(d["win_s"][:, WINDOW - NNEW:WINDOW, :],
                     d["win_rows"][SEQ:SEQ + NSMP, :].rearrange("(b t) n -> b t n", t=NNEW)).then_inc(rows_out, 16)

    def vector(dve):
        nc.vector.memset(res["kwT"][:, 0:WINDOW], 0.0)
        nc.vector.memset(res["vw"][:, 0:WINDOW // P, :], 0.0).then_inc(zeroed, 1)
        with dve.Fori(0, NT // 3) as i:
            for u in range(3):
                t = 3 * i + u
                dve.wait_ge(z_loaded[u], 32 * i + 32)
                nc.vector.tensor_copy(rin[:, u, 0:HEADS].rearrange("p h n -> p (h n)"), z[:, u, 0:512])
                nc.vector.tensor_copy(rin[:, u, 8:10].rearrange("p h n -> p (h n)"), z[:, u, 768:896])
                nc.vector.tensor_copy(rin[:, u, 10:12].rearrange("p h n -> p (h n)"), z[:, u, 1024:1152]
                                      ).then_inc(gathered, 1)
                dve.wait_ge(gathered, t + 1)
                x1, x2 = rin[:, u, :, 0:H2], rin[:, u, :, H2:HD]
                cos, sin = bc(tab[:, u, 0:H2], 1, NR), bc(tab[:, u, H2:HD], 1, NR)
                for n, (a, b) in enumerate(((x1, cos), (x2, sin), (x2, cos), (x1, sin))):
                    ins = nc.vector.tensor_tensor(t4[:, u, n], a, b, ALU.mult)
                ins.then_inc(multiplied, 1)
                dve.wait_ge(multiplied, t + 1)
                nc.vector.tensor_tensor(ro[:, u, :, 0:H2], t4[:, u, 0], t4[:, u, 1], ALU.subtract)
                nc.vector.tensor_tensor(ro[:, u, :, H2:HD], t4[:, u, 2], t4[:, u, 3], ALU.add).then_inc(turned, 1)
                dve.wait_ge(turned, t + 1)
                flat = ro[:, u].rearrange("p h n -> p (h n)")
                nc.vector.tensor_copy(skv[:, u, 0:P], flat[:, 512:640])
                nc.vector.tensor_copy(skv[:, u, P:KVW], z[:, u, 896:1024])
                nc.vector.tensor_copy(wkv[:, u, 0:P], flat[:, 640:768])
                nc.vector.tensor_copy(wkv[:, u, P:KVW], z[:, u, 1152:1280])
                nc.vector.tensor_copy(res["vs"][:, bass.ds(t, 1), :], z[:, u, 896:1024].unsqueeze(1))
                nc.vector.tensor_copy(res["vw"][:, bass.ds(t + WINDOW // P, 1), :], z[:, u, 1152:1280].unsqueeze(1)
                                      ).then_inc(rows_ready, 1)

    def tensor(pe):
        with pe.Fori(0, NT // 3) as i:
            for u in range(3):
                t = 3 * i + u
                flat = ro[:, u].rearrange("p h n -> p (h n)")
                pe.wait_ge(turned, t + 1)
                pe.wait_ge(act_copied, t + 1)
                for j in range(4):
                    nc.tensor.transpose(k.ps[:, 0, j * P:(j + 1) * P], z[:, u, j * P:(j + 1) * P], ident)
                    nc.tensor.transpose(k.ps[:, 1, j * P:(j + 1) * P], flat[:, j * P:(j + 1) * P], ident)
                nc.tensor.transpose(k.ps[:, 2, 0:P], flat[:, 512:640], ident)
                nc.tensor.transpose(k.ps[:, 2, P:2 * P], flat[:, 640:768], ident).then_inc(transposed, 1)

    def scalar(act):
        act.sem_inc(act_copied, 1)
        for u in range(3):
            act.sem_inc(stored[u], 32)
        with act.Fori(0, NT // 3) as i:
            for u in range(3):
                t = 3 * i + u
                act.wait_ge(transposed, t + 1)
                for n, name in enumerate(("qT", "qrT")):
                    nc.scalar.activation(res[name][:, :, tile(t)], k.ps[:, n].rearrange("p (j n) -> p j n", j=4),
                                         ACT.Copy)
                nc.scalar.activation(res["ksT"][:, tile(t)], k.ps[:, 2, 0:P], ACT.Copy)
                nc.scalar.activation(res["kwT"][:, bass.ds(t * P + WINDOW, P)], k.ps[:, 2, P:2 * P], ACT.Copy
                                     ).then_inc(act_copied, 1)
                act.wait_ge(act_copied, t + 2)
                act.wait_ge(rows_ready, t + 1)
                act.dma_start(d["slc_rows"][tile(t), :], skv[:, u]).then_inc(stored[u], 16)
                act.dma_start(d["win_rows"][tile(t), :], wkv[:, u]).then_inc(stored[u], 16)

    k.stage(sync=sync, vector=vector, tensor=tensor, scalar=scalar)


class Compress:

    def __init__(self, k, d, name, halves, chunks, ident, ckT, cv):
        self.k, self.d, self.ident, self.ckT, self.cv = k, d, ident, ckT, cv
        self.halves, self.chunks, self.n = halves, chunks, halves * chunks
        self.w1, self.w2 = k.buf(2, 16, P), k.buf(2, HD)
        self.b1, self.pe = k.buf(2), k.buf(2, 16)
        self.b2k, self.b2v, self.c0 = k.buf(1), k.buf(P), k.buf(2)
        self.xT = k.buf(2, 8, KVH * self.n)
        self.x, self.t, self.hid = (k.buf(KVH * self.n) for _ in range(3))
        s = lambda what: k.sem(f"{name}_{what}")
        self.params_loaded, self.chunks_transposed = s("params_loaded"), s("chunks_transposed")
        self.act_copied, self.dve_copied, self.hid_summed = s("act_copied"), s("dve_copied"), s("hid_summed")
        self.cubed, self.sigmoid_ready, self.hid_ready = s("cubed"), s("sigmoid_ready"), s("hid_ready")
        self.kv_summed, self.ckv_ready, self.step = s("kv_summed"), s("ckv_ready"), s("c_step")
        self.c0_summed, self.c0_ready = s("c0_summed"), s("c0_ready")

    def sync_start(self, sp):
        d = self.d
        for to, src in ((self.w1, d["cmp_w1"].rearrange("p (c j n) -> p c j n", c=2, j=16)),
                        (self.w2, d["cmp_w2"].rearrange("p (c n) -> p c n", c=2)), (self.b1, d["cmp_b1"]),
                        (self.pe, d["pe"].rearrange("p (c j) -> p c j", c=2)), (self.b2k, d["cmp_b2k"]),
                        (self.b2v, d["cmp_b2v"].partition_broadcast(P).rearrange("p o n -> p (o n)"))):
            sp.dma_start(to, src).then_inc(self.params_loaded, 16)

    def pe_start(self, pe):
        nc, ps = self.k.nc, self.k.ps
        pe.wait_ge(self.params_loaded, 96)
        for c in range(2):
            for j in range(16):
                ins = nc.tensor.matmul(ps[:, 7, c:c + 1], self.w1[:, c, j], self.pe[:, c, j:j + 1],
                                       start=(j == 0), stop=(j == 15))
        ins.then_inc(self.c0_summed, 1)
        pe.sem_inc(self.hid_summed, 2)
        pe.sem_inc(self.kv_summed, 1)

    def dve_start(self, dve):
        dve.wait_ge(self.c0_summed, 1)
        self.k.nc.vector.tensor_tensor(self.c0, self.k.ps[:, 7, 0:2], self.b1, ALU.add).then_inc(self.c0_ready, 1)
        dve.wait_ge(self.c0_ready, 1)
        dve.sem_inc(self.dve_copied, 2)
        dve.sem_inc(self.hid_ready, 2)
        dve.sem_inc(self.ckv_ready, 1)
        self.k.nc.vector.memset(self.t, 0.0).then_inc(self.c0_ready, 1)
        dve.wait_ge(self.c0_ready, 2)

    def act_start(self, act):
        act.sem_inc(self.act_copied, 2)

    def turn(self, pe, it, c, source):
        nc, ps, n = self.k.nc, self.k.ps, self.n
        for s2 in range(8):
            m = c * 8 + s2
            pe.wait_ge(self.act_copied if m % 2 == 0 else self.dve_copied, it * 8 + m // 2 + 1)
            for h in range(KVH):
                for half in range(self.halves):
                    o = h * n + half * self.chunks
                    lo = ((c * KVH + h) * CSTR + 2 * s2) * HD
                    ins = nc.tensor.transpose(ps[:, s2 % 4, o:o + self.chunks], source(half)[:, lo:lo + P],
                                              self.ident[0:self.chunks, 0:self.chunks])
            ins.then_inc(self.chunks_transposed, 1)

    def hidden(self, pe, it, c, parts=(0, 1)):
        nc, ps, n = self.k.nc, self.k.ps, self.n
        if 0 in parts:
            pe.wait_ge(self.act_copied, it * 8 + 4 * c + 6)
            pe.wait_ge(self.dve_copied, it * 8 + 4 * c + 6)
            pe.wait_ge(self.hid_ready, it * 2 + c + 1)
        out = ps[:, 4 + c, 0:KVH * n].rearrange("p (h n) -> p h n", h=KVH)[:, :, 0:n - 1]
        for part in parts:
            for s2 in range(8):
                x = self.xT[:, c, s2].rearrange("p (h n) -> p h n", h=KVH)[:, :, part:part + n - 1]
                ins = nc.tensor.matmul(out, self.w1[:, c, part * 8 + s2], x,
                                       start=(part + s2 == 0), stop=(part + s2 == 8))
        if 1 in parts:
            ins.then_inc(self.hid_summed, 1)

    def keys_values(self, pe, it, c):
        nc, ps, n = self.k.nc, self.k.ps, self.n
        pe.wait_ge(self.ckv_ready, it + 1)
        pe.wait_ge(self.hid_ready, it * 2 + c + 3)
        hid = self.hid.rearrange("p (h n) -> p h n", h=KVH)
        for h in range(KVH):
            if c == 0:
                ins = nc.tensor.matmul(ps[h * HD:(h + 1) * HD, 6, 0:n - 1], self.w2[:, 0], hid[:, h, 0:n - 1],
                                       start=True, stop=True)
            else:
                for b in range(self.halves):
                    rows = min(P, n - 1 - b * P)
                    ins = nc.tensor.matmul(ps[0:rows, 7, b * P + h * HD:b * P + (h + 1) * HD],
                                           hid[:, h, b * P:b * P + rows], self.w2[:, 1], start=True, stop=True)
        ins.then_inc(self.kv_summed, 1)

    def copies(self, eng, it, c, pieces):
        nc, ps, w = self.k.nc, self.k.ps, KVH * self.n
        eng.wait_ge(self.hid_summed, it * 2 + c + 1)
        for s2 in pieces:
            eng.wait_ge(self.chunks_transposed, it * 16 + c * 8 + s2 + 1)
            if s2 % 2 == 0:
                nc.scalar.activation(self.xT[:, c, s2], ps[:, s2 % 4, 0:w], ACT.Copy).then_inc(self.act_copied, 1)
            else:
                nc.vector.tensor_copy(self.xT[:, c, s2], ps[:, s2 % 4, 0:w]).then_inc(self.dve_copied, 1)

    def sigmoid(self, act, it, c):
        act.wait_ge(self.cubed, it * 2 + c + 1)
        self.k.nc.scalar.activation(self.t, self.t, ACT.Sigmoid, scale=2.0 * math.sqrt(2.0 / math.pi)
                                    ).then_inc(self.sigmoid_ready, 1)

    def heads(self, a):
        return a.rearrange("p (h n) -> p h n", h=KVH)[:, :, 0:self.n - 1]

    def cube(self, dve, it, c):
        nc, ps, n = self.k.nc, self.k.ps, self.n
        step = Steps(dve, self.step, 6 + self.halves, it)
        step.n = 3 * c
        dve.wait_ge(self.hid_summed, it * 2 + c + 3)
        x, t = self.heads(self.x), self.heads(self.t)
        step(nc.vector.tensor_scalar(x, self.heads(ps[:, 4 + c, 0:KVH * n]), self.c0[:, c:c + 1], None, ALU.add))
        step(nc.vector.tensor_tensor(t, x, x, ALU.mult))
        step(nc.vector.tensor_scalar(t, t, 0.044715, 1.0, ALU.mult, ALU.add))
        nc.vector.tensor_tensor(t, t, x, ALU.mult).then_inc(self.cubed, 1)

    def gelu(self, dve, it, c):
        dve.wait_ge(self.sigmoid_ready, it * 2 + c + 1)
        dve.wait_ge(self.kv_summed, it * 2 + c + 1)
        self.k.nc.vector.tensor_tensor(self.heads(self.hid), self.heads(self.t), self.heads(self.x), ALU.mult
                                       ).then_inc(self.hid_ready, 1)

    def biases(self, dve, it):
        nc, ps, n = self.k.nc, self.k.ps, self.n
        step = Steps(dve, self.step, 6 + self.halves, it)
        step.n = 6
        dve.wait_ge(self.kv_summed, it * 2 + 2 + 1)
        step(nc.vector.tensor_scalar(self.ckT[:, 0:n - 1], ps[:, 6, 0:n - 1], self.b2k, None, ALU.add))
        for b in range(self.halves):
            rows = min(P, n - 1 - b * P)
            ins = nc.vector.tensor_tensor(self.cv[0:rows, b * P:(b + 1) * P], ps[0:rows, 7, b * P:(b + 1) * P],
                                          self.b2v[0:rows], ALU.add)
            if b < self.halves - 1:
                step(ins)
        ins.then_inc(self.ckv_ready, 1)
        step.close()


def prompt_compress_stage(k, d, res, ident):
    n = SEQ // CSTR
    x = k.buf(CHW)
    comp = Compress(k, d, "pcmp", 1, n, ident, res["ckT"], res["cv"])
    rows_loaded = k.sem("pc_rows_loaded")

    def sync(sp):
        comp.sync_start(sp)
        for ch in range(2 * KVH):
            sp.dma_start(x[0:n, ch * CSTR * HD:(ch + 1) * CSTR * HD].rearrange("p (s n) -> p s n", s=CSTR),
                         d["zn"].rearrange("(p s) c -> p s c", s=CSTR)[0:n, :, 512 + ch * HD:512 + (ch + 1) * HD]
                         ).then_inc(rows_loaded, 16)

    def tensor(pe):
        comp.pe_start(pe)
        pe.wait_ge(rows_loaded, 64)
        comp.turn(pe, 0, 0, lambda half: x[0:n])
        comp.hidden(pe, 0, 0)
        comp.turn(pe, 0, 1, lambda half: x[0:n])
        comp.keys_values(pe, 0, 0)
        comp.hidden(pe, 0, 1)
        comp.keys_values(pe, 0, 1)

    def scalar(act):
        comp.act_start(act)
        for c in range(2):
            comp.copies(act, 0, c, range(0, 8, 2))
            comp.sigmoid(act, 0, c)

    def vector(dve):
        comp.dve_start(dve)
        for c in range(2):
            comp.copies(dve, 0, c, range(1, 8, 2))
            comp.cube(dve, 0, c)
            comp.gelu(dve, 0, c)
        comp.biases(dve, 0)

    k.stage(sync=sync, tensor=tensor, scalar=scalar, vector=vector)


def prompt_stage(k, d, res, ident):
    assert SEQ // SBLK == NSEL
    nc, ps = k.nc, k.ps
    WW = WINDOW + P
    NPAIR = QT // 2
    ks, kw, qr = ([k.attended[name, part][:, :] for part in ("high", "low")] for name in ("ks", "kw", "qr"))
    qr = [part.rearrange("p (j n) -> p j n", j=4) for part in qr]
    k.low = ATTENDED
    masks, s = k.buf(MASKW), k.buf(2, MASKW)
    q = k.buf(4, P)
    vw = k.buf(WW // P, P)
    pT, o = k.buf(2, 14, P), k.buf(3, HEADS, HD)
    mx, nb, rs, ri = (k.buf(2, 4) for _ in range(4))
    zero, zeroed, cleared = k.buf(D), k.sem("p_zero_ready"), k.sem("p_rows_cleared")
    masks_loaded, staged = k.sem("p_masks_loaded"), k.sem("p_staged")
    scores_ready, scores_read = k.sem("p_scores_ready"), k.sem("p_scores_read")
    probs_ready = k.sem("p_probs_ready")
    group_turned = [k.sem(f"p_group_turned{g}") for g in range(4)]
    group_copied = [k.sem(f"p_group_copied{g}") for g in range(4)]
    out_summed, out_read, stored = k.sem("p_out_summed"), k.sem("p_out_read"), k.sem("p_stored")
    step_sem, keys_high = k.sem("p_step"), k.sem("p_keys_high")
    PER = 8 * (1 + 2 + 2) + 1

    class Pair:

        def __init__(self, m):
            self.m = m
            self.keys = 2 * (m + 1) * P
            self.first = max(0, WINDOW // P - (2 * m + 1))
            self.window = WW - self.first * P
            lo = self.keys + self.window
            self.cuts = ((0, self.keys, 0), (self.keys, lo, SEQ + self.first * P), (lo, lo + PCMP, SEQ + WW))
            self.blocks = [(0, b, P) for b in range(self.keys // P)] + \
                          [(1, b, P) for b in range(self.window // P)] + [(2, 0, PCMP)]
            self.groups = -(-len(self.blocks) // 4)

    pairs = [Pair(m) for m in range(NPAIR)]
    copies_before = [[sum(16 for p in pairs[:m] if p.groups > g) for g in range(4)] for m in range(NPAIR)]

    def gpsimd(pool):
        nc.gpsimd.memset(zero, 0.0).then_inc(zeroed, 1)

    def sync(sp):
        sp.wait_ge(zeroed, 1)
        with sp.Fori(NE, NB) as b:
            sp.dma_start(d["yb"][tile(b), :], zero).then_inc(cleared, 16)
        with sp.Fori(0, QT) as i:
            sp.wait_ge(stored, 16 * i + 16)
            sp.dma_start(masks, d["prompt_masks"][bass.ds(i, 1)].rearrange("o p n -> (o p) n")
                         ).then_inc(masks_loaded, 16)
        sp.wait_ge(cleared, 16 * NOVER)

    def tensor(pe):
        pe.sem_inc(out_read, 1)
        for pair in pairs:
            with pe.Fori(0, 2) as u:
                tensor_tile(pe, pair, 2 * pair.m + u, 16 * pair.m + 8 * u, u)

    def tensor_tile(pe, pair, i, done, u):
        def scores(h):
            j, r = h % 4, slice(h // 4 * HD, (h // 4 + 1) * HD)
            if h:
                pe.wait_ge(scores_read, done + h)
            for c in range(0, pair.keys, 512):
                n = min(512, pair.keys - c)
                split_matmul(nc, ps[:, c // 512, 0:n], [part[r, j] for part in qr], [part[r, c:c + n] for part in ks],
                             start=True, stop=True)
            for c in range(0, pair.window, 512):
                n = min(512, pair.window - c)
                w = pair.first * P + c
                split_matmul(nc, ps[:, 2 + c // 512, 0:n], [part[r, j] for part in qr],
                             [part[r, w:w + n] for part in kw], start=True, stop=True)
            nc.tensor.matmul(ps[:, 3, P:P + PCMP], q[r, j], res["ckT"][r, 0:PCMP], start=True, stop=True
                             ).then_inc(scores_ready, 1)

        pe.wait_ge(staged, 4 * i + 4)
        scores(0)
        before = copies_before[pair.m]
        for h in range(HEADS):
            if h + 1 < HEADS:
                scores(h + 1)
            kv = h // 4 * HD
            pe.wait_ge(probs_ready, done + h + 1)
            for g in range(pair.groups):
                if g == 3:
                    pe.wait_ge(group_copied[0], before[0] + 8 * u + h + 2)
                else:
                    pe.wait_ge(group_copied[g], before[g] + 8 * u + h + 1)
                if g == 0 and pair.groups == 4:
                    pe.wait_ge(group_copied[3], before[3] + 8 * u + h + 1)
                if pair.blocks[4 * g][2] < P:
                    k.pin(pe)
                for m, (br, b, n) in enumerate(pair.blocks[4 * g:4 * g + 4]):
                    col = pair.cuts[br][0] + b * P
                    ins = nc.tensor.transpose(ps[0:n, 4 + g % 3, m * P:(m + 1) * P], s[:, h % 2, col:col + n],
                                              ident)
                ins.then_inc(group_turned[g], 1)
            pe.wait_ge(out_read, done + h + 1)
            for m, (br, b, n) in enumerate(pair.blocks):
                if m % 4 == 0:
                    pe.wait_ge(group_copied[m // 4], before[m // 4] + 8 * u + h + 2)
                v = res["vs"][:, b] if br == 0 else vw[:, pair.first + b] if br == 1 else res["cv"]
                lo, hi, _ = pair.cuts[br]
                ins = nc.tensor.matmul(ps[:, 7, br * HD:(br + 1) * HD], pT[0:n, h % 2, m], v[0:n, kv:kv + HD],
                                       start=(b == 0), stop=((b + 1) * P >= hi - lo))
            ins.then_inc(out_summed, 1)

    def scalar(act):
        for g in range(4):
            act.sem_inc(group_copied[g], 1)
        act.sem_inc(stored, 16)
        for pair in pairs:
            with act.Fori(0, 2) as u:
                scalar_tile(act, pair, 2 * pair.m + u, 16 * pair.m + 8 * u, u)
        act.wait_ge(stored, 16 * QT + 16)

    def scalar_tile(act, pair, i, done, u):
        before = copies_before[pair.m]
        for h in range(HEADS):
            act.wait_ge(scores_read, done + h + 1)
            for br, (lo, hi, _) in enumerate(pair.cuts):
                ins = nc.scalar.activation(s[:, h % 2, lo:hi], s[:, h % 2, lo:hi], ACT.Exp, scale=ATT_SCALE,
                                           bias=nb[:, h % 2, br:br + 1], accum_out=rs[:, h % 2, br:br + 1])
            ins.then_inc(probs_ready, 1)
            for g in range(pair.groups):
                act.wait_ge(group_turned[g], before[g] + 8 * u + h + 1)
                blocks = pair.blocks[4 * g:4 * g + 4]
                full = sum(n == P for _, _, n in blocks)
                bank = ps[:, 4 + g % 3]
                if full:
                    ins = nc.scalar.activation(pT[:, h % 2, 4 * g:4 * g + full].rearrange("p b n -> p (b n)"),
                                               bank[:, 0:full * P], ACT.Copy)
                if full < len(blocks):
                    ins = nc.scalar.activation(pT[0:PCMP, h % 2, 4 * g + full],
                                               bank[0:PCMP, full * P:(full + 1) * P], ACT.Copy)
                ins.then_inc(group_copied[g], 1)
        act.wait_ge(out_read, done + 8 + 1)
        act.dma_start(d["branches"][:, tile(i), :].rearrange("b p n -> p b n"),
                      o.rearrange("p b h n -> p b (h n)")).then_inc(stored, 16)

    def vector(dve):
        nc.vector.tensor_copy(ks[0], res["ksT"][:, 0:SEQ]).then_inc(keys_high, 1)
        dve.wait_ge(keys_high, 1)
        nc.vector.tensor_tensor(ks[1], res["ksT"][:, 0:SEQ], ks[0].bitcast(F32), ALU.subtract)
        for pair in pairs:
            with dve.Fori(0, 2) as u:
                vector_tile(dve, pair, 2 * pair.m + u, 16 * pair.m + 8 * u)

    def vector_tile(dve, pair, i, done):
        step = Steps(dve, step_sem, PER, i)
        dve.wait_ge(stored, 16 * i + 16)
        nc.vector.tensor_copy(q, res["qT"][:, :, tile(i)]).then_inc(staged, 1)
        nc.vector.tensor_copy(qr[0], res["qrT"][:, :, tile(i)])
        step(nc.vector.tensor_copy(kw[0], res["kwT"][:, bass.ds(i * P, WW)]))
        nc.vector.tensor_tensor(qr[1], res["qrT"][:, :, tile(i)], qr[0].bitcast(F32), ALU.subtract
                                ).then_inc(staged, 1)
        nc.vector.tensor_tensor(kw[1], res["kwT"][:, bass.ds(i * P, WW)], kw[0].bitcast(F32), ALU.subtract
                                ).then_inc(staged, 1)
        nc.vector.tensor_copy(vw, res["vw"][:, bass.ds(i, WW // P), :]).then_inc(staged, 1)
        dve.wait_ge(masks_loaded, 16 * i + 16)

        def maxima(h):
            w = h % 2
            dve.wait_ge(scores_ready, done + h + 1)
            k.pin(dve)
            for br, (lo, hi, at) in enumerate(pair.cuts):
                banks = (ps[:, 0:2], ps[:, 2:4], ps[:, 3:4, P:P + PCMP])[br].rearrange("p b n -> p (b n)")
                ins = nc.vector.tensor_tensor_reduce(s[:, w, lo:hi], banks[:, 0:hi - lo], masks[:, at:at + hi - lo],
                                                     1.0, -3e38, ALU.add, ALU.max, mx[:, w, br:br + 1])
            step(ins)
            nc.vector.tensor_scalar(nb[:, w, 0:3], mx[:, w, 0:3], -ATT_SCALE, None, ALU.mult
                                    ).then_inc(scores_read, 1)

        def outputs(h):
            w = h % 2
            dve.wait_ge(out_summed, done + h + 1)
            step(nc.vector.tensor_scalar(ri[:, w, 0:3], rs[:, w, 0:3], 1e-30, None, ALU.max))
            step(nc.vector.reciprocal(ri[:, w, 0:3], ri[:, w, 0:3]))
            step(nc.vector.tensor_tensor(ri[:, w, 2:3], ri[:, w, 2:3], masks[:, MASKW - 1:MASKW], ALU.mult))
            for br, ob in enumerate((1, 2, 0)):
                ins = nc.vector.tensor_scalar(o[:, ob, h], ps[:, 7, br * HD:(br + 1) * HD], ri[:, w, br:br + 1],
                                              None, ALU.mult)
                if br == 1:
                    step(ins)
            ins.then_inc(out_read, 1)

        maxima(0)
        for h in range(HEADS):
            if h + 1 < HEADS:
                maxima(h + 1)
            outputs(h)
        step.close()

    k.stage(sync=sync, tensor=tensor, scalar=scalar, vector=vector, gpsimd=gpsimd)


def sample_stage(k, d, res, ident):
    nc, ps = k.nc, k.ps
    R = KVH * GRP * NNEW
    NTILE = 2 * CSTR
    xc, xs = k.buf(2, CHW), k.buf(2, CHW)
    xw = k.buf(4, KVW)
    comp_n = 2 * P
    ckT, cv = k.buf(comp_n), k.buf(2 * P)
    comp = Compress(k, d, "scmp", 2, P, ident, ckT, cv)
    kT = comp.xT[:, 0].rearrange("p a b -> p (a b)")
    s = comp.xT[0:R, 1].rearrange("p a b -> p (a b)")
    sn, sw = k.buf(NNEW + 4)[0:R], k.buf(WINDOW + NNEW)[0:R]
    pT = k.buf(NTILE + 1, R)
    wT, pwT = k.buf(WINDOW), k.buf(5, R)
    q, qr = k.buf(R), k.buf(R)
    knew, vnew, wnew = k.buf(2, NNEW), k.buf(P)[0:NNEW], k.buf(P)[0:NNEW]
    pages, lane, chunk_f, chunk = k.buf(NSEQ * 2), k.buf(1), k.buf(NSEQ * 2), k.buf(NSEQ * 2)
    index = k.buf(4)
    p, pcT = k.buf(comp_n)[0:R], k.buf(2, R)
    cover, same, forced, smask = k.buf(2, NBLK), k.buf(R)[0:R], k.buf(2, NBLK)[0:R], k.buf(WINDOW + NNEW)[0:R]
    imp, score, top = k.buf(NBLK)[0:R], k.buf(3, NBLK)[0:R], k.buf(2, 8)[0:R]
    st, mx = k.buf(17)[0:R], k.buf(NBLK)[0:R]
    o = k.buf(3, P)[0:R]
    NKEYS = 9

    sem = lambda what: k.sem(f"s_{what}")
    consts_loaded, chunk_ready = sem("consts_loaded"), sem("chunk_ready")
    xc_loaded, xs_loaded = k.own_sem("s_xc_loaded"), k.own_sem("s_xs_loaded")
    small_loaded, stored, q_ready, dve_step = sem("small_loaded"), sem("stored"), sem("q_ready"), sem("step")
    keys_turned, keys_copied = sem("keys_turned"), sem("keys_copied")
    scores_ready, scores_copied = sem("scores_ready"), sem("scores_copied")
    cmp_scores_ready, cmp_max, cmp_exp = sem("cmp_scores_ready"), sem("cmp_max"), sem("cmp_exp")
    cmp_probs_ready, cmp_turned, pcT_ready = sem("cmp_probs_ready"), sem("cmp_turned"), sem("pcT_ready")
    cmp_out_summed, imp_ready, cmp_out_read = sem("cmp_out_summed"), sem("imp_ready"), sem("cmp_out_read")
    block_scores_ready, block_scores_read = sem("block_scores_ready"), sem("block_scores_read")
    win_max, win_probs_ready = sem("win_max"), sem("win_probs_ready")
    sel_max, sel_masked, sel_probs_ready = sem("sel_max"), sem("sel_masked"), sem("sel_probs_ready")
    probs_turned, act_pT, dve_pT = sem("probs_turned"), sem("act_pT"), sem("dve_pT")
    out_summed, out_ready = sem("out_summed"), sem("out_ready")

    def sync(sp):
        comp.sync_start(sp)
        for to, src in ((cover, d["cover"].rearrange("p (b n) -> p b n", b=2)), (same, d["same"]),
                        (forced, d["forced"].rearrange("p (b n) -> p b n", b=2)), (smask, d["smask"]),
                        (lane, d["lane8"])):
            sp.dma_start(to, src).then_inc(consts_loaded, 16)
        sp.dma_start(pages.bitcast(I32), d["pages"]).then_inc(consts_loaded, 16)
        sp.sem_inc(stored, 96)

        def small(b):
            sp.dma_start(xw, d["cache_win"][bass.ds(b, 1)].rearrange("o (p s) c -> (o p) s c", s=4)
                         ).then_inc(small_loaded, 16)
            sp.dma_start(vnew, d["slc_rows"][bass.ds(b * NNEW + SEQ, NNEW), P:KVW]).then_inc(small_loaded, 16)
            sp.dma_start(wnew, d["win_rows"][bass.ds(b * NNEW + SEQ, NNEW), P:KVW]).then_inc(small_loaded, 16)

        def store(b):
            sp.wait_ge(out_ready, b + 2)
            for br in range(3):
                for h in range(KVH):
                    sp.dma_start(d["branches"][br, bass.ds(b * NNEW + SEQ, NNEW), h * 256:(h + 1) * 256]
                                 .rearrange("t (g n) -> g t n", g=GRP),
                                 o[h * 16:(h + 1) * 16, br, h * HD:(h + 1) * HD]).then_inc(stored, 16)

        small(0)
        with sp.Fori(0, NSEQ - 1) as b:
            sp.wait_ge(out_summed, b + 1)
            small(b + 1)
            store(b)
        store(NSEQ - 1)
        sp.wait_ge(stored, 96 * NSEQ + 96)

    def gpsimd(pool):
        pool.wait_ge(consts_loaded, 16 * 6)
        nc.gpsimd.tensor_copy(chunk_f, pages.bitcast(I32)).then_inc(chunk_ready, 1)
        pool.wait_ge(chunk_ready, 1)
        nc.gpsimd.tensor_scalar(chunk_f, chunk_f, 8.0, lane, ALU.mult, ALU.add).then_inc(chunk_ready, 1)
        pool.wait_ge(chunk_ready, 2)
        nc.gpsimd.tensor_copy(chunk.bitcast(I32), chunk_f).then_inc(chunk_ready, 1)
        pool.wait_ge(chunk_ready, 3)

        def gather(b, n, x, loaded, cache):
            step = Steps(pool, chunk_ready, 2, b)
            step.n = 3 + n
            k.pin(pool)
            step(nc.gpsimd.tensor_copy(index[:, 2 * n:2 * n + 2].bitcast(I32),
                                       chunk.bitcast(I32)[:, bass.ds(2 * b, 2)]))
            k.pin(pool)
            for half in range(2):
                nc.gpsimd.indirect_dma_start(
                    x[:, half], None, d[cache],
                    bass.IndirectOffsetOnAxis(ap=index[:, 2 * n + half:2 * n + half + 1].bitcast(I32), axis=0)
                ).then_inc(loaded, 16)

        gather(0, 0, xc, xc_loaded, "cache_cmp")
        gather(0, 1, xs, xs_loaded, "cache_slc")
        with pool.Fori(0, NSEQ - 1) as b:
            pool.wait_ge(comp.chunks_transposed, 16 * b + 16)
            gather(b + 1, 0, xc, xc_loaded, "cache_cmp")
            pool.wait_ge(out_summed, b + 1)
            gather(b + 1, 1, xs, xs_loaded, "cache_slc")

    def each_sequence(eng, body):
        with eng.Fori(0, NSEQ - 1) as b:
            body(eng, b, True)
        body(eng, NSEQ - 1, False)

    def tensor(pe):
        comp.pe_start(pe)
        pe.wait_ge(consts_loaded, 16 * 6)
        pe.wait_ge(xc_loaded, 32)
        comp.turn(pe, 0, 0, lambda half: xc[:, half])
        comp.hidden(pe, 0, 0)
        each_sequence(pe, tensor_sequence)

    def tensor_sequence(pe, b, more):
        comp.turn(pe, b, 1, lambda half: xc[:, half])
        pe.wait_ge(block_scores_read, b + 1)
        comp.keys_values(pe, b, 0)
        pe.wait_ge(out_ready, b + 1)
        comp.hidden(pe, b, 1)

        pe.wait_ge(xs_loaded, 32 * b + 32)
        pe.wait_ge(q_ready, 6 * b + 6)
        for g in range(NKEYS + 2):
            if g < NKEYS:
                if g >= 4:
                    pe.wait_ge(keys_copied, NKEYS * b + g - 3)
                if g == 8:
                    pe.wait_ge(small_loaded, 48 * b + 48)
                for m in range(4):
                    n = 4 * g + m
                    keys = xw[:, m, 0:P] if g == 8 else xs[:, n // CSTR, n % CSTR * KVW:n % CSTR * KVW + P]
                    ins = nc.tensor.transpose(ps[:, g % 4, m * P:(m + 1) * P], keys, ident)
                ins.then_inc(keys_turned, 1)
            if g >= 2:
                n = g - 2
                pe.wait_ge(keys_copied, NKEYS * b + n + 1)
                if n == 1:
                    pe.wait_ge(comp.cubed, 2 * b + 2)
                if n >= 2:
                    pe.wait_ge(scores_copied, NKEYS * b + n - 1)
                nc.tensor.matmul(ps[0:R, 4 + n % 2], qr, wT if n == 8 else kT[:, n * 512:(n + 1) * 512],
                                 start=True, stop=True).then_inc(scores_ready, 1)

        pe.wait_ge(cmp_out_read, b + 1)
        comp.keys_values(pe, b, 1)
        pe.wait_ge(ckv_now, b + 2)
        pe.wait_ge(scores_copied, NKEYS * b + 8)
        nc.tensor.matmul(ps[0:R, 5, 0:SCMP], q, ckT[:, 0:SCMP], start=True, stop=True)
        nc.tensor.matmul(ps[0:R, 5, P * 2:P * 2 + NNEW], qr, knew[:, 0], start=True, stop=True)
        nc.tensor.matmul(ps[0:R, 5, P * 2 + NNEW:P * 2 + 2 * NNEW], qr, knew[:, 1], start=True, stop=True
                         ).then_inc(cmp_scores_ready, 1)
        if more:
            pe.wait_ge(xc_loaded, 32 * b + 64)
            comp.turn(pe, b + 1, 0, lambda half: xc[:, half])
        pe.wait_ge(cmp_probs_ready, b + 1)
        k.pin(pe)
        nc.tensor.transpose(ps[:, 6, 0:R], p[:, 0:P], ident[0:R, 0:R])
        nc.tensor.transpose(ps[0:SCMP - P, 6, R:2 * R], p[:, P:SCMP], ident[0:R, 0:R]).then_inc(cmp_turned, 1)
        if more:
            pe.wait_ge(scores_copied, NKEYS * b + 9)
            comp.hidden(pe, b + 1, 0, parts=(0,))
        pe.wait_ge(pcT_ready, b + 1)
        for n, rows in enumerate((P, SCMP - P)):
            nc.tensor.matmul(ps[0:R, 7, 0:P], pcT[0:rows, n], cv[0:rows, n * P:(n + 1) * P],
                             start=(n == 0), stop=(n == 1))
        for n, rows in enumerate((P, SCMP - P)):
            ins = nc.tensor.matmul(ps[0:R, 5, 0:NBLK], pcT[0:rows, n], cover[0:rows, n],
                                   start=(n == 0), stop=(n == 1))
        ins.then_inc(cmp_out_summed, 1)
        pe.wait_ge(imp_ready, b + 1)
        k.pin(pe)
        nc.tensor.matmul(ps[0:R, 6, 0:NBLK], same, imp, start=True, stop=True).then_inc(block_scores_ready, 1)
        if more:
            comp.hidden(pe, b + 1, 0, parts=(1,))

        pe.wait_ge(win_probs_ready, b + 1)
        for n in range(NTILE):
            if n % 16 == 0:
                pe.wait_ge(sel_probs_ready, 2 * b + n // 16 + 1)
                k.pin(pe)
            ins = nc.tensor.transpose(ps[:, n // 16, n % 16 * R:(n % 16 + 1) * R], s[:, n * P:(n + 1) * P],
                                      ident[0:R, 0:R])
            if n % 16 == 15:
                ins.then_inc(probs_turned, 1)
        for n in range(4):
            nc.tensor.transpose(ps[:, 2, n * R:(n + 1) * R], sw[:, n * P:(n + 1) * P], ident[0:R, 0:R])
        nc.tensor.transpose(ps[0:NNEW, 2, 4 * R:5 * R], sw[:, WINDOW:], ident[0:R, 0:R])
        nc.tensor.transpose(ps[0:NNEW, 2, 5 * R:6 * R], sn[:, 0:NNEW], ident[0:R, 0:R]).then_inc(probs_turned, 1)
        pe.wait_ge(act_pT, b + 1)
        pe.wait_ge(dve_pT, b + 1)
        for n in range(NTILE):
            nc.tensor.matmul(ps[0:R, 5, 0:P], pT[:, n],
                             xs[:, n // CSTR, n % CSTR * KVW + P:(n % CSTR + 1) * KVW],
                             start=(n == 0), stop=False)
        nc.tensor.matmul(ps[0:R, 5, 0:P], pT[0:NNEW, NTILE], vnew, start=False, stop=True)
        for n in range(4):
            nc.tensor.matmul(ps[0:R, 5, P:2 * P], pwT[:, n], xw[:, n, P:KVW], start=(n == 0), stop=False)
        nc.tensor.matmul(ps[0:R, 5, P:2 * P], pwT[0:NNEW, 4], wnew, start=False, stop=True).then_inc(out_summed, 1)

    def scalar(act):
        comp.act_start(act)
        comp.copies(act, 0, 0, range(0, 8, 2))
        comp.sigmoid(act, 0, 0)
        each_sequence(act, scalar_sequence)

    def scalar_sequence(act, b, more):
        comp.copies(act, b, 1, range(0, 8, 2))
        for g in range(NKEYS + 2):
            if g == 2:
                comp.sigmoid(act, b, 1)
            if g < NKEYS:
                act.wait_ge(keys_turned, NKEYS * b + g + 1)
                nc.scalar.activation(wT if g == 8 else kT[:, g * 512:(g + 1) * 512], ps[:, g % 4], ACT.Copy
                                     ).then_inc(keys_copied, 1)
            if g >= 2:
                n = g - 2
                act.wait_ge(scores_ready, NKEYS * b + n + 1)
                nc.scalar.activation(sw[:, 0:WINDOW] if n == 8 else s[:, n * 512:(n + 1) * 512],
                                     ps[0:R, 4 + n % 2], ACT.Copy).then_inc(scores_copied, 1)
        act.wait_ge(cmp_max, b + 1)
        nc.scalar.activation(p[:, 0:SCMP], p[:, 0:SCMP], ACT.Exp, scale=ATT_SCALE, bias=st[:, 1:2],
                             accum_out=st[:, 2:3]).then_inc(cmp_exp, 1)
        if more:
            comp.copies(act, b + 1, 0, (0,))
        act.wait_ge(win_max, b + 1)
        nc.scalar.activation(sw, sw, ACT.Exp, scale=ATT_SCALE, bias=st[:, 8:9], accum_out=st[:, 9:10]
                             ).then_inc(win_probs_ready, 1)
        if more:
            comp.copies(act, b + 1, 0, (2, 4, 6))
        act.wait_ge(sel_max, b + 1)
        nc.scalar.activation(sn[:, 0:NNEW], sn[:, 0:NNEW], ACT.Exp, scale=ATT_SCALE, bias=st[:, 4:5],
                             accum_out=st[:, 6:7])
        for half in range(2):
            act.wait_ge(sel_masked, 2 * b + half + 1)
            part = s[:, half * 2048:(half + 1) * 2048]
            nc.scalar.activation(part, part, ACT.Exp, scale=ATT_SCALE, bias=st[:, 4:5],
                                 accum_out=st[:, 15 + half:16 + half]).then_inc(sel_probs_ready, 1)
        act.wait_ge(probs_turned, 3 * b + 1)
        nc.scalar.activation(pT[:, 0:16].rearrange("p n r -> p (n r)"), ps[:, 0], ACT.Copy).then_inc(act_pT, 1)
        if more:
            comp.sigmoid(act, b + 1, 0)

    ckv_now = comp.ckv_ready

    def vector(dve):
        comp.dve_start(dve)
        nc.vector.memset(q, 0.0)
        nc.vector.memset(qr, 0.0).then_inc(comp.c0_ready, 1)
        dve.wait_ge(comp.c0_ready, 3)
        dve.wait_ge(consts_loaded, 16 * 6)
        for one_more in (block_scores_read, out_ready, cmp_out_read):
            dve.sem_inc(one_more, 1)
        comp.copies(dve, 0, 0, range(1, 8, 2))
        comp.cube(dve, 0, 0)
        comp.gelu(dve, 0, 0)
        each_sequence(dve, vector_sequence)

    def vector_sequence(dve, b, more):
        step = Steps(dve, dve_step, PER, b)
        for to, src in ((q, res["qT"]), (qr, res["qrT"])):
            for h in range(KVH):
                r = slice(h * HD, (h + 1) * HD)
                nc.vector.tensor_copy(to[r, h * 16:(h + 1) * 16].rearrange("p (g t) -> p g t", g=GRP),
                                      src[r, :, bass.ds(b * NNEW + SEQ, NNEW)]).then_inc(q_ready, 1)
        nc.vector.tensor_copy(knew[:, 0], res["ksT"][:, bass.ds(b * NNEW + SEQ, NNEW)]).then_inc(q_ready, 1)
        nc.vector.tensor_copy(knew[:, 1], res["kwT"][:, bass.ds(b * NNEW + SEQ + WINDOW, NNEW)]).then_inc(q_ready, 1)
        comp.copies(dve, b, 1, range(1, 8, 2))
        comp.cube(dve, b, 1)
        comp.gelu(dve, b, 1)
        comp.biases(dve, b)

        dve.wait_ge(cmp_scores_ready, b + 1)
        nc.vector.tensor_copy(p[:, 0:SCMP], ps[0:R, 5, 0:SCMP])
        step(nc.vector.tensor_reduce(st[:, 0:1], ps[0:R, 5, 0:SCMP], AX.X, ALU.max))
        nc.vector.tensor_scalar(st[:, 1:2], st[:, 0:1], -ATT_SCALE, None, ALU.mult).then_inc(cmp_max, 1)
        nc.vector.tensor_copy(sn[:, 0:NNEW], ps[0:R, 5, P * 2:P * 2 + NNEW])
        step(nc.vector.tensor_copy(sw[:, WINDOW:], ps[0:R, 5, P * 2 + NNEW:P * 2 + 2 * NNEW]))
        dve.wait_ge(scores_copied, NKEYS * b + 9)
        k.pin(dve)
        step(nc.vector.tensor_tensor_reduce(sw, sw, smask, 1.0, -3e38, ALU.add, ALU.max, st[:, 7:8]))
        nc.vector.tensor_scalar(st[:, 8:9], st[:, 7:8], -ATT_SCALE, None, ALU.mult).then_inc(win_max, 1)
        if more:
            comp.copies(dve, b + 1, 0, (1, 3))
        dve.wait_ge(cmp_exp, b + 1)
        step(nc.vector.tensor_scalar(st[:, 2:3], st[:, 2:3], 1e-30, None, ALU.max))
        step(nc.vector.reciprocal(st[:, 2:3], st[:, 2:3]))
        nc.vector.tensor_scalar(p[:, 0:SCMP], p[:, 0:SCMP], st[:, 2:3], None, ALU.mult).then_inc(cmp_probs_ready, 1)
        if more:
            comp.copies(dve, b + 1, 0, (5, 7))
        dve.wait_ge(cmp_turned, b + 1)
        step(nc.vector.tensor_copy(pcT[:, 0], ps[:, 6, 0:R]))
        nc.vector.tensor_copy(pcT[0:SCMP - P, 1], ps[0:SCMP - P, 6, R:2 * R]).then_inc(pcT_ready, 1)
        for half in range(2):
            a = s[:, half * 2048:(half + 1) * 2048].rearrange("p (s a c) -> p a s c", s=CSTR, c=4)
            ins = nc.vector.tensor_reduce(mx[:, half * 32:(half + 1) * 32], a, AX.XY, ALU.max)
        step(ins)
        k.pin(dve)
        step(nc.vector.tensor_tensor_reduce(sn[:, 0:NNEW], sn[:, 0:NNEW], smask[:, WINDOW:], 1.0, -3e38, ALU.add,
                                            ALU.max, mx[:, NBLK - 1:NBLK]))
        dve.wait_ge(cmp_out_summed, b + 1)
        nc.vector.tensor_copy(imp, ps[0:R, 5, 0:NBLK]).then_inc(imp_ready, 1)
        dve.wait_ge(stored, 96 * b + 96)
        nc.vector.tensor_copy(o[:, 0], ps[0:R, 7, 0:P]).then_inc(cmp_out_read, 1)
        dve.wait_ge(block_scores_ready, b + 1)
        nc.vector.tensor_tensor(score[:, 0], ps[0:R, 6, 0:NBLK], forced[:, 0], ALU.mult
                                ).then_inc(block_scores_read, 1)
        dve.wait_ge(block_scores_read, b + 2)
        step(nc.vector.tensor_tensor(score[:, 0], score[:, 0], forced[:, 1], ALU.add))
        for n in range(NSEL // 8):
            k.pin(dve)
            step(nc.vector.max(top[:, n], score[:, n]))
            k.pin(dve)
            step(nc.vector.match_replace(score[:, n + 1], top[:, n], score[:, n], -3e38))
        step(nc.vector.tensor_scalar(score[:, 0], score[:, 2], -3e38, NEG, ALU.not_equal, ALU.mult))
        step(nc.vector.tensor_tensor(mx[:, 0:NBLK - 1], mx[:, 0:NBLK - 1], score[:, 0, 0:NBLK - 1], ALU.add))
        step(nc.vector.tensor_reduce(st[:, 3:4], mx, AX.X, ALU.max))
        nc.vector.tensor_scalar(st[:, 4:5], st[:, 3:4], -ATT_SCALE, None, ALU.mult).then_inc(sel_max, 1)
        for half in range(2):
            a = s[:, half * 2048:(half + 1) * 2048].rearrange("p (s a c) -> p s a c", s=CSTR, c=4)
            block = bc(bc(score[:, 0, half * 32:(half + 1) * 32], 2, 4), 1, CSTR)
            nc.vector.tensor_tensor(a, a, block, ALU.add).then_inc(sel_masked, 1)
        if more:
            comp.cube(dve, b + 1, 0)
        dve.wait_ge(probs_turned, 3 * b + 2)
        nc.vector.tensor_copy(pT[:, 16:32].rearrange("p n r -> p (n r)"), ps[:, 1])
        dve.wait_ge(probs_turned, 3 * b + 3)
        nc.vector.tensor_copy(pT[0:NNEW, 32], ps[0:NNEW, 2, 5 * R:6 * R])
        nc.vector.tensor_copy(pwT[:, 0:4].rearrange("p n r -> p (n r)"), ps[:, 2, 0:4 * R])
        nc.vector.tensor_copy(pwT[0:NNEW, 4], ps[0:NNEW, 2, 4 * R:5 * R]).then_inc(dve_pT, 1)
        if more:
            comp.gelu(dve, b + 1, 0)
        step(nc.vector.tensor_tensor(st[:, 5:6], st[:, 15:16], st[:, 16:17], ALU.add))
        step(nc.vector.tensor_tensor(st[:, 10:11], st[:, 5:6], st[:, 6:7], ALU.add))
        step(nc.vector.tensor_copy(st[:, 11:12], st[:, 9:10]))
        step(nc.vector.tensor_scalar(st[:, 10:12], st[:, 10:12], 1e-30, None, ALU.max))
        step(nc.vector.reciprocal(st[:, 12:14], st[:, 10:12]))
        dve.wait_ge(out_summed, b + 1)
        step(nc.vector.tensor_scalar(o[:, 1], ps[0:R, 5, 0:P], st[:, 12:13], None, ALU.mult))
        nc.vector.tensor_scalar(o[:, 2], ps[0:R, 5, P:2 * P], st[:, 13:14], None, ALU.mult).then_inc(out_ready, 1)
        step.close()

    PER = 22

    k.stage(sync=sync, tensor=tensor, scalar=scalar, vector=vector, gpsimd=gpsimd)




class Lower:

    def __init__(self, k, d, name):
        self.k, self.d = k, d
        self.logits, self.lb, self.lbc = k.buf(2, HH), k.buf(HH), k.buf(HH)
        self.loaded, self.exp, self.diff = (k.sem(f"{name}_lb_{w}") for w in ("loaded", "exp", "step"))

    def sync(self, sp):
        sp.dma_start(self.logits, self.d["lb_logits"].rearrange("p (a h) -> p a h", a=2)).then_inc(self.loaded, 16)

    def scalar(self, act):
        act.wait_ge(self.diff, 1)
        self.k.nc.scalar.activation(self.lb, self.lb, ACT.Sigmoid).then_inc(self.exp, 1)

    def vector(self, dve):
        nc = self.k.nc
        dve.wait_ge(self.loaded, 16)
        nc.vector.tensor_tensor(self.lb, self.logits[:, 0], self.logits[:, 1], ALU.subtract).then_inc(self.diff, 1)
        dve.wait_ge(self.exp, 1)
        nc.vector.tensor_scalar(self.lbc, self.lb, -1.0, 1.0, ALU.mult, ALU.add).then_inc(self.diff, 1)
        dve.wait_ge(self.diff, 2)


def hgrn_prompt_stage(k, d, ident):
    nc, ps = k.nc, k.ps
    NS = P // SUB
    W = HH * P
    lower = Lower(k, d, "hp")
    ek, ecum, key, q, qh, v, gate, kd = (k.buf(HH, SEQ) for _ in range(8))
    kh_flat = k.buf(2 * HH * NS * P + P)
    kh = kh_flat[:, 0:2 * HH * NS * P].rearrange("p (u h s n) -> p u h s n", u=2, h=HH, s=NS)
    kl, klT, qe, att, o = (k.buf(2, HH, P) for _ in range(5))
    S, osq, nlbc = k.buf(HH, P), k.buf(HH, P), k.buf(HH)
    R = k.buf(HH, QT, NS + 1, NS)
    reset, tri, gn = k.buf(W), k.buf(P), k.buf(P)
    ss, last = k.buf(2, 3, HH), k.buf(2, HH)
    sem = lambda what: k.sem(f"hp_{what}")
    f_loaded, q_loaded, v_loaded, gate_loaded, consts = (sem(n) for n in ("f_loaded", "q_loaded", "v_loaded",
                                                                          "gate_loaded", "consts_loaded"))
    f_sigmoid, q_sigmoid, gate_sigmoid, gated = sem("f_sigmoid"), sem("q_sigmoid"), sem("gate_sigmoid"), sem("gated")
    key_ready, log_ready, diffs_ready, kd_ready = sem("key_ready"), sem("log_ready"), sem("diffs_ready"), sem("kd_ready")
    exps_ready, step_sem, tile_step, state_out = sem("exps_ready"), sem("step"), sem("tile_step"), sem("state_stored")
    kh_ready, kl_ready, att_ready, att_masked = sem("kh_ready"), sem("kl_ready"), sem("att_ready"), sem("att_masked")
    kl_turned, klT_ready, out_summed, state_summed = (sem(n) for n in ("kl_turned", "klT_ready", "out_summed",
                                                                       "state_summed"))
    S_ready, squared, root_ready, o_ready = sem("S_ready"), sem("squared"), sem("root_ready"), sem("o_ready")
    stored = [sem(f"stored{u}") for u in range(2)]
    flat = lambda a: a.rearrange("p h n -> p (h n)")
    rows = lambda c: d["zh"][0:SEQ, c * W:(c + 1) * W].rearrange("(t p) n -> p t n", p=P)
    by_tile = lambda a: flat(a).rearrange("p (t n) -> p t n", t=QT)

    def each_tile(eng, body):
        with eng.Fori(0, QT // 2 - 1) as i:
            for u in range(2):
                body(eng, 2 * i + u, u, i, True)
        for u in range(2):
            body(eng, QT - 2 + u, u, QT // 2 - 1, u == 0)

    def sync(sp):
        lower.sync(sp)
        sp.dma_start(ek, d["zT"][HH:2 * HH, :, 0:SEQ].rearrange("h p n -> p h n")).then_inc(f_loaded, 16)
        sp.dma_start(q, d["zT"][0:HH, :, 0:SEQ].rearrange("h p n -> p h n")).then_inc(q_loaded, 16)
        for to, src in ((reset, d["reset"]), (tri, d["tri"]),
                        (gn, d["gnorm"].partition_broadcast(P).rearrange("p o n -> p (o n)"))):
            sp.dma_start(to, src).then_inc(consts, 16)
        sp.dma_start(by_tile(gate), rows(1)).then_inc(gate_loaded, 16)
        sp.dma_start(by_tile(v), rows(0)).then_inc(v_loaded, 16)

        def store(eng, i, u, r, more):
            sp.wait_ge(o_ready, i + 3)
            sp.dma_start(d["ob"][tile(i), :], flat(o[:, u])).then_inc(stored[u], 16)

        for u in range(2):
            sp.sem_inc(stored[u], 16)
        each_tile(sp, store)
        sp.wait_ge(S_ready, QT + 1)
        sp.dma_start(d["hgrn_p"].rearrange("h p n -> p h n"), S).then_inc(state_out, 16)
        sp.wait_ge(state_out, 16)
        for u in range(2):
            sp.wait_ge(stored[u], 16 * (QT // 2) + 16)

    def gpsimd(pool):
        pool.wait_ge(consts, 48)
        pool.wait_ge(gate_sigmoid, 1)
        nc.gpsimd.tensor_tensor(flat(gate), flat(gate), flat(kd), ALU.mult).then_inc(gated, 1)
        pool.wait_ge(gated, 1)
        g = flat(gate).rearrange("p (t n) -> p t n", n=P)
        nc.gpsimd.tensor_tensor(g, g, bc(gn, 1, HH * QT), ALU.mult).then_inc(gated, 1)

    def scalar(act):
        lower.scalar(act)
        act.wait_ge(f_loaded, 16)
        for h in range(HH):
            nc.scalar.activation(ek[:, h], ek[:, h], ACT.Sigmoid).then_inc(f_sigmoid, 1)
        act.wait_ge(q_loaded, 16)
        nc.scalar.activation(flat(qh), flat(q), ACT.Sigmoid).then_inc(q_sigmoid, 1)
        act.wait_ge(gate_loaded, 16)
        nc.scalar.activation(flat(kd), flat(gate), ACT.Sigmoid).then_inc(gate_sigmoid, 1)
        for h in range(HH):
            act.wait_ge(key_ready, h + 1)
            nc.scalar.activation(ek[:, h], ek[:, h], ACT.Ln, scale=lower.lbc[:, h:h + 1], bias=lower.lb[:, h:h + 1]
                                 ).then_inc(log_ready, 1)
        act.wait_ge(gated, 1)
        for h in range(HH):
            act.wait_ge(diffs_ready, h + 1)
            nc.scalar.activation(kd[:, h], qh[:, h], ACT.Exp, scale=-1.0).then_inc(kd_ready, 1)
            nc.scalar.activation(ek[:, h], ek[:, h], ACT.Exp)
            nc.scalar.activation(ecum[:, h], ecum[:, h], ACT.Exp)
            r = R[:, h].rearrange("p t a b -> p (t a b)")
            nc.scalar.activation(r, r, ACT.Exp)
            act.wait_ge(kd_ready, h + 1)
            nc.scalar.activation(qh[:, h], qh[:, h], ACT.Exp).then_inc(exps_ready, 1)

        def turned_keys(i, u):
            act.wait_ge(kl_turned, i + 1)
            nc.scalar.activation(flat(klT[:, u]), ps[:, 2 + u], ACT.Copy).then_inc(klT_ready, 1)

        def root(eng, i, u, r, more):
            act.wait_ge(out_summed, i + 1)
            for h in range(HH):
                ins = nc.scalar.activation(osq[:, h], ps[:, 4 + u, h * P:(h + 1) * P], ACT.Square,
                                           accum_out=ss[:, u, 0, h:h + 1])
            ins.then_inc(squared, 1)
            act.wait_ge(squared, i + 1)
            nc.scalar.activation(ss[:, u, 1], ss[:, u, 0], ACT.Sqrt, scale=1.0 / DK, bias=k.eps
                                 ).then_inc(root_ready, 1)
            if more:
                turned_keys(i + 1, 1 - u)

        turned_keys(0, 0)
        each_tile(act, root)

    def tensor(pe):
        pe.wait_ge(v_loaded, 16)

        def inside(i, u):
            for h in range(HH):
                pe.wait_ge(kh_ready, HH * i + h + 1)
                for n in range(NS):
                    ins = nc.tensor.matmul(ps[:, u, h * P + SUB * n:h * P + SUB * (n + 1)], kh[:, u, h, n],
                                           qh[:, h, bass.ds(i * P + SUB * n, SUB)], start=True, stop=True)
            ins.then_inc(att_ready, 1)
            pe.wait_ge(kl_ready, i + 1)
            for h in range(HH):
                ins = nc.tensor.transpose(ps[:, 2 + u, h * P:(h + 1) * P], kl[:, u, h], ident)
            ins.then_inc(kl_turned, 1)

        def outputs(eng, i, u, r, more):
            pe.wait_ge(att_masked, i + 1)
            pe.wait_ge(S_ready, i + 1)
            pe.wait_ge(o_ready, i + 1)
            vt = by_tile(v)[:, bass.ds(i, 1), :].rearrange("p o n -> p (o n)")
            for h in range(HH):
                c = slice(h * P, (h + 1) * P)
                nc.tensor.matmul(ps[:, 4 + u, c], att[:, u, h], vt[:, c], start=True, stop=False)
                ins = nc.tensor.matmul(ps[:, 4 + u, c], qe[:, u, h], S[:, h], start=False, stop=True)
            ins.then_inc(out_summed, 1)
            pe.wait_ge(klT_ready, i + 1)
            for h in range(HH):
                c = slice(h * P, (h + 1) * P)
                ins = nc.tensor.matmul(ps[:, 6 + u, c], klT[:, u, h], vt[:, c], start=True, stop=True)
            ins.then_inc(state_summed, 1)
            if more:
                inside(i + 1, 1 - u)

        inside(0, 0)
        each_tile(pe, outputs)

    def vector(dve):
        lower.vector(dve)
        step = Steps(dve, step_sem)
        step(nc.vector.tensor_scalar(nlbc, lower.lbc, -1.0, None, ALU.mult))
        nc.vector.memset(flat(S), 0.0).then_inc(S_ready, 1)
        dve.sem_inc(o_ready, 2)
        dve.wait_ge(consts, 48)
        for h in range(HH):
            dve.wait_ge(f_sigmoid, h + 1)
            nc.vector.tensor_scalar(key[:, h], ek[:, h], -1.0, nlbc[:, h:h + 1], ALU.add, ALU.mult
                                    ).then_inc(key_ready, 1)
        dve.wait_ge(q_sigmoid, 1)
        step(nc.vector.scalar_tensor_tensor(out=flat(q), in0=flat(qh), scalar=DK ** -0.5, in1=flat(q),
                                            op0=ALU.mult, op1=ALU.mult))
        for h in range(HH):
            dve.wait_ge(log_ready, h + 1)
            for c in range(0, SEQ, W):
                ins = nc.vector.tensor_tensor_scan(ecum[:, h, c:c + W], reset, ek[:, h, c:c + W], 0.0, ALU.mult, ALU.add)
            step(ins)
            c3 = ecum[:, h].rearrange("p (g s) -> p g s", s=SUB)
            middle, end = c3[:, :, SUB // 2 - 1:SUB // 2], c3[:, :, SUB - 1:SUB]
            nc.vector.tensor_tensor(qh[:, h].rearrange("p (g s) -> p g s", s=SUB), c3,
                                    middle.broadcast_to([P, QT * NS, SUB]), ALU.subtract)
            nc.vector.tensor_tensor(ek[:, h].rearrange("p (g s) -> p g s", s=SUB),
                                    end.broadcast_to([P, QT * NS, SUB]), c3, ALU.subtract)
            c4 = ecum[:, h].rearrange("p (t g s) -> p t g s", g=NS, s=SUB)
            ends = c4[:, :, :, SUB - 1:SUB].rearrange("p t g o -> p t (g o)")
            middles = c4[:, :, :, SUB // 2 - 1:SUB // 2].rearrange("p t g o -> p t (g o)")
            nc.vector.tensor_tensor(R[:, h, :, 0:NS], middles.unsqueeze(3).broadcast_to([P, QT, NS, NS]),
                                    bc(ends, 2, NS), ALU.subtract)
            step(nc.vector.tensor_tensor(R[:, h, :, NS], ends[:, :, NS - 1:NS].broadcast_to([P, QT, NS]), ends,
                                         ALU.subtract))
            r = R[:, h].rearrange("p t a b -> p (t a b)")
            nc.vector.tensor_scalar(r, r, 0.0, None, ALU.min).then_inc(diffs_ready, 1)
        for h in range(HH):
            dve.wait_ge(exps_ready, h + 1)
            nc.vector.tensor_tensor(ek[:, h], ek[:, h], key[:, h], ALU.mult)
            nc.vector.tensor_tensor(kd[:, h], kd[:, h], key[:, h], ALU.mult)
            ins = nc.vector.tensor_tensor(qh[:, h], qh[:, h], q[:, h], ALU.mult)
        for n in range(NS):
            ins = nc.vector.memset(R.rearrange("p h t a b -> p (h t) a b")[:, :, n, n:NS], 0.0)
        step(ins)

        def factors(i, u, tile_steps):
            for h in range(HH):
                e = ek[:, h, tile(i)].rearrange("p (j s) -> p j s", s=SUB)
                r = R[:, h, bass.ds(i, 1), 0:NS].rearrange("p o n j -> p (o n) j")
                tile_steps(nc.vector.tensor_tensor(kh[:, u, h].rearrange("p n (j s) -> p n j s", s=SUB),
                                                   bc(e, 1, NS), r.unsqueeze(3).broadcast_to([P, NS, NS, SUB]),
                                                   ALU.mult))
                at = (u * HH + h) * NS * P
                own = kh_flat[:, at:at + NS * (P + SUB)].rearrange("p (n x) -> p n x", n=NS)[:, :, 0:SUB]
                nc.vector.tensor_copy(own, kd[:, h, tile(i)].rearrange("p (j s) -> p j s", s=SUB)
                                      ).then_inc(kh_ready, 1)
            nc.vector.tensor_copy(last[:, u], ecum[:, :, bass.ds(i * P + P - 1, 1)].rearrange("p h o -> p (h o)"))
            nc.vector.tensor_tensor(qe[:, u], q[:, :, tile(i)], ecum[:, :, tile(i)], ALU.mult)
            for h in range(HH):
                r = R[:, h, bass.ds(i, 1), NS].rearrange("p o j -> p (o j)")
                ins = nc.vector.tensor_tensor(kl[:, u, h].rearrange("p (j s) -> p j s", s=SUB),
                                              ek[:, h, tile(i)].rearrange("p (j s) -> p j s", s=SUB),
                                              r.unsqueeze(2).broadcast_to([P, NS, SUB]), ALU.mult)
            ins.then_inc(kl_ready, 1)

        def one_tile(eng, i, u, r, more):
            dve.wait_ge(att_ready, i + 1)
            nc.vector.tensor_tensor(att[:, u], ps[:, u].rearrange("p (h n) -> p h n", h=HH), bc(tri, 1, HH), ALU.mult
                                    ).then_inc(att_masked, 1)
            if more:
                factors(i + 1, 1 - u, Steps(dve, tile_step, HH, i + 1))
            dve.wait_ge(state_summed, i + 1)
            for h in range(HH):
                ins = nc.vector.scalar_tensor_tensor(out=S[:, h], in0=S[:, h], scalar=last[:, u, h:h + 1],
                                                     in1=ps[:, 6 + u, h * P:(h + 1) * P], op0=ALU.mult, op1=ALU.add)
            ins.then_inc(S_ready, 1)
            dve.wait_ge(root_ready, i + 1)
            nc.vector.reciprocal(ss[:, u, 2], ss[:, u, 1]).then_inc(recip_ready, 1)
            dve.wait_ge(recip_ready, i + 1)
            dve.wait_ge(stored[u], 16 * r + 16)
            g = by_tile(gate)[:, bass.ds(i, 1), :].rearrange("p o n -> p (o n)")
            for h in range(HH):
                c = slice(h * P, (h + 1) * P)
                ins = nc.vector.scalar_tensor_tensor(out=o[:, u, h], in0=ps[:, 4 + u, c], scalar=ss[:, u, 2, h:h + 1],
                                                     in1=g[:, c], op0=ALU.mult, op1=ALU.mult)
            ins.then_inc(o_ready, 1)

        dve.wait_ge(gated, 2)
        factors(0, 0, Steps(dve, tile_step, HH, 0))
        each_tile(dve, one_tile)

    recip_ready = sem("recip_ready")
    k.stage(sync=sync, tensor=tensor, scalar=scalar, vector=vector, gpsimd=gpsimd)


def hgrn_sample_stage(k, d, ident):
    nc, ps = k.nc, k.ps
    N = NSMP
    lower = Lower(k, d, "hs")
    hq, hf, sq, f, key, cum, ecum, qe, qh, kh, kl = (k.buf(HH, N) for _ in range(11))
    v, hg, sg, o, osq = (k.buf(HH, DK)[0:N] for _ in range(5))
    klT, oT = k.buf(HH, DK)[0:N], k.buf(HH, N)
    att = k.buf(HH, N)[0:N]
    vm = k.buf(HH, NSEQ, DK)[0:N]
    S = k.buf(HH, NSEQ, DK)
    reset, tri, seqmask, gn = k.buf(HH * N), k.buf(N)[0:N], k.buf(NSEQ)[0:N], k.buf(DK)[0:N]
    ss = k.buf(3, HH)[0:N]
    loaded, act_done, pe_done, dve_out, step_sem, stored = (
        k.sem(f"hs_{w}") for w in ("loaded", "act_done", "pe_done", "dve_out", "step", "stored"))
    flat = lambda a: a.rearrange("p h n -> p (h n)")
    rows = slice(SEQ, SEQ + N)

    def sync(sp):
        lower.sync(sp)
        for to, src in ((hq, d["zT"][0:HH, :, rows].rearrange("h p n -> p h n")),
                        (hf, d["zT"][HH:2 * HH, :, rows].rearrange("h p n -> p h n")),
                        (flat(v), d["zh"][rows, 0:512]), (flat(hg), d["zh"][rows, 512:1024]),
                        (reset, d["reset4"]), (tri, d["blocktri"]), (seqmask, d["seqmask"]),
                        (gn, d["gnorm"].partition_broadcast(N).rearrange("p o n -> p (o n)"))):
            sp.dma_start(to, src).then_inc(loaded, 16)
        for h in range(HH):
            sp.dma_start(S[:, h], d["state"][:, h].rearrange("b p n -> p b n")).then_inc(loaded, 16)
        sp.wait_ge(dve_out, 10)
        for h in range(HH):
            sp.dma_start(d["hgrn_s"][:, h].rearrange("b p n -> p b n"), S[:, h]).then_inc(stored, 16)
        sp.dma_start(d["ob"][rows, :], flat(o)).then_inc(stored, 16)
        sp.wait_ge(stored, 80)

    def scalar(act):
        lower.scalar(act)
        act.wait_ge(loaded, 192)
        nc.scalar.activation(flat(f), flat(hf), ACT.Sigmoid).then_inc(act_done, 1)
        nc.scalar.activation(flat(sq), flat(hq), ACT.Sigmoid).then_inc(act_done, 1)
        nc.scalar.activation(flat(sg), flat(hg), ACT.Sigmoid).then_inc(act_done, 1)
        act.wait_ge(dve_out, 1)
        nc.scalar.activation(flat(f), flat(f), ACT.Ln).then_inc(act_done, 1)
        act.wait_ge(dve_out, 2)
        nc.scalar.activation(flat(ecum), flat(cum), ACT.Exp).then_inc(act_done, 1)
        act.wait_ge(dve_out, 3)
        nc.scalar.activation(flat(kh), flat(qh), ACT.Exp, scale=-1.0).then_inc(act_done, 1)
        act.wait_ge(act_done, 6)
        nc.scalar.activation(flat(qh), flat(qh), ACT.Exp).then_inc(act_done, 1)
        nc.scalar.activation(flat(kl), flat(kl), ACT.Exp).then_inc(act_done, 1)
        act.wait_ge(dve_out, 8)
        nc.scalar.activation(ss[:, 1], ss[:, 0], ACT.Sqrt, scale=1.0 / DK, bias=k.eps[0:N]).then_inc(act_done, 1)

    def tensor(pe):
        pe.wait_ge(dve_out, 5)
        for h in range(HH):
            nc.tensor.matmul(ps[0:N, 0, h * N:(h + 1) * N], kh[:, h], qh[:, h], start=True, stop=True)
            ins = nc.tensor.transpose(ps[0:N, 1, h * DK:(h + 1) * DK], kl[:, h], ident)
        ins.then_inc(pe_done, 1)
        pe.wait_ge(dve_out, 6)
        for h in range(HH):
            nc.tensor.matmul(ps[:, 2, h * N:(h + 1) * N], v[:, h], att[:, h], start=True, stop=False)
            for b in range(NSEQ):
                c = b * NNEW
                ins = nc.tensor.matmul(ps[:, 2, h * N + c:h * N + c + NNEW], S[:, h, b], qe[:, h, c:c + NNEW],
                                       start=False, stop=(b == NSEQ - 1))
        ins.then_inc(pe_done, 1)
        pe.wait_ge(dve_out, 7)
        for h in range(HH):
            ins = nc.tensor.transpose(ps[0:N, 3, h * DK:(h + 1) * DK], oT[:, h], ident)
        ins.then_inc(pe_done, 1)
        for h in range(HH):
            if h >= 2:
                pe.wait_ge(states, h - 1)
            for half in range(2):
                ins = nc.tensor.matmul(ps[:, 4 + 2 * (h % 2) + half], klT[:, h],
                                       vm[:, h, 4 * half:4 * half + 4].rearrange("p b n -> p (b n)"),
                                       start=True, stop=True)
            ins.then_inc(pe_done, 1)

    states = k.sem("hs_states_updated")

    def vector(dve):
        lower.vector(dve)
        step = Steps(dve, step_sem)
        dve.wait_ge(act_done, 1)
        for h in range(HH):
            ins = nc.vector.tensor_scalar(f[:, h], f[:, h], lower.lbc[:, h:h + 1], lower.lb[:, h:h + 1],
                                          ALU.mult, ALU.add)
        step(ins)
        nc.vector.tensor_scalar(flat(key), flat(f), -1.0, 1.0, ALU.mult, ALU.add).then_inc(dve_out, 1)
        dve.wait_ge(act_done, 4)
        nc.vector.tensor_tensor_scan(flat(cum), reset, flat(f), 0.0, ALU.mult, ALU.add).then_inc(dve_out, 1)
        dve.wait_ge(dve_out, 2)
        c4, q4, l4 = (flat(a).rearrange("p (g s) -> p g s", s=NNEW) for a in (cum, qh, kl))
        n4 = [P, HH * NSEQ, NNEW]
        step(nc.vector.tensor_tensor(l4, c4[:, :, NNEW - 1:NNEW].broadcast_to(n4), c4, ALU.subtract))
        nc.vector.tensor_tensor(q4, c4, c4[:, :, 1:2].broadcast_to(n4), ALU.subtract).then_inc(dve_out, 1)
        step(nc.vector.scalar_tensor_tensor(out=flat(sq), in0=flat(sq), scalar=DK ** -0.5, in1=flat(hq),
                                            op0=ALU.mult, op1=ALU.mult))
        dve.wait_ge(act_done, 8)
        step(nc.vector.tensor_tensor(flat(qe), flat(sq), flat(ecum), ALU.mult))
        step(nc.vector.tensor_tensor(flat(qh), flat(sq), flat(qh), ALU.mult))
        nc.vector.tensor_tensor(flat(kh), flat(kh), flat(key), ALU.mult).then_inc(dve_out, 1)
        nc.vector.tensor_tensor(flat(kl), flat(kl), flat(key), ALU.mult).then_inc(dve_out, 1)
        for h in range(HH):
            ins = nc.vector.tensor_tensor(vm[:, h], bc(v[:, h], 1, NSEQ),
                                          seqmask.unsqueeze(2).broadcast_to([N, NSEQ, DK]), ALU.mult)
        dve.wait_ge(pe_done, 1)
        step(nc.vector.tensor_copy(flat(klT), ps[0:N, 1]))
        nc.vector.tensor_tensor(att, ps[0:N, 0, 0:HH * N].rearrange("p (h n) -> p h n", h=HH), bc(tri, 1, HH),
                                ALU.mult).then_inc(dve_out, 1)
        dve.wait_ge(pe_done, 2)
        nc.vector.tensor_copy(flat(oT), ps[:, 2, 0:HH * N]).then_inc(dve_out, 1)
        dve.wait_ge(pe_done, 3)
        step(nc.vector.tensor_copy(flat(o), ps[0:N, 3]))
        step(nc.vector.tensor_tensor(flat(osq), flat(o), flat(o), ALU.mult))
        nc.vector.tensor_reduce(ss[:, 0], osq, AX.X, ALU.add).then_inc(dve_out, 1)
        for h in range(HH):
            dve.wait_ge(pe_done, 4 + h)
            last = ecum[:, h].rearrange("p (b t) -> p b t", t=NNEW)[:, :, NNEW - 1:NNEW]
            step(nc.vector.tensor_tensor(S[:, h], S[:, h], last.broadcast_to([P, NSEQ, DK]), ALU.mult))
            for half in range(2):
                g = S[:, h, 4 * half:4 * half + 4].rearrange("p b n -> p (b n)")
                ins = nc.vector.tensor_tensor(g, g, ps[:, 4 + 2 * (h % 2) + half], ALU.add)
            ins.then_inc(states, 1)
        step(nc.vector.tensor_tensor(flat(sg), flat(sg), flat(hg), ALU.mult))
        step(nc.vector.tensor_tensor(sg, sg, bc(gn, 1, HH), ALU.mult))
        dve.wait_ge(act_done, 9)
        step(nc.vector.reciprocal(ss[:, 2], ss[:, 1]))
        step(nc.vector.tensor_tensor(o, o, ss[:, 2].unsqueeze(2).broadcast_to([N, HH, DK]), ALU.mult))
        dve.wait_ge(states, HH)
        nc.vector.tensor_tensor(flat(o), flat(o), flat(sg), ALU.mult).then_inc(dve_out, 2)

    k.stage(sync=sync, tensor=tensor, scalar=scalar, vector=vector)


def merge_stage(k, d, ident, route):
    nc, ps = k.nc, k.ps
    W3 = TPAD // 3
    assert NT % 3 == 0 and NT % 2 == 1
    oT, mT = k.buf(2, 4, TPAD), k.buf(KD, TPAD)
    wo, wr, br_, g2, iota = k.buf(KD, D), k.buf(KD, NG + NE), k.buf(NG + NE), k.buf(D), k.buf(NE)
    w, m, tmp = k.buf(2, 2, 4, P), k.buf(2, 2, TPAD), k.buf(3, 2, W3)
    lg, sel = k.buf(NG + NE), k.buf(NG, EPG)
    g8, e8, top, idx, idf = k.buf(8), k.buf(8), k.buf(2, 8), k.buf(2, 8), k.buf(2, 8)
    st, hot = k.buf(16), k.buf(NG)
    low = k.low
    bo, ob, oa, t3, gates = k.buf(3, 3, 512), k.buf(3, 512), k.buf(3, 512), k.buf(3, 3, 512), k.buf(NT, 24)
    k.low = low
    x, x2, h2, sq, h2T = k.buf(D), k.buf(D), k.buf(D), k.buf(D), k.buf(KD, P)
    mg = k.buf(2, KD, P)
    sem = lambda what: k.sem(f"m_{what}")
    weights, padded, gates_loaded, gates_ready = (sem(n) for n in ("weights_loaded", "pads_zeroed", "gates_loaded",
                                                                   "gates_ready"))
    rows_loaded, rows_turned = [sem(f"rows_loaded{u}") for u in range(3)], [sem(f"rows_turned{u}") for u in range(3)]
    oa_ready, transposed = sem("oa_ready"), sem("transposed")
    block_loaded = [sem(f"block_loaded{u}") for u in range(2)]
    sigmoid_ready, products_ready, merged = sem("sigmoid_ready"), sem("products_ready"), sem("merged")
    mg_ready, projected, x_loaded, x2_ready = sem("mg_ready"), sem("projected"), sem("x_loaded"), sem("x2_ready")
    squared, root_ready, h2_ready, h2_turned = sem("squared"), sem("root_ready"), sem("h2_ready"), sem("h2_turned")
    h2T_ready, logits_ready, logits_read = sem("h2T_ready"), sem("logits_ready"), sem("logits_read")
    group_max, group_exp, two_max, two_exp = sem("group_max"), sem("group_exp"), sem("two_max"), sem("two_exp")
    x2_stored, h2_stored = sem("x2_stored"), sem("h2_stored")
    sum_step, merge_step, norm_step, route_step = sem("sum_step"), sem("merge_step"), sem("norm_step"), sem("route_step")

    def sync(sp):
        pad = slice(SEQ + NSMP, TPAD)
        for n in range(3):
            sp.dma_start(d["branches"][n, pad, :], d["x_all"][pad, 0:512]).then_inc(padded, 16)
        sp.dma_start(d["ob"][pad, :], d["x_all"][pad, 0:512]).then_inc(padded, 16)
        sp.dma_start(gates, d["zn"].rearrange("(t p) c -> p t c", p=P)[:, :, ZC - 24:ZC]).then_inc(gates_loaded, 16)
        sp.wait_ge(padded, 64)
        with sp.Fori(0, NT // 3) as i:
            for u in range(3):
                sp.wait_ge(rows_turned[u], i + 1)
                t = tile(3 * i + u)
                sp.dma_start(bo[:, u], d["branches"][:, t, :].rearrange("b p n -> p b n")
                             ).then_inc(rows_loaded[u], 16)
                sp.dma_start(ob[:, u], d["ob"][t, :]).then_inc(rows_loaded[u], 16)
        with sp.Fori(0, KD // 2) as i:
            for u in range(2):
                b = 2 * i + u
                sp.wait_ge(merged, 3 * b + 3)
                for n, name in enumerate(("w_pa", "w_pb")):
                    sp.dma_start(w[:, u, n], d[name].rearrange("p (c n) -> p c n", c=4)[:, :, tile(b)]
                                 ).then_inc(block_loaded[u], 16)
                sp.dma_start(m[:, u], d["zT"][2 * HH:24].rearrange("(s b) p n -> b p s n", s=2)[bass.ds(b, 1)]
                             .rearrange("o p s n -> (o p) s n")).then_inc(block_loaded[u], 16)
        sp.sem_inc(x2_stored, 16)
        sp.sem_inc(h2_stored, 16)
        with sp.Fori(0, NT) as t:
            sp.wait_ge(x2_ready, t + 2)
            sp.dma_start(x, d["x_all"][tile(t), :]).then_inc(x_loaded, 16)
            sp.wait_ge(x2_ready, t + 3)
            sp.dma_start(d["x2"][tile(t), :], x2).then_inc(x2_stored, 16)
            sp.wait_ge(h2_ready, t + 1)
            sp.dma_start(d["h2"][tile(t), :], h2).then_inc(h2_stored, 16)
        sp.wait_ge(x2_stored, 16 * NT + 16)
        sp.wait_ge(h2_stored, 16 * NT + 16)

    def gpsimd(pool):
        pool.wait_ge(merged, 3 * KD + 6)

        def stage(t, u):
            pool.wait_ge(projected, 2 * t + 2)
            nc.gpsimd.tensor_copy(mg[:, u], mT[:, :, tile(t)]).then_inc(mg_ready, 1)

        with pool.Fori(0, NT // 2) as i:
            for u in range(2):
                stage(2 * i + u, u)
        stage(NT - 1, 0)

    def scalar(act):
        for to, src in ((wo, d["w_out"].rearrange("p (c n) -> p c n", c=KD)),
                        (wr, d["w_router"].rearrange("p (c n) -> p c n", c=KD)),
                        (br_, d["b_router"].partition_broadcast(P).rearrange("p o n -> p (o n)")),
                        (g2, d["norm2"].partition_broadcast(P).rearrange("p o n -> p (o n)")),
                        (iota, d["iota"][:, 0:NE])):
            act.dma_start(to, src).then_inc(weights, 16)
        for u in range(3):
            act.sem_inc(rows_turned[u], 1)
        act.wait_ge(gates_loaded, 16)
        nc.scalar.activation(gates, gates, ACT.Sigmoid).then_inc(gates_ready, 1)
        with act.Fori(0, NT // 3) as i:
            for u in range(3):
                t = 3 * i + u
                act.wait_ge(transposed, t + 1)
                for n in range(2):
                    ins = nc.scalar.activation(oT[:, n, :, tile(t)], ps[:, 2 * u + n].rearrange("p (c n) -> p c n", c=4),
                                               ACT.Copy)
                ins.then_inc(rows_turned[u], 1)
        with act.Fori(0, KD // 2) as i:
            for u in range(2):
                act.wait_ge(block_loaded[u], 48 * i + 48)
                mf = m[:, u].rearrange("p s n -> p (s n)")
                nc.scalar.activation(mf, mf, ACT.Sigmoid).then_inc(sigmoid_ready, 1)
        act.sem_inc(h2T_ready, 1)

        def norm(t):
            act.wait_ge(x2_ready, t + 3)
            nc.scalar.activation(sq, x2, ACT.Square, accum_out=st[:, 0:1]).then_inc(squared, 1)
            act.wait_ge(squared, t + 1)
            nc.scalar.activation(st[:, 1:2], st[:, 0:1], ACT.Sqrt, scale=1.0 / D, bias=k.eps).then_inc(root_ready, 1)
            act.wait_ge(h2_turned, t + 2)
            for n in range(2):
                ins = nc.scalar.activation(h2T[:, 4 * n:4 * n + 4].rearrange("p c n -> p (c n)"), ps[:, n], ACT.Copy)
            ins.then_inc(h2T_ready, 1)

        def router(t):
            act.wait_ge(group_max, t + 1)
            nc.scalar.activation(hot, lg[:, 0:NG], ACT.Exp, bias=st[:, 3:4], accum_out=st[:, 4:5]
                                 ).then_inc(group_exp, 1)
            act.wait_ge(two_max, t + 1)
            nc.scalar.activation(st[:, 5:6], top[:, 1, 1:2], ACT.Exp, bias=st[:, 6:7]).then_inc(two_exp, 1)

        norm(0)
        with act.Fori(0, NT - 1) as t:
            norm(t + 1)
            router(t)
        router(NT - 1)

    def tensor(pe):
        with pe.Fori(0, NT // 3) as i:
            for u in range(3):
                pe.wait_ge(oa_ready, 3 * i + u + 1)
                for c in range(4):
                    nc.tensor.transpose(ps[:, 2 * u, c * P:(c + 1) * P], oa[:, u, c * P:(c + 1) * P], ident)
                    ins = nc.tensor.transpose(ps[:, 2 * u + 1, c * P:(c + 1) * P], ob[:, u, c * P:(c + 1) * P], ident)
                ins.then_inc(transposed, 1)
        for u in range(3):
            pe.wait_ge(rows_turned[u], NT // 3 + 1)
        with pe.Fori(0, KD // 2) as i:
            for u in range(2):
                pe.wait_ge(block_loaded[u], 48 * i + 48)
                for g in range(3):
                    pe.wait_ge(merged, 3 * (2 * i + u) + g + 4)
                    for n in range(2):
                        for c in range(4):
                            ins = nc.tensor.matmul(ps[:, 2 * g + n, 0:W3], w[:, u, n, c],
                                                   oT[:, n, c, g * W3:(g + 1) * W3], start=(c == 0), stop=(c == 3))
                    ins.then_inc(products_ready, 1)
        pe.wait_ge(weights, 80)
        pe.sem_inc(projected, 4)
        pe.sem_inc(h2_turned, 1)

        def project(t, u, half):
            if half == 0:
                pe.wait_ge(mg_ready, t + 1)
                pe.wait_ge(x2_ready, t + 1)
            for c in range(KD):
                ins = nc.tensor.matmul(ps[:, 4 + 2 * u + half], mg[:, u, c], wo[:, c, half * 512:(half + 1) * 512],
                                       start=(c == 0), stop=(c == KD - 1))
            ins.then_inc(projected, 1)

        def turn(t):
            pe.wait_ge(h2_ready, t + 1)
            pe.wait_ge(h2T_ready, t + 1)
            for c in range(KD):
                ins = nc.tensor.transpose(ps[:, c // 4, c % 4 * P:(c % 4 + 1) * P], h2[:, c * P:(c + 1) * P], ident)
            ins.then_inc(h2_turned, 1)

        def logits(t):
            pe.wait_ge(h2T_ready, t + 2)
            pe.wait_ge(logits_read, t + 1)
            for c in range(KD):
                ins = nc.tensor.matmul(ps[:, 2, 0:NG + NE], h2T[:, c], wr[:, c], start=(c == 0), stop=(c == KD - 1))
            ins.then_inc(logits_ready, 1)

        for half in range(2):
            project(0, 0, half)
        with pe.Fori(0, NT // 2) as i:
            for u in range(2):
                t = 2 * i + u
                project(t + 1, 1 - u, 0)
                turn(t)
                project(t + 1, 1 - u, 1)
                logits(t)
        turn(NT - 1)
        logits(NT - 1)

    def vector(dve):
        dve.wait_ge(gates_ready, 1)
        with dve.Fori(0, NT // 3) as i:
            step = Steps(dve, sum_step, 6, i)
            for u in range(3):
                dve.wait_ge(rows_loaded[u], 32 * i + 32)
                g = gates[:, bass.ds(3 * i + u, 1), :].rearrange("p o (h n) -> p (o h) n", n=3)
                for n in range(3):
                    ins = nc.vector.tensor_tensor(t3[:, u, n].rearrange("p (h n) -> p h n", h=HEADS),
                                                  bo[:, u, n].rearrange("p (h n) -> p h n", h=HEADS),
                                                  g[:, :, n:n + 1].broadcast_to([P, HEADS, HD]), ALU.mult)
                step(ins)
                step(nc.vector.tensor_tensor(t3[:, u, 0], t3[:, u, 0], t3[:, u, 1], ALU.add))
                nc.vector.tensor_tensor(oa[:, u], t3[:, u, 0], t3[:, u, 2], ALU.add).then_inc(oa_ready, 1)
            step.close()
        dve.sem_inc(merged, 6)
        with dve.Fori(0, KD // 2) as i:
            step = Steps(dve, merge_step, 6, i)
            for u in range(2):
                b = 2 * i + u
                dve.wait_ge(sigmoid_ready, b + 1)
                for g in range(3):
                    c = slice(g * W3, (g + 1) * W3)
                    dve.wait_ge(products_ready, 3 * b + g + 1)
                    for n in range(2):
                        ins = nc.vector.tensor_tensor(tmp[:, g, n], ps[:, 2 * g + n, 0:W3], m[:, u, n, c], ALU.mult)
                    step(ins)
                    nc.vector.tensor_tensor(mT[:, bass.ds(b, 1), c], tmp[:, g, 0:1], tmp[:, g, 1:2], ALU.add
                                            ).then_inc(merged, 1)
            step.close()
        dve.wait_ge(weights, 80)
        dve.sem_inc(x2_ready, 2)
        dve.sem_inc(logits_read, 1)

        def norm(t, u):
            step = Steps(dve, norm_step, 1, t)
            dve.wait_ge(x_loaded, 16 * t + 16)
            dve.wait_ge(x2_stored, 16 * t + 16)
            for half in range(2):
                c = slice(512 * half, 512 * half + 512)
                dve.wait_ge(projected, 2 * t + 5 + half)
                ins = nc.vector.tensor_tensor(x2[:, c], ps[:, 4 + 2 * u + half], x[:, c], ALU.add)
            ins.then_inc(x2_ready, 1)
            dve.wait_ge(root_ready, t + 1)
            step(nc.vector.reciprocal(st[:, 2:3], st[:, 1:2]))
            dve.wait_ge(h2_stored, 16 * t + 16)
            dve.wait_ge(h2_turned, t + 1)
            nc.vector.scalar_tensor_tensor(out=h2, in0=x2, scalar=st[:, 2:3], in1=g2, op0=ALU.mult, op1=ALU.mult
                                           ).then_inc(h2_ready, 1)

        def router(t):
            step = Steps(dve, route_step, 15, t)
            dve.wait_ge(logits_ready, t + 1)
            step(nc.vector.memset(g8, -3e38))
            nc.vector.tensor_tensor(lg, ps[:, 2, 0:NG + NE], br_, ALU.add).then_inc(logits_read, 1)
            dve.wait_ge(logits_read, t + 2)
            step(nc.vector.tensor_copy(g8[:, 0:NG], lg[:, 0:NG]))
            k.pin(dve)
            step(nc.vector.max(top[:, 0], g8))
            k.pin(dve)
            step(nc.vector.max_index(idx[:, 0].bitcast(U32), top[:, 0], g8))
            nc.vector.tensor_scalar(st[:, 3:4], top[:, 0, 0:1], -1.0, None, ALU.mult).then_inc(group_max, 1)
            step(nc.vector.tensor_copy(idf[:, 0], idx[:, 0].bitcast(U32)))
            dve.wait_ge(group_exp, t + 1)
            step(nc.vector.tensor_scalar(hot, iota[:, 0:NG], idf[:, 0, 0:1], None, ALU.is_equal))
            step(nc.vector.tensor_tensor(sel, lg[:, NG:].rearrange("p (g e) -> p g e", g=NG),
                                         hot.unsqueeze(2).broadcast_to([P, NG, EPG]), ALU.mult))
            step(nc.vector.tensor_reduce(e8, sel.rearrange("p g e -> p e g"), AX.X, ALU.add))
            k.pin(dve)
            step(nc.vector.max(top[:, 1], e8))
            k.pin(dve)
            step(nc.vector.max_index(idx[:, 1].bitcast(U32), top[:, 1], e8))
            nc.vector.tensor_scalar(st[:, 6:7], top[:, 1, 0:1], -1.0, None, ALU.mult).then_inc(two_max, 1)
            step(nc.vector.tensor_copy(idf[:, 1], idx[:, 1].bitcast(U32)))
            dve.wait_ge(two_exp, t + 1)
            step(nc.vector.scalar_tensor_tensor(out=st[:, 7:8], in0=st[:, 5:6], scalar=1.0, in1=st[:, 4:5],
                                                op0=ALU.add, op1=ALU.mult))
            step(nc.vector.reciprocal(st[:, 10:11], st[:, 7:8]))
            step(nc.vector.tensor_tensor(st[:, 11:12], st[:, 10:11], st[:, 5:6], ALU.mult))
            step(nc.vector.scalar_tensor_tensor(out=st[:, 8:10], in0=idf[:, 0, 0:1].broadcast_to([P, 2]),
                                                scalar=float(EPG), in1=idf[:, 1, 0:2], op0=ALU.mult, op1=ALU.add))
            nc.vector.tensor_copy(route[:, bass.ds(t, 1), :], st[:, 8:12].unsqueeze(1))
            step.close()

        norm(0, 0)
        with dve.Fori(0, NT // 2) as i:
            for u in range(2):
                norm(2 * i + u + 1, 1 - u)
                router(2 * i + u)
        router(NT - 1)

    k.stage(sync=sync, tensor=tensor, scalar=scalar, vector=vector, gpsimd=gpsimd)


def dispatch_stage(k, d, route, gather, blocks):
    nc, ps = k.nc, k.ps
    iota, valid, before, ones = k.buf(NE), k.buf(NT), k.buf(P), k.buf(P)
    hot, a, rank = k.buf(2, NT, NE), k.buf(NT, NE), k.buf(NT, NE)
    tmp, r, lim = k.buf(2, NT, NE), k.buf(2, NT), k.buf(EPG)
    more, upto, start, one = k.buf(NE), k.buf(NE), k.buf(NE), k.buf(NE)
    cmp_e, cmp_r, cmp_b = k.buf(NE, 8), k.buf(2, NT, 8), k.buf(NOVER, NE)
    rb, blk, alt, scat = k.buf(2, NT), k.buf(2, NT), k.buf(2, NT), k.buf(2, NT)
    tbl, fill, token = k.buf(NB + 2), k.buf((NB + 1)), k.buf(NT)
    base = k.buf(NT + 1, NE)
    scat_i = k.buf(2, NT)
    consts, step_sem, pe_done, prefix_ready, filled, table = (
        k.sem(f"d_{w}") for w in ("consts_loaded", "step", "pe_done", "hot_ready", "filled", "dest_ready"))
    scattered = k.own_sem("d_scattered")

    def sync(sp):
        for to, src in ((iota, d["iota"][:, 0:NE]), (valid, d["valid"]), (before, d["before"]), (lim, d["limits"]),
                        (tbl, d["block_ids"]), (token, d["token_ids"])):
            sp.dma_start(to if to is not token else to.bitcast(I32), src).then_inc(consts, 16)
        sp.wait_ge(table, 1)
        sp.dma_start(d["source"].rearrange("(p n) o -> p (n o)", p=P), fill.bitcast(I32)).then_inc(filled, 16)

    def gpsimd(pool):
        pool.wait_ge(filled, 16)
        pool.wait_ge(table, 2)
        for t in range(NT):
            parts = P if t < QT else NSMP
            for n in range(2):
                nc.gpsimd.indirect_dma_start(
                    d["source"], bass.IndirectOffsetOnAxis(ap=scat_i[0:parts, n, t:t + 1].bitcast(I32), axis=0),
                    token[0:parts, t:t + 1].bitcast(I32), None).then_inc(scattered, 16)
        pool.wait_ge(scattered, 16 * 2 * NT)

    def tensor(pe):
        pe.wait_ge(prefix_ready, 1)
        flat = a.rearrange("p t e -> p (t e)")
        nc.tensor.matmul(ps[:, 0, 0:NT * NE], before, flat, start=True, stop=True)
        nc.tensor.matmul(ps[:, 1, 0:NT * NE], ones, flat, start=True, stop=True).then_inc(pe_done, 1)

    def vector(dve):
        step = Steps(dve, step_sem)
        step(nc.vector.memset(fill.bitcast(I32), SEQ + NSMP))
        nc.vector.memset(ones, 1.0)
        nc.vector.memset(one, 1.0)
        step(nc.vector.memset(base[:, 0], 0.0))
        nc.vector.memset(r, 0.0).then_inc(table, 1)
        dve.wait_ge(consts, 96)
        shape = [P, NT, NE]
        for n in range(2):
            ins = nc.vector.tensor_tensor(hot[:, n], bc(iota, 1, NT), route[:, :, n:n + 1].broadcast_to(shape),
                                          ALU.is_equal)
        step(ins)
        for n in range(2):
            ins = nc.vector.tensor_tensor(hot[:, n], hot[:, n], valid.unsqueeze(2).broadcast_to(shape), ALU.mult)
        step(ins)
        nc.vector.tensor_tensor(a, hot[:, 0], hot[:, 1], ALU.add).then_inc(prefix_ready, 1)
        dve.wait_ge(pe_done, 1)
        total = ps[:, 1, 0:NT * NE].rearrange("p (t e) -> p t e", t=NT)
        for t in range(NT):
            step(nc.vector.tensor_tensor(base[:, t + 1], base[:, t], total[:, t], ALU.add))
        count = base[:, NT]
        step(nc.vector.tensor_tensor(rank, ps[:, 0, 0:NT * NE].rearrange("p (t e) -> p t e", t=NT), base[:, 0:NT],
                                     ALU.add))
        for n in range(2):
            ins = nc.vector.tensor_tensor(tmp[:, n], hot[:, n], rank, ALU.mult)
        step(ins)
        step(nc.vector.tensor_reduce(r, tmp, AX.X, ALU.add))
        step(nc.vector.tensor_tensor(cmp_e, count.unsqueeze(2).broadcast_to([P, NE, 8]), bc(lim, 1, NE), ALU.is_gt))
        step(nc.vector.tensor_reduce(more, cmp_e, AX.X, ALU.add))
        step(nc.vector.tensor_tensor_scan(upto, one, more, 0.0, ALU.mult, ALU.add))
        step(nc.vector.tensor_tensor(start, upto, more, ALU.subtract))
        step(nc.vector.tensor_tensor(cmp_b, bc(upto, 1, NOVER), iota[:, 0:NOVER].unsqueeze(2)
                                     .broadcast_to([P, NOVER, NE]), ALU.is_le))
        step(nc.vector.tensor_reduce(tbl[:, NE:NB], cmp_b, AX.X, ALU.add))
        step(nc.vector.tensor_scalar(tbl[:, NE:NB], tbl[:, NE:NB], float(NE - 1), None, ALU.min))
        step(nc.vector.tensor_scalar(tbl[:, NB:NB + 1], upto[:, NE - 1:NE], 0.5, NE / 2 + 0.25, ALU.mult, ALU.add))
        step(nc.vector.tensor_copy(blocks.bitcast(I32), tbl))
        for n in range(2):
            ins = nc.vector.tensor_tensor(cmp_r[:, n], r[:, n].unsqueeze(2).broadcast_to([P, NT, 8]), bc(lim, 1, NT),
                                          ALU.is_ge)
        step(ins)
        step(nc.vector.tensor_reduce(rb, cmp_r, AX.X, ALU.add))
        for n in range(2):
            ins = nc.vector.tensor_tensor(tmp[:, n], hot[:, n], bc(start, 1, NT), ALU.mult)
        step(ins)
        step(nc.vector.tensor_reduce(alt, tmp, AX.X, ALU.add))
        step(nc.vector.tensor_tensor(alt, alt, rb, ALU.add))
        step(nc.vector.tensor_scalar(alt, alt, float(NE - 1), None, ALU.add))
        step(nc.vector.tensor_scalar(scat, rb, 0.0, None, ALU.is_gt))
        for n in range(2):
            eid = route[:, :, n:n + 1].rearrange("p t o -> p (t o)")
            ins = nc.vector.tensor_tensor(blk[:, n], alt[:, n], eid, ALU.subtract)
        step(ins)
        step(nc.vector.tensor_tensor(blk, blk, scat, ALU.mult))
        for n in range(2):
            eid = route[:, :, n:n + 1].rearrange("p t o -> p (t o)")
            ins = nc.vector.tensor_tensor(blk[:, n], blk[:, n], eid, ALU.add)
        step(ins)
        step(nc.vector.scalar_tensor_tensor(out=r, in0=rb, scalar=-float(P), in1=r, op0=ALU.mult, op1=ALU.add))
        step(nc.vector.scalar_tensor_tensor(out=alt, in0=blk, scalar=float(P), in1=r, op0=ALU.mult, op1=ALU.add))
        step(nc.vector.scalar_tensor_tensor(out=scat, in0=r, scalar=float(NB + 1), in1=blk, op0=ALU.mult,
                                            op1=ALU.add))
        for n in range(2):
            ins = nc.vector.tensor_tensor(alt[:, n], alt[:, n], valid, ALU.mult)
        step(ins)
        step(nc.vector.tensor_copy(gather.bitcast(I32), alt))
        nc.vector.tensor_copy(scat_i.bitcast(I32), scat).then_inc(table, 1)

    k.stage(sync=sync, tensor=tensor, vector=vector, gpsimd=gpsimd)


def experts_stage(k, d, ident, blocks):
    nc, ps = k.nc, k.ps
    FJ = DE // P
    wg, wu, wd = k.buf(2, KD, DE), k.buf(2, KD, DE), k.buf(2, FJ, D)
    x, xT, y = k.buf(2, D), k.buf(2, KD, P), k.buf(2, D)
    sg, hid = k.buf(2, FJ * P), k.buf(2, FJ, P)
    src, index = k.buf(NB + 1), k.buf(2)
    up_loaded = [k.sem(f"e_up_loaded{u}") for u in (0, 1)]
    down_loaded = [k.sem(f"e_down_loaded{u}") for u in (0, 1)]
    src_loaded, index_ready = k.sem("e_src_loaded"), k.sem("e_index_ready")
    x_loaded = [k.own_sem(f"e_x_loaded{u}") for u in (0, 1)]
    x_turned, act_xT, dve_xT = k.sem("e_x_turned"), k.sem("e_act_xT"), k.sem("e_dve_xT")
    gate_ready, up_ready, sig_ready, hid_ready = (k.sem(f"e_{w}") for w in
                                                  ("gate_ready", "up_ready", "sigmoid_ready", "hid_ready"))
    y_summed, act_y, dve_y = k.sem("e_y_summed"), k.sem("e_act_y"), k.sem("e_dve_y")
    stored = [k.sem(f"e_stored{u}") for u in (0, 1)]
    step_sem = k.sem("e_step")

    def rounds(eng):
        return eng.value_load(blocks[0:1, NB:NB + 1].bitcast(I32), min_val=NE // 2, max_val=NB // 2)

    def sync(sp):
        sp.dma_start(src.bitcast(I32), d["source"].rearrange("(p n) o -> p (n o)", p=P)).then_inc(src_loaded, 16)
        with sp.Fori(0, rounds(sp)) as i:
            for u in range(2):
                e = sp.value_load(blocks[0:1, bass.ds(2 * i + u, 1)].bitcast(I32), min_val=0, max_val=NE - 1)
                sp.wait_ge(up_ready, 2 * i + u + 1)
                for to, w in ((wg, "w_gate"), (wu, "w_up")):
                    sp.dma_start(to[:, u], d[w][bass.ds(e, 1)].rearrange("o (p c) n -> (o p) c n", p=P)
                                 ).then_inc(up_loaded[u], 16)
                sp.wait_ge(y_summed, 2 * (2 * i + u) + 2)
                sp.dma_start(wd[:, u], d["w_down"][bass.ds(e, 1)].rearrange("o (p j) n -> (o p) j n", p=P)
                             ).then_inc(down_loaded[u], 16)

    def gpsimd(pool):
        pool.wait_ge(src_loaded, 16)

        def fetch(u, column, n):
            nc.gpsimd.tensor_copy(index[:, u:u + 1].bitcast(I32), src[:, column].bitcast(I32)
                                  ).then_inc(index_ready, 1)
            pool.wait_ge(index_ready, n + 1)
            k.pin(pool)
            nc.gpsimd.indirect_dma_start(
                x[:, u], None, d["h2"], bass.IndirectOffsetOnAxis(ap=index[:, u:u + 1].bitcast(I32), axis=0)
            ).then_inc(x_loaded[u], 16)

        total = rounds(pool)
        with pool.Fori(0, total) as i:
            for u in range(2):
                pool.wait_ge(x_turned, 2 * i + u + 1)
                fetch(u, bass.ds(2 * i + u, 1), 2 * i + u)
        pool.wait_ge(x_turned, 2 * total + 1)
        k.pin(pool)
        fetch(0, slice(NB, NB + 1), 2 * total)

    def turn(pe, u, i, n):
        pe.wait_ge(x_loaded[u], 16 * i + 16)
        pe.wait_ge(act_xT, n + 1)
        pe.wait_ge(dve_xT, n + 1)
        for c in range(KD):
            ins = nc.tensor.transpose(ps[:, c // 4, c % 4 * P:(c % 4 + 1) * P], x[:, u, c:D:KD], ident)
        ins.then_inc(x_turned, 1)

    def tensor(pe):
        pe.sem_inc(up_ready, 2)
        pe.sem_inc(y_summed, 4)
        pe.sem_inc(x_turned, 2)
        turn(pe, 0, 0, 0)
        with pe.Fori(0, rounds(pe)) as i:
            for u in range(2):
                n = 2 * i + u
                pe.wait_ge(act_xT, n + 2)
                pe.wait_ge(dve_xT, n + 2)
                pe.wait_ge(up_loaded[u], 32 * i + 32)
                pe.wait_ge(hid_ready, n + 1)
                for w, bank, ready in ((wg, 2, gate_ready), (wu, 3, up_ready)):
                    for j in range(FJ):
                        for c in range(KD):
                            ins = nc.tensor.matmul(ps[:, bank, j * P:(j + 1) * P], w[:, u, c, j:DE:FJ], xT[:, u, c],
                                                   start=(c == 0), stop=(c == KD - 1))
                    ins.then_inc(ready, 1)
                turn(pe, 1 - u, i + u, n + 1)
                pe.wait_ge(hid_ready, n + 2)
                pe.wait_ge(down_loaded[u], 16 * i + 16)
                pe.wait_ge(act_y, n + 1)
                pe.wait_ge(dve_y, n + 1)
                for half in range(2):
                    for j in range(FJ):
                        ins = nc.tensor.matmul(ps[:, 4 + half], hid[:, u, j], wd[:, u, j, half * 512:half * 512 + 512],
                                               start=(j == 0), stop=(j == FJ - 1))
                    ins.then_inc(y_summed, 1)

    def scalar(act):
        act.sem_inc(act_xT, 1)
        act.sem_inc(act_y, 1)
        for u in range(2):
            act.sem_inc(stored[u], 16)

        def copy_x(u, n):
            act.wait_ge(x_turned, n + 3)
            nc.scalar.activation(xT[:, u, 0:4].rearrange("p c n -> p (c n)"), ps[:, 0], ACT.Copy).then_inc(act_xT, 1)

        copy_x(0, 0)
        total = rounds(act)
        with act.Fori(0, total) as i:
            for u in range(2):
                n = 2 * i + u
                act.wait_ge(gate_ready, n + 1)
                nc.scalar.activation(sg[:, u], ps[:, 2], ACT.Sigmoid).then_inc(sig_ready, 1)
                copy_x(1 - u, n + 1)
                act.wait_ge(stored[u], 16 * i + 16)
                act.wait_ge(y_summed, 2 * n + 5)
                nc.scalar.activation(y[:, u, 0:512], ps[:, 4], ACT.Copy).then_inc(act_y, 1)
                act.wait_ge(act_y, n + 2)
                act.wait_ge(dve_y, n + 2)
                act.dma_start(d["yb"][bass.ds((2 * i + u) * P, P), :], y[:, u]).then_inc(stored[u], 16)
        for u in range(2):
            act.wait_ge(stored[u], 16 * total + 16)
        k.pin(act)

    def vector(dve):
        dve.sem_inc(dve_xT, 1)
        dve.sem_inc(dve_y, 1)
        dve.sem_inc(hid_ready, 1)

        def copy_x(u, n):
            dve.wait_ge(x_turned, n + 3)
            nc.vector.tensor_copy(xT[:, u, 4:8].rearrange("p c n -> p (c n)"), ps[:, 1]).then_inc(dve_xT, 1)

        copy_x(0, 0)
        with dve.Fori(0, rounds(dve)) as i:
            for u in range(2):
                n = 2 * i + u
                dve.wait_ge(sig_ready, n + 1)
                nc.vector.tensor_tensor(sg[:, u], sg[:, u], ps[:, 2], ALU.mult).then_inc(step_sem, 1)
                dve.wait_ge(step_sem, n + 1)
                dve.wait_ge(up_ready, n + 3)
                nc.vector.tensor_tensor(hid[:, u].rearrange("p j n -> p (j n)"), sg[:, u], ps[:, 3], ALU.mult
                                        ).then_inc(hid_ready, 1)
                copy_x(1 - u, n + 1)
                dve.wait_ge(stored[u], 16 * i + 16)
                dve.wait_ge(y_summed, 2 * n + 6)
                nc.vector.tensor_copy(y[:, u, 512:D], ps[:, 5]).then_inc(dve_y, 1)

    k.stage(sync=sync, tensor=tensor, scalar=scalar, vector=vector, gpsimd=gpsimd)


def combine_stage(k, d, route, gather, rows_out):
    nc = k.nc
    G = NT // 3
    g = k.buf(D)
    x2, y1, y2, st = k.buf(NT, D), k.buf(NT, D), k.buf(NT, D), k.buf(NT, 4)
    gain, x_loaded = k.sem("f_gain_loaded"), [k.sem(f"f_x_loaded{n}") for n in range(3)]
    rows = [k.own_sem(f"f_rows_loaded{n}") for n in range(3)]
    step_sem, summed, squared, rooted, y_ready, stored = (
        k.sem(f"f_{w}") for w in ("step", "summed", "squared", "rooted", "y_ready", "stored"))

    def sync(sp):
        sp.dma_start(g, d["final_norm"].partition_broadcast(P).rearrange("p o n -> p (o n)")).then_inc(gain, 16)
        for n in range(3):
            sp.dma_start(x2[:, n * G:(n + 1) * G], d["x2"][n * G * P:(n + 1) * G * P, :]
                         .rearrange("(t p) n -> p t n", p=P)).then_inc(x_loaded[n], 16)
        for t in range(NT):
            sp.wait_ge(y_ready, t + 1)
            sp.dma_start(d["y"][t * P:(t + 1) * P, :], y2[:, t]).then_inc(stored, 16)
        sp.wait_ge(stored, 16 * NT)
        sp.wait_ge(rows_out, 16 * 7)

    def gpsimd(pool):
        for t in range(NT):
            for n, to in enumerate((y1, y2)):
                nc.gpsimd.indirect_dma_start(
                    to[:, t], None, d["yb"],
                    bass.IndirectOffsetOnAxis(ap=gather[:, n, t:t + 1].bitcast(I32), axis=0)
                ).then_inc(rows[t // G], 16)

    def scalar(act):
        for t in range(NT):
            act.wait_ge(summed, t + 1)
            nc.scalar.activation(y1[:, t], x2[:, t], ACT.Square, accum_out=st[:, t, 0:1]).then_inc(squared, 1)
            act.wait_ge(squared, t + 1)
            nc.scalar.activation(st[:, t, 1:2], st[:, t, 0:1], ACT.Sqrt, scale=1.0 / D, bias=k.eps
                                 ).then_inc(rooted, 1)

    def vector(dve):
        step = Steps(dve, step_sem)

        def total(t):
            if t % G == 0:
                dve.wait_ge(x_loaded[t // G], 16)
                dve.wait_ge(rows[t // G], 32 * G)
            step(nc.vector.scalar_tensor_tensor(out=x2[:, t], in0=y1[:, t], scalar=route[:, t, 2:3], in1=x2[:, t],
                                                op0=ALU.mult, op1=ALU.add))
            nc.vector.scalar_tensor_tensor(out=x2[:, t], in0=y2[:, t], scalar=route[:, t, 3:4], in1=x2[:, t],
                                           op0=ALU.mult, op1=ALU.add).then_inc(summed, 1)

        dve.wait_ge(gain, 16)
        total(0)
        for t in range(NT):
            if t + 1 < NT:
                total(t + 1)
            dve.wait_ge(rooted, t + 1)
            step(nc.vector.reciprocal(st[:, t, 2:3], st[:, t, 1:2]))
            nc.vector.scalar_tensor_tensor(out=y2[:, t], in0=x2[:, t], scalar=st[:, t, 2:3], in1=g,
                                           op0=ALU.mult, op1=ALU.mult).then_inc(y_ready, 1)

    k.stage(sync=sync, scalar=scalar, vector=vector, gpsimd=gpsimd)


def build(nc, d, upto=99):
    with ExitStack() as ctx:
        k = Kernel(nc, ctx)
        ident = k.keep(P)
        rows_out = ctx.enter_context(nc.semaphore("kv_rows_stored"))
        route, gather, blocks = k.keep(NT, 4), k.keep(2, NT), k.keep(NB + 2)

        top = k.high
        res = {"qT": k.keep(4, TPAD), "qrT": k.keep(4, TPAD), "ksT": k.keep(TPAD), "kwT": k.keep(WINDOW + TPAD),
               "vs": k.keep(NT, P), "vw": k.keep(NT + WINDOW // P, P), "ckT": k.keep(PCMP + 1), "cv": k.keep(P)}
        attention = k.high
        k.high = top
        stages = [
            lambda: projections_stage(k, d, ident),
            lambda: (release(k, attention), rotary_stage(k, d, res, ident, rows_out)),
            lambda: prompt_compress_stage(k, d, res, ident),
            lambda: prompt_stage(k, d, res, ident),
            lambda: sample_stage(k, d, res, ident),
            lambda: (release(k, top), hgrn_prompt_stage(k, d, ident)),
            lambda: hgrn_sample_stage(k, d, ident),
            lambda: merge_stage(k, d, ident, route),
            lambda: dispatch_stage(k, d, route, gather, blocks),
            lambda: experts_stage(k, d, ident, blocks),
            lambda: combine_stage(k, d, route, gather, rows_out),
        ]
        for s in stages[:upto]:
            s()
        block = ctx.enter_context(nc.Block())
        k.emit(block)


def release(k, high):
    k.high = high


SCRATCH = {
    "zn": (TPAD, ZC), "zh": (TPAD, 1024), "zT": (24, P, TPAD), "slc_rows": (TPAD, KVW), "win_rows": (TPAD, KVW),
    "branches": (3, TPAD, 512), "ob": (TPAD, 512), "x2": (TPAD, D), "h2": (TPAD, D),
    "source": (ROWS + P, 1), "yb": (ROWS, D),
}
OUTPUTS = {
    "y": (TPAD, D), "cmp_p": (SEQ, KVW), "cmp_s": (NSMP, KVW), "slc_p": (SEQ, KVW), "slc_s": (NSMP, KVW),
    "win_p": (WINDOW, KVW), "win_s": (NSEQ, WINDOW, KVW), "hgrn_p": (HH, DK, DK), "hgrn_s": (NSEQ, HH, DK, DK),
}


def shape_constants(np):
    f = np.float32
    p = np.arange(P)[:, None]
    pos = np.concatenate([np.arange(SEQ), np.tile(PAST + np.arange(NNEW), NSEQ), np.zeros(TPAD - SEQ - NSMP)]).astype(f)
    inv = f(10000.0) ** (-np.arange(HD // 2, dtype=f) / f(HD // 2))
    ang = pos[:, None] * inv[None, :].astype(f)
    masks = np.zeros((QT, P, MASKW), f)
    for b in range(QT):
        t = b * P + p
        masks[b, :, 0:SEQ] = np.where(np.arange(SEQ)[None] <= t, 0, NEG)
        kp = b * P - WINDOW + np.arange(WINDOW + P)[None]
        masks[b, :, SEQ:SEQ + WINDOW + P] = np.where((kp >= 0) & (kp <= t) & (kp > t - WINDOW), 0, NEG)
        end = np.arange(PCMP)[None] * CSTR + CBLK - 1
        masks[b, :, SEQ + WINDOW + P:-1] = np.where(end <= t, 0, NEG)
        masks[b, :, -1:] = (t >= CBLK - 1)
    r = np.arange(32)
    smask = np.zeros((32, WINDOW + NNEW), f)
    tok = (r % NNEW)[:, None]
    c = np.arange(WINDOW)[None]
    smask[:, :WINDOW] = np.where((c % P) * 4 + c // P > tok, 0, NEG)
    smask[:, WINDOW:] = np.where(np.arange(NNEW)[None] <= tok, 0, NEG)
    n = np.arange(2 * P)[:, None]
    j = np.arange(NBLK)[None]
    cover = ((n * CSTR < (j + 1) * SBLK) & (n * CSTR + CBLK > j * SBLK) & (n < SCMP)).astype(f)
    same = ((r[:, None] % NNEW == r[None] % NNEW) & (r[:, None] // 16 == r[None] // 16)).astype(f)
    forced = np.zeros((32, 2, NBLK), f)
    forced[:, 0] = 1
    for b in (0, NBLK - 2, NBLK - 1):
        forced[:, 0, b], forced[:, 1, b] = 0, 1e9
    small = np.zeros((P, 2 * NBLK), f)
    small[:] = cover.reshape(2, P, NBLK).transpose(1, 0, 2).reshape(P, -1)
    sub = np.ones((P, HH, P), f)
    sub[:, :, 0] = 0
    reset4 = np.ones((P, HH, 32), f)
    reset4[:, :, ::NNEW] = 0
    s, t = np.arange(P)[:, None], np.arange(P)[None]
    blocktri = ((s <= t) & (s // NNEW == t // NNEW)).astype(f)
    seqmask = (np.arange(32)[:, None] // NNEW == np.arange(NSEQ)[None]).astype(f)
    return {
        "ident": np.eye(P, dtype=f), "rope": np.concatenate([np.cos(ang), np.sin(ang)], 1).astype(f),
        "prompt_masks": masks, "smask": smask, "cover": small, "same": same, "forced": forced.reshape(32, -1),
        "reset": sub.reshape(P, -1), "reset4": reset4.reshape(P, -1), "tri": (s <= t).astype(f),
        "before": (s < t).astype(f), "blocktri": blocktri[:32, :32].copy(), "seqmask": seqmask,
        "iota": np.tile(np.arange(NB, dtype=f), (P, 1)), "limits": np.tile(P * np.arange(1, 9, dtype=f), (P, 1)),
        "valid": ((np.arange(NT) * P)[None] + p < SEQ + NSMP).astype(f),
        "block_ids": np.tile(np.arange(NB + 2, dtype=f), (P, 1)),
        "token_ids": ((np.arange(NT) * P)[None] + p).astype(np.int32),
        "lane8": (np.arange(P)[:, None] % 8).astype(f),
    }


def laid_out(inputs, np):
    a = {n: np.asarray(v) for n, v in inputs.items()}
    x = np.concatenate([a["x_prompt"].reshape(SEQ, D), a["x_sample"].reshape(NSMP, D),
                        np.zeros((TPAD - SEQ - NSMP, D), np.float32)])
    w = a["w_in"][0]
    q = w[:, :512].reshape(D, KVH, GRP, HD).transpose(0, 2, 1, 3).reshape(D, 512)
    rows1 = np.concatenate([q, w[:, 512:ZC]], 1)
    rows2 = w[:, 2328:3352]
    cols = np.concatenate([w[:, ZC:2328], w[:, 3352:5400]], 1)

    def chunked(m, width):
        n = m.shape[1] // width
        return np.ascontiguousarray(m.reshape(KD, P, n, width).transpose(2, 1, 0, 3).reshape(n, P, KD * width))

    def by_k(m):
        return np.ascontiguousarray(m.reshape(-1, P, m.shape[1]).transpose(1, 0, 2).reshape(P, -1))

    router = np.concatenate([a["w_router_group"][0], a["w_router_expert"][0].transpose(1, 0, 2).reshape(D, NE)], 1)
    return {
        "x_all": x, "norm1": a["norm1"], "w_rows1": chunked(rows1, ZCH), "w_rows2": chunked(rows2, 256),
        "w_cols": chunked(cols, P), "cache_cmp": np.ascontiguousarray(a["cache_cmp_kv"].reshape(-1, CSTR, 2 * KVH, HD).transpose(0, 2, 1, 3)
                                          ).reshape(-1, CHW),
        "cache_slc": a["cache_slc_kv"].reshape(-1, CHW), "cache_win": a["cache_win_kv"].reshape(NSEQ, WINDOW, KVW),
        "state": a["state_hgrn"][0], "pages": np.repeat(a["page_table"].reshape(NSEQ, 2, 16).transpose(2, 0, 1).reshape(16, -1), 8, axis=0),
        "pe": np.ascontiguousarray(a["cmp_pe"][0].reshape(2, 16, P).transpose(2, 0, 1).reshape(P, 32)),
        "cmp_w1": np.ascontiguousarray(a["cmp_w1"][0].reshape(2, 16, P, P).transpose(2, 0, 1, 3).reshape(P, -1)),
        "cmp_b1": np.ascontiguousarray(a["cmp_b1"][0].T),
        "cmp_w2": np.ascontiguousarray(a["cmp_w2"][0].transpose(1, 0, 2).reshape(P, P)),
        "cmp_b2k": np.concatenate([a["cmp_b2"][0, 0]] * 2).reshape(P, 1),
        "cmp_b2v": np.concatenate([a["cmp_b2"][0, 1]] * 2).reshape(1, P),
        "lb_logits": np.ascontiguousarray(a["hgrn_lb_logits"].reshape(2, HH, DK).transpose(2, 0, 1).reshape(DK, -1)),
        "gnorm": a["hgrn_gnorm"], "w_pa": by_k(a["w_proj_a"][0]), "w_pb": by_k(a["w_proj_b"][0]),
        "w_out": by_k(a["w_out"][0]), "norm2": a["norm2"], "w_router": by_k(router),
        "b_router": np.concatenate([a["b_router_group"].reshape(1, NG), a["b_router_expert"].reshape(1, NE)], 1),
        "w_gate": a["w_exp_gate"][0], "w_up": a["w_exp_up"][0], "w_down": a["w_exp_down"][0],
        "final_norm": a["final_norm"].reshape(1, D),
    }


def kernel(**inputs):
    import numpy as np
    import concourse.bacc as bacc
    from concourse import mybir
    from concourse.bass_utils import run_bass_kernel_spmd

    nc = bacc.Bacc("TRN2", target_bir_lowering=False, num_devices=1)
    arrays = {n: np.ascontiguousarray(v) for n, v in {**laid_out(inputs, np), **shape_constants(np)}.items()}
    d = {n: nc.dram_tensor(f"in_{n}", v.shape, mybir.dt.from_np(v.dtype), kind="ExternalInput").ap()
         for n, v in arrays.items()}
    for n, shape in SCRATCH.items():
        dt = mybir.dt.int32 if n == "source" else mybir.dt.float32
        d[n] = nc.dram_tensor(f"scratch_{n}", shape, dt, kind="Internal").ap()
    for n, shape in OUTPUTS.items():
        d[n] = nc.dram_tensor(f"out_{n}", shape, mybir.dt.float32, kind="ExternalOutput").ap()
    build(nc, d)
    r = run_bass_kernel_spmd(nc, [{f"in_{n}": v for n, v in arrays.items()}], core_ids=[0]).results[0]
    o = {n: r[f"out_{n}"] for n in OUTPUTS}
    return (o["y"][:SEQ].reshape(1, SEQ, D), o["y"][SEQ:SEQ + NSMP].reshape(NSEQ, NNEW, D),
            o["cmp_p"].reshape(1, 1, SEQ, 2, KVH, HD), o["cmp_s"].reshape(1, NSEQ, NNEW, 2, KVH, HD),
            o["slc_p"].reshape(1, 1, SEQ, 2, KVH, HD), o["slc_s"].reshape(1, NSEQ, NNEW, 2, KVH, HD),
            o["win_p"].reshape(1, 1, WINDOW, 2, KVH, HD), o["win_s"].reshape(1, NSEQ, WINDOW, 2, KVH, HD),
            o["hgrn_p"].reshape(1, 1, HH, DK, DK), o["hgrn_s"].reshape(1, NSEQ, HH, DK, DK))
```
